# Optimizing a Trainium2 kernel written in Bass

```python
import math
import jax, jax.numpy as jnp
from jax import lax
import numpy as np

D_MODEL = 1024
BATCH = 1
SEQ = 256
DEPTH = 2

GRID_W = 64
ROPE_THETA = 500000.0
Q_BLOCK = 128

A_HEADS = 4
A_HEAD_DIM = 64
A_ROT = A_HEAD_DIM // 4
A_Q = A_HEADS * 2 * A_HEAD_DIM
A_K = A_HEADS * 2 * A_HEAD_DIM
A_V = A_HEADS * 2 * A_HEAD_DIM

B_HEADS = 8
B_NOPE = 64
B_ROPE = 32
B_V = 64
B_Q_RANK = 256
B_KV_RANK = 128

C_HEADS = 16
C_HEAD_DIM = 64
C_WIDTH = C_HEADS * C_HEAD_DIM
NA_ROWS = 8
NA_COLS = 16

N_GROUPS = 4
EXPERTS_PER_GROUP = 8
N_EXPERTS = N_GROUPS * EXPERTS_PER_GROUP
TOP_K = 2
D_EXPERT = 512
MOE_BLOCK = 128

DN_ALPHA = (2 * DEPTH) ** 0.25
DN_BETA = (8 * DEPTH) ** -0.25
LN_EPS = 1e-5
RMS_EPS = 1e-6

EVEN_IN = A_Q + A_K + A_V + B_Q_RANK + B_KV_RANK + B_ROPE
EVEN_SPLITS = (A_Q, A_Q + A_K, A_Q + A_K + A_V, A_Q + A_K + A_V + B_Q_RANK,
               A_Q + A_K + A_V + B_Q_RANK + B_KV_RANK)
EVEN_OUT = A_HEADS * 2 * A_HEAD_DIM + B_HEADS * B_V
N_EVEN = (DEPTH + 1) // 2
N_ODD = DEPTH // 2


def layer_norm(x, g, b):
    xf = x.astype(jnp.float32)
    mu = jnp.mean(xf, axis=-1, keepdims=True)
    var = jnp.mean(jnp.square(xf - mu), axis=-1, keepdims=True)
    y = (xf - mu) * lax.rsqrt(var + LN_EPS) * g.astype(jnp.float32) + b.astype(jnp.float32)
    return y.astype(x.dtype)

def rms_norm(x, g):
    xf = x.astype(jnp.float32)
    y = xf * lax.rsqrt(jnp.mean(xf * xf, axis=-1, keepdims=True) + RMS_EPS) * g.astype(jnp.float32)
    return y.astype(x.dtype)

def rope_tables(seq, rot_dim):
    inv_freq = ROPE_THETA ** (-jnp.arange(0, rot_dim, 2, dtype=jnp.float32) / rot_dim)
    ang = jnp.arange(seq, dtype=jnp.float32)[:, None] * inv_freq[None, :]
    return jnp.cos(ang), jnp.sin(ang)

def apply_rope(x, cos, sin):
    half = cos.shape[-1]
    r = 2 * half
    cos = cos.astype(x.dtype)
    sin = sin.astype(x.dtype)
    x1 = x[..., :half]
    x2 = x[..., half:r]
    return jnp.concatenate([x1 * cos - x2 * sin, x2 * cos + x1 * sin, x[..., r:]], axis=-1)

def diff_attention(q, k, v, lam, subln_g, lambda_init, cos, sin):
    B, S, H, _, d = q.shape
    nb = S // Q_BLOCK
    q = apply_rope(q.transpose(0, 2, 3, 1, 4), cos, sin)
    k = apply_rope(k.transpose(0, 2, 3, 1, 4), cos, sin)
    v = v.transpose(0, 2, 1, 3)
    q_blocks = q.reshape(B, H, 2, nb, Q_BLOCK, d).transpose(3, 0, 1, 2, 4, 5)
    scale = d ** -0.5

    def block(qb):
        s = jnp.einsum('bhmqd,bhmkd->bhmqk', qb, k).astype(jnp.float32) * scale
        p = jax.nn.softmax(s, axis=-1)
        w = p[:, :, 0] - lam * p[:, :, 1]
        return jnp.einsum('bhqk,bhke->bhqe', w.astype(v.dtype), v)

    o = lax.map(block, q_blocks)
    o = rms_norm(o, subln_g) * (1.0 - lambda_init)
    return o.transpose(1, 0, 3, 2, 4).reshape(B, S, H * 2 * d)

def latent_attention(c_q, c_kv, k_r, q_norm_g, w_uq, kv_norm_g, w_ukv, cos, sin):
    B, S, _ = c_q.shape
    H = B_HEADS
    nb = S // Q_BLOCK
    q = (rms_norm(c_q, q_norm_g) @ w_uq).reshape(B, S, H, B_NOPE + B_ROPE).transpose(0, 2, 1, 3)
    q_nope = q[..., :B_NOPE]
    q_rope = apply_rope(q[..., B_NOPE:], cos, sin)
    kv = (rms_norm(c_kv, kv_norm_g) @ w_ukv).reshape(B, S, H, B_NOPE + B_V).transpose(0, 2, 1, 3)
    k_nope = kv[..., :B_NOPE]
    v = kv[..., B_NOPE:]
    k_rope = apply_rope(k_r, cos, sin)
    qn_blocks = q_nope.reshape(B, H, nb, Q_BLOCK, B_NOPE).transpose(2, 0, 1, 3, 4)
    qr_blocks = q_rope.reshape(B, H, nb, Q_BLOCK, B_ROPE).transpose(2, 0, 1, 3, 4)
    scale = (B_NOPE + B_ROPE) ** -0.5

    def block(args):
        qn, qr = args
        s = (jnp.einsum('bhqd,bhkd->bhqk', qn, k_nope)
             + jnp.einsum('bhqr,bkr->bhqk', qr, k_rope)).astype(jnp.float32) * scale
        p = jax.nn.softmax(s, axis=-1)
        return jnp.einsum('bhqk,bhke->bhqe', p.astype(v.dtype), v)

    o = lax.map(block, (qn_blocks, qr_blocks))
    return o.transpose(1, 0, 3, 2, 4).reshape(B, S, H * B_V)

def neighbourhood_attention(q, k, v, rel_bias):
    B, S, H, d = q.shape
    rows = S // GRID_W
    kh = min(NA_ROWS, rows)
    kw = NA_COLS
    to_grid = lambda t: t.reshape(B, rows, GRID_W, H, d).transpose(0, 3, 1, 2, 4)
    qg, kg, vg = to_grid(q), to_grid(k), to_grid(v)
    cols = jnp.arange(GRID_W)
    col_start = jnp.clip(cols - kw // 2, 0, GRID_W - kw)
    col_idx = col_start[:, None] + jnp.arange(kw)[None, :]
    col_off = col_idx - cols[:, None] + (NA_COLS - 1)
    scale = d ** -0.5

    def row(args):
        r, q_row = args
        r0 = jnp.clip(r - kh // 2, 0, rows - kh)
        k_band = lax.dynamic_slice_in_dim(kg, r0, kh, axis=2)
        v_band = lax.dynamic_slice_in_dim(vg, r0, kh, axis=2)
        k_win = k_band[:, :, :, col_idx]
        v_win = v_band[:, :, :, col_idx]
        row_off = r0 + jnp.arange(kh) - r + (NA_ROWS - 1)
        bias = rel_bias[:, row_off[:, None, None], col_off[None]]
        bias = bias.transpose(0, 2, 1, 3).astype(jnp.float32)
        s = jnp.einsum('bhcd,bhicjd->bhcij', q_row, k_win).astype(jnp.float32) * scale + bias[None]
        p = jax.nn.softmax(s.reshape(B, H, GRID_W, kh * kw), axis=-1).reshape(B, H, GRID_W, kh, kw)
        return jnp.einsum('bhcij,bhicje->bhce', p.astype(v_win.dtype), v_win)

    o = lax.map(row, (jnp.arange(rows), qg.transpose(2, 0, 1, 3, 4)))
    return o.transpose(1, 0, 3, 2, 4).reshape(B, S, H * d)

def even_mixer(x, w_in, lam_q1, lam_k1, lam_q2, lam_k2, subln_g, q_norm_g, w_uq,
               kv_norm_g, w_ukv, w_o, lambda_init, rope_a, rope_b):
    B, S, _ = x.shape
    h = x @ w_in
    qa, ka, va, cq, ckv, kr = jnp.split(h, EVEN_SPLITS, axis=-1)
    f32 = jnp.float32
    lam = (jnp.exp(jnp.sum(lam_q1.astype(f32) * lam_k1.astype(f32)))
           - jnp.exp(jnp.sum(lam_q2.astype(f32) * lam_k2.astype(f32))) + lambda_init)
    a_out = diff_attention(qa.reshape(B, S, A_HEADS, 2, A_HEAD_DIM),
                           ka.reshape(B, S, A_HEADS, 2, A_HEAD_DIM),
                           va.reshape(B, S, A_HEADS, 2 * A_HEAD_DIM),
                           lam, subln_g, lambda_init, rope_a[0], rope_a[1])
    b_out = latent_attention(cq, ckv, kr, q_norm_g, w_uq, kv_norm_g, w_ukv, rope_b[0], rope_b[1])
    return jnp.concatenate([a_out, b_out], axis=-1) @ w_o

def odd_mixer(x, w_qkv, rel_bias, w_o):
    B, S, _ = x.shape
    q, k, v = jnp.split(x @ w_qkv, 3, axis=-1)
    shp = (B, S, C_HEADS, C_HEAD_DIM)
    o = neighbourhood_attention(q.reshape(shp), k.reshape(shp), v.reshape(shp), rel_bias)
    return o @ w_o

def hier_moe(x, w_rg, b_rg, w_re, b_re, w1, w3, w2):
    B, S, D = x.shape
    N = B * S
    xt = x.reshape(N, D)
    g_prob = jax.nn.softmax((xt @ w_rg).astype(jnp.float32) + b_rg.astype(jnp.float32), axis=-1)
    grp = jnp.argmax(g_prob, axis=-1).astype(jnp.int32)
    g_w = jnp.take_along_axis(g_prob, grp[:, None], axis=-1)
    e_logits = ((xt @ w_re).astype(jnp.float32) + b_re.astype(jnp.float32)).reshape(N, N_GROUPS, EXPERTS_PER_GROUP)
    idx = jnp.broadcast_to(grp[:, None, None], (N, 1, EXPERTS_PER_GROUP))
    e_logits = jnp.take_along_axis(e_logits, idx, axis=1)[:, 0]
    top_v, top_i = lax.top_k(e_logits, TOP_K)
    gate = jax.nn.softmax(top_v, axis=-1) * g_w
    expert = grp[:, None] * EXPERTS_PER_GROUP + top_i.astype(jnp.int32)
    A = N * TOP_K
    e_flat = expert.reshape(A)
    w_flat = gate.reshape(A)
    tok = jnp.repeat(jnp.arange(N, dtype=jnp.int32), TOP_K)
    order = jnp.argsort(e_flat)
    e_s, tok_s, w_s = e_flat[order], tok[order], w_flat[order]
    counts = jnp.bincount(e_flat, length=N_EXPERTS)
    start = jnp.cumsum(counts) - counts
    padded = (counts + MOE_BLOCK - 1) // MOE_BLOCK * MOE_BLOCK
    pad_end = jnp.cumsum(padded)
    pad_start = pad_end - padded
    dest = pad_start[e_s] + jnp.arange(A) - start[e_s]
    n_blocks = -(-A // MOE_BLOCK) + N_EXPERTS
    P = n_blocks * MOE_BLOCK
    slot_tok = jnp.full((P,), N, jnp.int32).at[dest].set(tok_s)
    slot_w = jnp.zeros((P,), jnp.float32).at[dest].set(w_s)
    block_exp = jnp.minimum(jnp.searchsorted(pad_end, jnp.arange(n_blocks) * MOE_BLOCK, side='right'),
                            N_EXPERTS - 1).astype(jnp.int32)
    x_pad = jnp.concatenate([xt, jnp.zeros((1, D), xt.dtype)], axis=0)

    def block(args):
        tids, e, w = args
        xb = x_pad[tids]
        hdn = jax.nn.silu(xb @ w1[e]) * (xb @ w3[e])
        return (hdn @ w2[e]) * w[:, None].astype(xb.dtype)

    y = lax.map(block, (slot_tok.reshape(n_blocks, MOE_BLOCK), block_exp,
                        slot_w.reshape(n_blocks, MOE_BLOCK)))
    out = jax.ops.segment_sum(y.reshape(P, D), slot_tok, num_segments=N + 1)[:N]
    return out.reshape(B, S, D)

def first_inputs(seed: int = 0) -> dict:
    key = jax.random.key(seed)
    ks = iter(jax.random.split(key, 32))
    nrm = lambda shape, scale: jax.random.normal(next(ks), shape, jnp.float32) * scale
    gain = lambda shape: 1.0 + nrm(shape, 0.02)
    D = D_MODEL
    return {
        "x": nrm((BATCH, SEQ, D), 1.0),
        "even_w_in": nrm((N_EVEN, D, EVEN_IN), D ** -0.5),
        "even_lam_q1": nrm((N_EVEN, A_HEAD_DIM), 0.1),
        "even_lam_k1": nrm((N_EVEN, A_HEAD_DIM), 0.1),
        "even_lam_q2": nrm((N_EVEN, A_HEAD_DIM), 0.1),
        "even_lam_k2": nrm((N_EVEN, A_HEAD_DIM), 0.1),
        "even_subln_g": gain((N_EVEN, 2 * A_HEAD_DIM)),
        "even_q_norm_g": gain((N_EVEN, B_Q_RANK)),
        "even_w_uq": nrm((N_EVEN, B_Q_RANK, B_HEADS * (B_NOPE + B_ROPE)), B_Q_RANK ** -0.5),
        "even_kv_norm_g": gain((N_EVEN, B_KV_RANK)),
        "even_w_ukv": nrm((N_EVEN, B_KV_RANK, B_HEADS * (B_NOPE + B_V)), B_KV_RANK ** -0.5),
        "even_w_o": nrm((N_EVEN, EVEN_OUT, D), EVEN_OUT ** -0.5 * DN_BETA),
        "odd_w_qkv": nrm((N_ODD, D, 3 * C_WIDTH), D ** -0.5),
        "odd_rel_bias": nrm((N_ODD, C_HEADS, 2 * NA_ROWS - 1, 2 * NA_COLS - 1), 0.02),
        "odd_w_o": nrm((N_ODD, C_WIDTH, D), C_WIDTH ** -0.5 * DN_BETA),
        "ln1_g": gain((DEPTH, D)),
        "ln1_b": nrm((DEPTH, D), 0.02),
        "ln2_g": gain((DEPTH, D)),
        "ln2_b": nrm((DEPTH, D), 0.02),
        "w_router_group": nrm((DEPTH, D, N_GROUPS), D ** -0.5),
        "b_router_group": nrm((DEPTH, N_GROUPS), 0.01),
        "w_router_expert": nrm((DEPTH, D, N_EXPERTS), D ** -0.5),
        "b_router_expert": nrm((DEPTH, N_EXPERTS), 0.01),
        "w_gate": nrm((DEPTH, N_EXPERTS, D, D_EXPERT), D ** -0.5),
        "w_up": nrm((DEPTH, N_EXPERTS, D, D_EXPERT), D ** -0.5),
        "w_down": nrm((DEPTH, N_EXPERTS, D_EXPERT, D), D_EXPERT ** -0.5 * DN_BETA),
    }

def first_block(x, even_w_in, even_lam_q1, even_lam_k1, even_lam_q2, even_lam_k2, even_subln_g,
              even_q_norm_g, even_w_uq, even_kv_norm_g, even_w_ukv, even_w_o,
              odd_w_qkv, odd_rel_bias, odd_w_o, ln1_g, ln1_b, ln2_g, ln2_b,
              w_router_group, b_router_group, w_router_expert, b_router_expert,
              w_gate, w_up, w_down):
    S = x.shape[1]
    rope_a = rope_tables(S, A_ROT)
    rope_b = rope_tables(S, B_ROPE)
    for i in range(DEPTH):
        j = i // 2
        if i % 2 == 0:
            lambda_init = 0.8 - 0.6 * math.exp(-0.3 * i)
            m = even_mixer(x, even_w_in[j], even_lam_q1[j], even_lam_k1[j], even_lam_q2[j],
                           even_lam_k2[j], even_subln_g[j], even_q_norm_g[j], even_w_uq[j],
                           even_kv_norm_g[j], even_w_ukv[j], even_w_o[j], lambda_init, rope_a, rope_b)
        else:
            m = odd_mixer(x, odd_w_qkv[j], odd_rel_bias[j], odd_w_o[j])
        x = layer_norm(DN_ALPHA * x + m, ln1_g[i], ln1_b[i])
        f = hier_moe(x, w_router_group[i], b_router_group[i], w_router_expert[i], b_router_expert[i],
                     w_gate[i], w_up[i], w_down[i])
        x = layer_norm(DN_ALPHA * x + f, ln2_g[i], ln2_b[i])
    return x


DEPTH_2 = 1

D_MIX = D_MODEL
D_LRU = D_MIX // 2
LRU_HEADS = 8
LRU_HEAD_DIM = D_LRU // LRU_HEADS
LRU_CONV = 4
LRU_C = 8.0
D_RET = D_MIX - D_LRU
RET_HEADS = 4
RET_HEAD_DIM = D_RET // RET_HEADS
RET_CHUNK = 128
ROPE_BASE = 10000.0
D_IN = 2 * D_LRU + 4 * D_RET
SPLITS = (D_LRU, 2 * D_LRU, 2 * D_LRU + D_RET, 2 * D_LRU + 2 * D_RET, 2 * D_LRU + 3 * D_RET)
D_FF = 3 * D_MODEL
FFN_CONV = 3
NORM_EPS = 1e-6


def rms_norm_2(x, gain):
    xf = x.astype(jnp.float32)
    y = xf * lax.rsqrt(jnp.mean(xf * xf, axis=-1, keepdims=True) + NORM_EPS)
    return (y * gain.astype(jnp.float32)).astype(x.dtype)

def causal_depthwise_conv(x, w, b):
    width, ch = w.shape
    y = lax.conv_general_dilated(
        x, w[:, None, :].astype(x.dtype), window_strides=(1,),
        padding=[(width - 1, 0)], dimension_numbers=("NWC", "WIO", "NWC"),
        feature_group_count=ch)
    return y + b.astype(x.dtype)

def _linear_recurrence_combine(left, right):
    a1, b1 = left
    a2, b2 = right
    return a1 * a2, a2 * b1 + b2

def rg_lru(x, wa, ba, wx, bx, lam):
    bsz, slen, _ = x.shape
    xf = x.astype(jnp.float32)
    xh = xf.reshape(bsz, slen, LRU_HEADS, LRU_HEAD_DIM)
    r = jax.nn.sigmoid(jnp.einsum("bshi,hij->bshj", xh, wa.astype(jnp.float32)).reshape(bsz, slen, D_LRU)
                       + ba.astype(jnp.float32))
    i = jax.nn.sigmoid(jnp.einsum("bshi,hij->bshj", xh, wx.astype(jnp.float32)).reshape(bsz, slen, D_LRU)
                       + bx.astype(jnp.float32))
    log_a = -LRU_C * r * jax.nn.softplus(-lam.astype(jnp.float32))
    a = jnp.exp(log_a)
    inp = jnp.sqrt(-jnp.expm1(2.0 * log_a)) * (i * xf)
    _, h = lax.associative_scan(_linear_recurrence_combine, (a, inp), axis=1)
    return h

def rotary(x, cos, sin):
    half = x.shape[-1] // 2
    x1, x2 = x[..., :half], x[..., half:]
    return jnp.concatenate([x1 * cos - x2 * sin, x2 * cos + x1 * sin], axis=-1)

def retention_chunkwise(q, k, v):
    bsz, slen, nh, dk = q.shape
    dv = v.shape[-1]
    c = RET_CHUNK
    n = slen // c
    log_g = jnp.log1p(-jnp.exp2(-5.0 - jnp.arange(nh, dtype=jnp.float32)))
    q = q.reshape(bsz, n, c, nh, dk)
    k = (k * (dk ** -0.5)).reshape(bsz, n, c, nh, dk)
    v = v.reshape(bsz, n, c, nh, dv)
    idx = jnp.arange(c, dtype=jnp.float32)
    diff = idx[:, None] - idx[None, :]
    decay_in = jnp.where(diff[None] >= 0, jnp.exp(jnp.maximum(diff, 0.0)[None] * log_g[:, None, None]), 0.0)
    scores = jnp.einsum("bnihd,bnjhd->bnhij", q, k) * decay_in[None, None]
    inner = jnp.einsum("bnhij,bnjhe->bnihe", scores, v)
    zeta = jnp.exp((c - 1 - idx)[None, :] * log_g[:, None])
    kv = jnp.einsum("bnjhd,bnjhe,hj->nbhde", k, v, zeta)
    g_chunk = jnp.exp(c * log_g)[None, :, None, None]

    def step(state, kv_n):
        return state * g_chunk + kv_n, state

    init = jnp.zeros((bsz, nh, dk, dv), jnp.float32)
    _, prev = lax.scan(step, init, kv)
    xi = jnp.exp((idx + 1.0)[None, :] * log_g[:, None])
    cross = jnp.einsum("bnihd,nbhde,hi->bnihe", q, prev, xi)
    return (inner + cross).reshape(bsz, slen, nh, dv)

def head_group_norm(o, gain):
    mu = jnp.mean(o, axis=-1, keepdims=True)
    var = jnp.mean(jnp.square(o - mu), axis=-1, keepdims=True)
    return (o - mu) * lax.rsqrt(var + NORM_EPS) * gain.astype(jnp.float32).reshape(RET_HEADS, RET_HEAD_DIM)

def second_inputs(seed: int = 0) -> dict:
    key = jax.random.key(seed)
    ks = jax.random.split(key, 20)
    f32 = jnp.float32

    def nrm(k, shape, fan_in):
        return jax.random.normal(k, shape, f32) * (fan_in ** -0.5)

    def gain(k, shape):
        return 1.0 + 0.05 * jax.random.normal(k, shape, f32)

    def bias(k, shape):
        return 0.02 * jax.random.normal(k, shape, f32)

    a0 = jax.random.uniform(ks[9], (DEPTH_2, D_LRU), f32, minval=0.9, maxval=0.999)
    return {
        "x": jax.random.normal(ks[0], (BATCH, SEQ, D_MODEL), f32),
        "norm1_gain": gain(ks[1], (DEPTH_2, D_MODEL)),
        "w_in": nrm(ks[2], (DEPTH_2, D_MODEL, D_IN), D_MODEL),
        "lru_conv_w": nrm(ks[3], (DEPTH_2, LRU_CONV, D_LRU), LRU_CONV),
        "lru_conv_b": bias(ks[4], (DEPTH_2, D_LRU)),
        "lru_gate_a_w": nrm(ks[5], (DEPTH_2, LRU_HEADS, LRU_HEAD_DIM, LRU_HEAD_DIM), LRU_HEAD_DIM),
        "lru_gate_a_b": bias(ks[6], (DEPTH_2, D_LRU)),
        "lru_gate_x_w": nrm(ks[7], (DEPTH_2, LRU_HEADS, LRU_HEAD_DIM, LRU_HEAD_DIM), LRU_HEAD_DIM),
        "lru_gate_x_b": bias(ks[8], (DEPTH_2, D_LRU)),
        "lru_lambda": jnp.log(a0) - jnp.log1p(-a0),
        "lru_norm_gain": gain(ks[10], (DEPTH_2, D_LRU)),
        "ret_norm_gain": gain(ks[11], (DEPTH_2, D_RET)),
        "w_out": nrm(ks[12], (DEPTH_2, D_MIX, D_MODEL), D_MIX),
        "norm2_gain": gain(ks[13], (DEPTH_2, D_MODEL)),
        "ffn_up_w": nrm(ks[14], (DEPTH_2, D_MODEL, 2 * D_FF), D_MODEL),
        "ffn_conv_w": nrm(ks[15], (DEPTH_2, FFN_CONV, 2 * D_FF), FFN_CONV),
        "ffn_conv_b": bias(ks[16], (DEPTH_2, 2 * D_FF)),
        "ffn_down_w": nrm(ks[17], (DEPTH_2, D_FF, D_MODEL), D_FF),
        "final_norm_gain": gain(ks[18], (D_MODEL,)),
    }

def second_block(x, norm1_gain, w_in, lru_conv_w, lru_conv_b, lru_gate_a_w, lru_gate_a_b,
              lru_gate_x_w, lru_gate_x_b, lru_lambda, lru_norm_gain, ret_norm_gain, w_out,
              norm2_gain, ffn_up_w, ffn_conv_w, ffn_conv_b, ffn_down_w, final_norm_gain):
    bsz, slen, _ = x.shape
    dt = x.dtype
    pos = jnp.arange(slen, dtype=jnp.float32)
    inv_freq = ROPE_BASE ** (-jnp.arange(0, RET_HEAD_DIM, 2, dtype=jnp.float32) / RET_HEAD_DIM)
    ang = pos[:, None] * inv_freq[None, :]
    cos = jnp.cos(ang)[:, None, :]
    sin = jnp.sin(ang)[:, None, :]

    h = x
    for l in range(DEPTH_2):
        u = rms_norm_2(h, norm1_gain[l])
        proj = u @ w_in[l].astype(dt)
        x_lru, g_lru, q, k, v, g_ret = jnp.split(proj, SPLITS, axis=-1)

        xc = causal_depthwise_conv(x_lru, lru_conv_w[l], lru_conv_b[l])
        hl = rg_lru(xc, lru_gate_a_w[l], lru_gate_a_b[l], lru_gate_x_w[l], lru_gate_x_b[l], lru_lambda[l])
        y_lru = rms_norm_2(hl.astype(dt) * jax.nn.gelu(g_lru), lru_norm_gain[l])

        qh = rotary(q.astype(jnp.float32).reshape(bsz, slen, RET_HEADS, RET_HEAD_DIM), cos, sin)
        kh = rotary(k.astype(jnp.float32).reshape(bsz, slen, RET_HEADS, RET_HEAD_DIM), cos, sin)
        vh = v.astype(jnp.float32).reshape(bsz, slen, RET_HEADS, RET_HEAD_DIM)
        o = head_group_norm(retention_chunkwise(qh, kh, vh), ret_norm_gain[l]).reshape(bsz, slen, D_RET)
        y_ret = o.astype(dt) * jax.nn.silu(g_ret)

        mixed = jnp.concatenate([y_lru, y_ret], axis=-1)
        h = h + mixed @ w_out[l].astype(dt)

        u = rms_norm_2(h, norm2_gain[l])
        up = causal_depthwise_conv(u @ ffn_up_w[l].astype(dt), ffn_conv_w[l], ffn_conv_b[l])
        a_branch, v_branch = jnp.split(up, 2, axis=-1)
        h = h + (jax.nn.gelu(a_branch) * v_branch) @ ffn_down_w[l].astype(dt)

    return rms_norm_2(h, final_norm_gain)


def setup_inputs(seed=0):
    out = dict(first_inputs(seed))
    for name, value in second_inputs(seed + 1).items():
        if name != "x":
            out[name + "_2"] = value
    return out


def reference(
    x, even_w_in, even_lam_q1, even_lam_k1, even_lam_q2, even_lam_k2, even_subln_g,
    even_q_norm_g, even_w_uq, even_kv_norm_g, even_w_ukv, even_w_o, odd_w_qkv, odd_rel_bias,
    odd_w_o, ln1_g, ln1_b, ln2_g, ln2_b, w_router_group, b_router_group, w_router_expert,
    b_router_expert, w_gate, w_up, w_down, norm1_gain_2, w_in_2, lru_conv_w_2, lru_conv_b_2,
    lru_gate_a_w_2, lru_gate_a_b_2, lru_gate_x_w_2, lru_gate_x_b_2, lru_lambda_2,
    lru_norm_gain_2, ret_norm_gain_2, w_out_2, norm2_gain_2, ffn_up_w_2, ffn_conv_w_2,
    ffn_conv_b_2, ffn_down_w_2, final_norm_gain_2,
):
    x = first_block(
        x, even_w_in, even_lam_q1, even_lam_k1, even_lam_q2, even_lam_k2, even_subln_g,
        even_q_norm_g, even_w_uq, even_kv_norm_g, even_w_ukv, even_w_o, odd_w_qkv, odd_rel_bias,
        odd_w_o, ln1_g, ln1_b, ln2_g, ln2_b, w_router_group, b_router_group, w_router_expert,
        b_router_expert, w_gate, w_up, w_down,
    )
    return second_block(
        x, norm1_gain_2, w_in_2, lru_conv_w_2, lru_conv_b_2, lru_gate_a_w_2, lru_gate_a_b_2,
        lru_gate_x_w_2, lru_gate_x_b_2, lru_lambda_2, lru_norm_gain_2, ret_norm_gain_2, w_out_2,
        norm2_gain_2, ffn_up_w_2, ffn_conv_w_2, ffn_conv_b_2, ffn_down_w_2, final_norm_gain_2,
    )


_drawn_inputs = setup_inputs


def setup_inputs(seed=0):
    import zlib

    import numpy as np

    out = dict(_drawn_inputs(seed))
    spreads = {}
    factors = {'even_lam_k2': 3.211,
     'even_subln_g': 5.215,
     'even_q_norm_g': 8.0,
     'even_kv_norm_g': 8.0,
     'odd_rel_bias': 23.407,
     'b_router_group': 4.393,
     'b_router_expert': 6.351,
     'lru_gate_a_b_2': 31.081,
     'lru_gate_x_b_2': 8.0,
     'ret_norm_gain_2': 3.044,
     'ffn_conv_b_2': 4.514,
     'lru_norm_gain_2': 2.892,
     'norm2_gain_2': 3.235}
    for name, (base, spread) in spreads.items():
        noise = np.random.default_rng([zlib.crc32(name.encode()), seed]).standard_normal(out[name].shape)
        drawn = base * np.exp(spread * noise) if base else spread * noise
        out[name] = __import__('jax').numpy.asarray(drawn.astype(out[name].dtype))
    for name, factor in factors.items():
        out[name] = (out[name] * factor).astype(out[name].dtype)
    return out
```

```python
import math
from contextlib import ExitStack

import numpy as np
import concourse.bass as bass
from concourse import mybir

F32 = mybir.dt.float32
I32 = mybir.dt.int32
ALU = mybir.AluOpType
ACT = mybir.ActivationFunctionType
AX = mybir.AxisListType.X

P = 128
SEQ, D = 256, 1024
T = SEQ // P
C = D // P
DEPTH = 2
ALPHA = (2 * DEPTH) ** 0.25
LN_EPS, RMS_EPS = 1e-5, 1e-6
NEG = -1e30

A_HEADS, A_DIM = 4, 64
A_HALF = A_DIM // 4 // 2
LAMBDA_INIT = 0.8 - 0.6 * math.exp(-0.3 * 0)
B_HEADS, B_NOPE, B_ROPE, B_V = 8, 64, 32, 64
B_QK = B_NOPE + B_ROPE
B_HALF = B_ROPE // 2
Q_RANK, KV_RANK = 256, 128
VA0 = 1024
CQ0, CKV0, KR0, EVEN_IN = 1536, 1792, 1920, 1952
C_HEADS, C_DIM = 16, 64
GRID_W, NA_COLS = 64, 16
GRID_R = SEQ // GRID_W
BIAS_ROWS = 6
GROUPS, PER_GROUP, EXPERTS, FE = 4, 8, 32, 512
SLOTS = 64
PAIRS = EXPERTS // 2
ROUNDS_MORE = SEQ // SLOTS - 1
ROUTE = GROUPS + EXPERTS
LRU, LRU_T, LRU_CONV = 512, 4, 4
RET_HEADS, RET_DIM = 4, 128
FF2, FF2_T, FF_CONV = 6144, 48, 3
DOWN_T = FF2_T // 2

RING = 6
SLOT = 4096


def shape_constants():
    f = np.float32

    def rotation(theta, rot):
        inv = f(theta) ** (-np.arange(0, rot, 2, dtype=f) / f(rot))
        ang = np.arange(SEQ, dtype=f)[:, None] * inv[None].astype(f)
        both = np.stack([np.cos(ang), np.sin(ang)]).astype(f)
        return both.reshape(2, T, P, -1).transpose(2, 0, 1, 3).reshape(P, -1)

    first = [
        np.eye(P, dtype=f),
        np.triu(np.ones((P, P), f), 1),
        np.ones((P, P), f),
        np.zeros((P, P), f),
        np.tile(np.arange(SLOTS, dtype=f), (P, 1)),
        np.tile(np.arange(EXPERTS, dtype=f) - 64, (P, 1)),
        rotation(500000.0, 2 * A_HALF),
        rotation(500000.0, B_ROPE),
    ]
    log_g = np.log1p(-np.exp2(-5.0 - np.arange(RET_HEADS, dtype=np.float64)))
    diff = np.arange(SEQ)[None] - np.arange(P)[:, None]
    decay = np.where(diff >= 0, np.exp(np.maximum(diff, 0) * log_g[:, None, None]), 0.0) * RET_DIM ** -0.5
    decay = np.concatenate([decay, decay[:, :, :P]], axis=2)
    later = [rotation(10000.0, RET_DIM), decay.transpose(1, 0, 2).reshape(P, -1).astype(f)]
    return np.concatenate(first, 1).astype(f), np.concatenate(later, 1).astype(f)


K_ID, K_LT, K_ONE, K_ZERO, K_IO = 0, 128, 256, 384, 512
K_IE = K_IO + SLOTS
K_RA = K_IE + EXPERTS
K_RB = K_RA + 2 * T * A_HALF
K_W = K_RB + 2 * T * B_HALF
L_ROT, L_DEC = 0, 2 * T * (RET_DIM // 2)
DEC_W = SEQ + P
L_W = L_DEC + RET_HEADS * DEC_W
R_SUB, R_LAM, R_BR = 0, 128, 128 + 256
R_W = R_BR + DEPTH * ROUTE
Q_N1, Q_CW, Q_CB, Q_BA, Q_BX, Q_LAM, Q_LN, Q_N2 = 0, 8, 24, 28, 32, 36, 40, 44
Q_FW, Q_FB = 52, 52 + FF_CONV * FF2_T
Q_QN = Q_FB + FF2_T
Q_KVN = Q_QN + 2
Q_W = Q_KVN + 1


def bass_two_blocks(nc, x, w_in, w_uq, w_ukv, w_o, w_qkv, na_bias, w_o2, ln_rows, rows, cols, w_route,
                    w_gate, w_up, w_down, w_in2, gates, w_out2, ffn_up, ffn_down, table, table2, out):
    with ExitStack() as ctx:
        def sb(name, shape, dt=F32):
            return ctx.enter_context(nc.sbuf_tensor(name, shape, dt))

        def sem(name):
            return ctx.enter_context(nc.semaphore(name))

        ring = sb("ring", [P, RING, SLOT])
        X = sb("X", [P, T, D])
        XT = sb("XT", [P, C, SEQ])
        MT = sb("MT", [P, C, SEQ])
        LNR = sb("LNR", [P, 2, D])
        KT = sb("KT", [P, K_W])
        ROWS = sb("ROWS", [P, R_W])
        COLS = sb("COLS", [P, Q_W])
        WR = sb("WR", [P, DEPTH, C, ROUTE])
        ST = sb("ST", [P, 512])
        FLAG = sb("FLAG", [1, DEPTH], I32)
        ARENA_W = 17500
        arena = sb("arena", [P, ARENA_W])
        bank = [ctx.enter_context(nc.psum_tensor(f"bank{i}", [P, 512], F32)) for i in range(8)]

        def cut(off, *shape):
            n = int(np.prod(shape))
            assert off + n <= ARENA_W, (off, shape)
            v = arena[:, off:off + n]
            if len(shape) == 2:
                v = v.rearrange("p (a b) -> p a b", b=shape[1])
            if len(shape) == 3:
                v = v.rearrange("p (a b c) -> p a b c", b=shape[1], c=shape[2])
            return v

        stat_at = [0]

        def stat(*shape):
            n = int(np.prod(shape))
            v = ST[:, stat_at[0]:stat_at[0] + n]
            stat_at[0] += n
            assert stat_at[0] <= 512
            if len(shape) == 2:
                v = v.rearrange("p (a b) -> p a b", b=shape[1])
            if len(shape) == 3:
                v = v.rearrange("p (a b c) -> p a b c", b=shape[1], c=shape[2])
            return v

        ident, earlier = KT[:, K_ID:K_ID + P], KT[:, K_LT:K_LT + P]
        ones, zeros = KT[:, K_ONE:K_ONE + P], KT[:, K_ZERO:K_ZERO + P]
        iota_s, iota_e = KT[:, K_IO:K_IO + SLOTS], KT[:, K_IE:K_IE + EXPERTS]
        rot_a = KT[:, K_RA:K_RB].rearrange("p (s t f) -> p s t f", s=2, t=T)
        rot_b = KT[:, K_RB:K_W].rearrange("p (s t f) -> p s t f", s=2, t=T)

        E = cut(0, T, EVEN_IN)
        QKT = cut(3904, C, SEQ)
        QBT, KBT = QKT, XT
        PB = [cut(5952 + 512 * i, T, SEQ) for i in range(4)]
        ROT = [cut(5952 + 512 * i, 512) for i in range(4)]
        PT = [cut(8000 + 512 * i, T, SEQ) for i in range(2)]
        QB = cut(9024, T, B_HEADS * B_QK)
        KV = cut(10560, T, B_HEADS * (B_NOPE + B_V))
        KC = E[:, :, 0:B_HEADS * B_QK]
        CT = cut(12608, 3, SEQ)
        AO = cut(13376, T, A_HEADS * 2 * A_DIM)
        SQA = cut(14400, T, A_HEADS * 2 * A_DIM)
        G = cut(0, C_HEADS, BIAS_ROWS * GRID_W)
        OQ, OK, OV = cut(10560, C, SEQ), cut(12608, C, SEQ), cut(14656, T, D)
        PN = [cut(6144 + 512 * i, T, SEQ) for i in range(3)]
        PTN = [cut(7680 + 512 * i, T, SEQ) for i in range(2)]
        SEL = cut(6144, T, 2 * SLOTS)
        SELW = cut(6400, T, 2 * SLOTS)
        SWT = cut(6656, T, P)
        XG = cut(6912, C, 2 * SLOTS)
        SG = cut(7936, FE)
        H = cut(8448, FE)
        HT = cut(8960, FE // P, 2 * SLOTS)
        Y = cut(9472, D)
        KT2 = cut(0, L_W)
        rot_c = KT2[:, L_ROT:L_DEC].rearrange("p (s t f) -> p s t f", s=2, t=T)
        XL, GL = cut(1792, LRU_T, SEQ), cut(2816, LRU_T, SEQ)
        LX, LA, LI, LT_ = (cut(3840 + 1024 * i, LRU_T, SEQ) for i in range(4))
        GATE = cut(7936, 2, LRU_T * P)
        TOK = cut(8960, T, 4 * RET_HEADS * RET_DIM)
        RQK = cut(13056, C, SEQ)
        RS = cut(15104, RET_HEADS, DEC_W)
        ROT2 = [cut(15104 + 512 * i, 512) for i in range(4)]
        YR = TOK[:, :, 0:RET_HEADS * RET_DIM]
        XN = MT[:, :, :].rearrange("p c s -> p (c s)").rearrange("p (t d) -> p t d", t=T)
        ACTT = cut(1792, DOWN_T, SEQ)
        CV = [cut(8960 + 256 * i, SEQ) for i in range(4)]

        mx, nb, sm = stat(4, T), stat(4, T), stat(4, T)
        dmx, dnb, dsm = stat(2, 2, T), stat(2, 2, T), stat(2, 2, T)
        lamv, nlam = stat(2), stat(1)
        var_b, rs_b = stat(T, 2), stat(T, 2)
        var_a, rs_a = stat(T, A_HEADS), stat(T, A_HEADS)
        bst, mv = stat(T, 2, 6), stat(T, 2)
        var_l, rs_l = stat(T), stat(T)
        rg, ru = stat(T, 8), stat(T, 8)
        gmn, gsum, gw = stat(T), stat(T), stat(T)
        m1, m2, i1, i2, p2, g1, g2 = (stat(T) for _ in range(7))
        rtop, rtop2 = stat(1), stat(1)
        hst, hmv = stat(T, RET_HEADS, 6), stat(T, RET_HEADS, 2)
        var_h, rs_h = stat(T, RET_HEADS), stat(T, RET_HEADS)
        spl = [stat(LRU_T) for _ in range(5)]
        spl_series = stat(LRU_T)
        LOG = sb("LOG", [P, T, ROUTE])
        ONE1, ONE2, ELOG = sb("ONE1", [P, T, EXPERTS]), sb("ONE2", [P, T, EXPERTS]), sb("ELOG", [P, T, EXPERTS])
        RANK, WGT = sb("RANK", [P, T, EXPERTS + 2]), sb("WGT", [P, T, EXPERTS + 2])

        x_loaded, const_loaded, table2_loaded, bias_loaded = (sem(n) for n in (
            "x_loaded", "const_loaded", "table2_loaded", "bias_loaded"))
        ln_loaded = sem("ln_loaded")
        slot_loaded = [sem(f"slot_loaded{i}") for i in range(RING)]
        x_ready, xn_ready = sem("x_ready"), sem("xn_ready")
        dve_step, act_step = sem("dve_step"), sem("act_step")
        tr_done, tr_act, tr_dve = sem("tr_done"), sem("tr_act"), sem("tr_dve")
        pj_done, pj_free = sem("pj_done"), [sem("pj_free0"), sem("pj_free1")]
        var_ready, std_ready = sem("var_ready"), sem("std_ready")
        rope_ready, rank_ready, mla_ready, lam_ready, lam_exp = (sem(n) for n in (
            "rope_ready", "rank_normed", "mla_ready", "lam_ready", "lam_exp"))
        d_score, d_nb, d_exp, d_w, d_pt, d_ptc, d_pv, d_o = (sem(n) for n in (
            "d_score_done", "d_nb_ready", "d_exp_done", "d_w_ready", "d_pT_done", "d_pT_copied", "d_pv_done",
            "d_o_copied"))
        ao_ready = sem("ao_ready")
        a_score, a_free, a_nb, a_exp, a_p, a_pt, a_ptc, a_pv, a_o = (sem(n) for n in (
            "score_done", "score_free", "nb_ready", "exp_done", "prob_ready", "pT_done", "pT_copied", "pv_done",
            "o_copied"))
        logits_done, r_gmax, r_gexp, r_d, r_p2, r_one, rank_done, r_top, top_done, flag_ready, route_ready = (
            sem(n) for n in ("logits_done", "group_max", "group_exp", "top_gap", "second_exp", "chosen_ready",
                             "rank_done", "rank_top", "top_done", "flag_ready", "route_ready"))

        def signals(tag):
            return {n: sem(f"{tag}_{n}") for n in (
                "sel_ready", "selw_ready", "gather_lo", "gather_hi", "xg_lo", "xg_hi", "gate_done", "up_done",
                          "silu_done", "h_ready", "hT_done", "hT_copied", "swt_done", "swt_copied", "y0_done",
                          "y1_done", "y0_copied", "y1_copied")}

        moe = signals("moe")
        over = [signals(f"over{l}") for l in range(DEPTH)]
        over_loaded = [[sem(f"over{l}_loaded{i}") for i in range(RING)] for l in range(DEPTH)]
        over_free = [sem(f"over{l}_slots_free") for l in range(DEPTH)]
        over_shift = [sem(f"over{l}_shifted") for l in range(DEPTH)]
        acc_done = sem("acc_done")
        lru_cv, lru_cvd, lru_gm, lru_g, lru_t, lru_a, lru_sq, lru_sqr, lru_y = (sem(n) for n in (
            "lru_conv0", "lru_conv", "lru_gate_mm", "lru_gates", "lru_tanh", "lru_decay", 
            "lru_squares", "lru_sum", "lru_out"))
        sp_exp, sp_in = sem("softplus_exp"), sem("softplus_in")
        r_rope, r_sc, r_scd, r_o, r_oc, r_y, r_silu = (sem(n) for n in (
            "ret_rope", "ret_score", "ret_decayed", "ret_out", "ret_out_copied", "ret_y", "ret_silu"))
        f_up, f_cv0, f_cv, f_act, f_gelu, f_down = (sem(n) for n in (
            "ffn_up_done", "ffn_conv0", "ffn_conv", "ffn_act", "ffn_gelu", "ffn_down_done"))
        out_ready, stored = sem("out_ready"), sem("stored")

        def columns(w, n, width=512):
            return w[:, n * 512:n * 512 + width].rearrange("(c p) f -> p c f", p=P)

        def slot(i, a, b):
            return ring[:, i % RING, 0:a * b].rearrange("p (a b) -> p a b", b=b)

        items = []

        def item(src, a, b, used, value):
            items.append((src, slot(len(items), a, b), used, value))
            return len(items) - 1

        chunk = 0
        I_EIN = [item(columns(w_in, n, min(512, EVEN_IN - 512 * n)), C, min(512, EVEN_IN - 512 * n), pj_done,
                      2 * n + 2) for n in range(4)]
        I_UQ = item(w_uq.rearrange("(c p) f -> p c f", p=P), 2, 768, pj_done, 12)
        I_UKV = item(w_ukv.rearrange("(c p) f -> p c f", p=P), 1, 1024, pj_done, 16)
        I_EO = [item(columns(w_o, n), C, 512, pj_done, 18 + 2 * n) for n in range(2)]
        G_EIN, G_UQ, G_UKV, G_EO, G_QKV, G_OO, G_IN2, G_OUT2 = 0, 4, 6, 8, 10, 16, 18, 24

        def expert_source(l, e, k):
            if k < 2:
                return w_gate[l, bass.ds(e, 1)].rearrange("o (c p) f -> p (o c) f", p=P)
            if k < 4:
                return w_up[l, bass.ds(e, 1)].rearrange("o (c p) f -> p (o c) f", p=P)
            return w_down[l, bass.ds(e, 1)].rearrange("o (j p) f -> p (o j) f", p=P)

        def expert_view(i, k):
            return slot(i, C, FE) if k < 4 else slot(i, FE // P, D)

        def expert_items(l):
            first = len(items)
            for p in range(PAIRS):
                for k in range(6):
                    used = (moe["gate_done"], moe["up_done"], moe["y1_done"])[k // 2]
                    items.append((None, None, used, PAIRS * l + p + 1))
            return first

        I_MOE = [expert_items(0)]
        I_QKV = [item(columns(w_qkv, n), C, 512, pj_done, 2 * (G_QKV + n) + 2) for n in range(6)]
        I_OO = [item(columns(w_o2, n), C, 512, pj_done, 2 * (G_OO + n) + 2) for n in range(2)]
        I_MOE.append(expert_items(1))
        I_IN2 = [item(columns(w_in2, n), C, 512, pj_done, 2 * (G_IN2 + n) + 2) for n in range(6)]
        I_OUT2 = [item(columns(w_out2, n), C, 512, pj_done, 2 * (G_OUT2 + n) + 2) for n in range(2)]
        I_UP = [item(columns(ffn_up, n), C, 512, f_up, 4 * n + 4) for n in range(FF2 // 512)]
        I_DN = [item(ffn_down[512 * n:512 * (n + 1), :].rearrange("(c p) f -> p c f", p=P), 4, D, f_down, n + 1)
                for n in range(6)]

        def arrived(i):
            return slot_loaded[i % RING], 16 * (i // RING + 1)

        TR = {}
        tr_groups = 0
        for name, groups in (("x", 4), ("qk", 4), ("c", 2), ("qb", 4), ("kb", 4), ("ao", 2), ("ln0", 4), ("ln1", 4),
                             ("ln2", 4), ("n1", 4), ("rqk", 4), ("yr", 2), ("n2", 4)):
            TR[name] = (tr_groups, groups)
            tr_groups += groups

        N_MLA0, N_NA0 = 0, B_HEADS

        block = ctx.enter_context(nc.Block())

        @block.sync
        def _(sp):
            sp.dma_start(X[:, :, :], x.rearrange("(t p) d -> p t d", p=P)).then_inc(x_loaded, 16)

            def load(i):
                src, view, _, _ = items[i]
                if i >= RING:
                    sp.wait_ge(items[i - RING][2], items[i - RING][3])
                sp.dma_start(view, src).then_inc(slot_loaded[i % RING], 16)

            def load_expert(l, k, e, sems):
                i = I_MOE[l] + k
                sp.dma_start(expert_view(i, k), expert_source(l, e, k)).then_inc(sems[i % RING], 16)

            def load_experts(l):
                for k in range(6):
                    sp.wait_ge(items[I_MOE[l] + k - RING][2], items[I_MOE[l] + k - RING][3])
                    load_expert(l, k, k % 2, slot_loaded)
                with sp.Fori(1, PAIRS) as p:
                    for k in range(6):
                        used = (moe["gate_done"], moe["up_done"], moe["y1_done"])[k // 2]
                        sp.wait_ge(used, p + PAIRS * l)
                        load_expert(l, k, p * 2 + k % 2, slot_loaded)
                sp.wait_ge(flag_ready, l + 1)
                more = sp.value_load(FLAG[0:1, l:l + 1], min_val=0, max_val=1)
                with sp.If(more > 0):
                    with sp.Fori(0, ROUNDS_MORE) as r:
                        with sp.Fori(0, PAIRS) as p:
                            sp.wait_ge(over_free[l], r * PAIRS + p + 1)
                            for k in range(6):
                                load_expert(l, k, p * 2 + k % 2, over_loaded[l])
                    sp.wait_ge(over_free[l], ROUNDS_MORE * PAIRS + 1)

            for i in range(I_MOE[0]):
                load(i)
            load_experts(0)
            for i in I_QKV + I_OO:
                load(i)
                if i == I_QKV[0]:
                    sp.dma_start(G[:, :, :], na_bias).then_inc(bias_loaded, 16)
            load_experts(1)
            for i in I_IN2 + I_OUT2 + I_UP + I_DN:
                load(i)
                if i == I_IN2[5]:
                    sp.dma_start(KT2[:, :], table2).then_inc(table2_loaded, 16)
                    sp.dma_start(GATE[:, :, :], gates).then_inc(table2_loaded, 16)
            sp.wait_ge(out_ready, 1)
            sp.dma_start(out.rearrange("(t p) d -> p t d", p=P), X[:, :, :]).then_inc(stored, 16)
            sp.wait_ge(stored, 16)

        @block.gpsimd
        def _(pool):
            pool.dma_start(LNR[:, :, :].rearrange("p a d -> p (a d)"),
                           ln_rows[0, :].partition_broadcast(P)).then_inc(ln_loaded, 16)
            for n in range(1, 6):
                pool.wait_ge(*((x_ready, n) if n < 5 else (r_y, 1)))
                pool.dma_start(LNR[:, :, :].rearrange("p a d -> p (a d)"),
                               ln_rows[n, :].partition_broadcast(P)).then_inc(ln_loaded, 16)

        @block.tensor
        def _(pe):
            def transposes(name, source, width=P, blocks=None):
                k0, groups = TR[name]
                blocks = 2 * groups if blocks is None else blocks
                for g in range(groups):
                    k = k0 + g
                    if k >= 4:
                        pe.wait_ge(tr_dve if k % 2 else tr_act, (k - 4) // 2 + 1)
                    for b in range(2 * g, min(2 * g + 2, blocks)):
                        for t in range(T):
                            last = nc.tensor.transpose(
                                bank[4 + k % 4][0:width, (b % 2) * SEQ + t * P:(b % 2) * SEQ + (t + 1) * P],
                                source(b, t), ident)
                    last.then_inc(tr_done, 1)

            def transposed(name):
                k = sum(TR[name])
                pe.wait_ge(tr_act, k // 2)
                pe.wait_ge(tr_dve, k // 2)

            def project(g, i, lhsT, rhs, kt):
                pe.wait_ge(*arrived(i))
                for t in range(T):
                    if g >= 2:
                        pe.wait_ge(pj_free[t], g - 1)
                    width = rhs(0).shape[1]
                    for c in range(kt):
                        last = nc.tensor.matmul(bank[g % 2 * 2 + t][:, 0:width], lhsT(c, t), rhs(c),
                                                start=(c == 0), stop=(c == kt - 1))
                    last.then_inc(pj_done, 1)

            def project_t(g, i):
                pe.wait_ge(*arrived(i))
                for half in range(2):
                    if g >= 2:
                        pe.wait_ge(pj_free[half], g - 1)
                    for f in range(2):
                        for c in range(C):
                            last = nc.tensor.matmul(
                                bank[g % 2 * 2 + half][:, f * SEQ:(f + 1) * SEQ],
                                slot(i, C, 512)[:, c, (2 * half + f) * P:(2 * half + f + 1) * P],
                                XT[:, c, :], start=(c == 0), stop=(c == C - 1))
                    last.then_inc(pj_done, 1)

            def x_tile(c, t):
                return XT[:, c, t * P:(t + 1) * P]

            def mixed_tile(c, t):
                return MT[:, c, t * P:(t + 1) * P]

            def attention(a0, n, q, k, v, probs, probs_t, free):
                for i in range(n + 3):
                    if i < n:
                        a = a0 + i
                        if i >= 3:
                            pe.wait_ge(free, i - 2)
                        for t in range(T):
                            last = nc.tensor.matmul(bank[4 + a % 3][:, t * SEQ:(t + 1) * SEQ], q(i, t), k(i),
                                                    start=True, stop=True)
                        last.then_inc(a_score, 1)
                    if 0 <= i - 2 < n:
                        a = a0 + i - 2
                        pe.wait_ge(a_p, a + 1)
                        if a >= 2:
                            pe.wait_ge(a_ptc, a - 1)
                        for t in range(T):
                            for kt in range(T):
                                last = nc.tensor.transpose(
                                    bank[a % 2][:, kt * SEQ + t * P:kt * SEQ + (t + 1) * P],
                                    probs[a % 3][:, t, kt * P:(kt + 1) * P], ident)
                        last.then_inc(a_pt, 1)
                    if 0 <= i - 3 < n:
                        a = a0 + i - 3
                        pair = a // 2
                        pe.wait_ge(a_ptc, a + 1)
                        if a % 2 == 0 and pair >= 2:
                            pe.wait_ge(a_o, pair - 1)
                        for kt in range(T):
                            last = nc.tensor.matmul(bank[2 + pair % 2][(a % 2) * 64:(a % 2) * 64 + 64, 0:SEQ],
                                                    v(i - 3, kt), probs_t[a % 2][:, kt, :],
                                                    start=(kt == 0), stop=(kt == T - 1))
                        last.then_inc(a_pv, 1)

            def gather(s):
                for c in range(C):
                    for t in range(T):
                        last = nc.tensor.matmul(bank[6 + c // 4][:, c % 4 * P:(c % 4 + 1) * P],
                                                X[:, t, c * P:(c + 1) * P], SEL[:, t, :],
                                                start=(t == 0), stop=(t == T - 1))
                    if c == C // 2 - 1:
                        last.then_inc(s["gather_lo"], 1)
                last.then_inc(s["gather_hi"], 1)

            def experts(l, s, n, g, loaded, load_count, used=None):
                def weights(k):
                    i = I_MOE[l] + k
                    pe.wait_ge(loaded[i % RING], load_count(i))
                    return expert_view(i, k)

                pe.wait_ge(s["xg_lo"], g + 1)
                pe.wait_ge(s["xg_hi"], g + 1)
                for m, done in ((0, s["gate_done"]), (1, s["up_done"])):
                    w = [weights(2 * m), weights(2 * m + 1)]
                    for c in range(C):
                        for e in range(2):
                            last = nc.tensor.matmul(bank[4 + m][64 * e:64 * e + 64, :],
                                                    XG[:, c, 64 * e:64 * e + 64], w[e][:, c, :],
                                                    start=(c == 0), stop=(c == C - 1))
                    last.then_inc(done, 1)
                pe.wait_ge(s["sel_ready"], g + 2)
                gather(s)
                pe.wait_ge(s["h_ready"], n + 1)
                for j in range(FE // P):
                    last = nc.tensor.transpose(bank[4][:, j * P:(j + 1) * P], H[:, j * P:(j + 1) * P], ident)
                last.then_inc(s["hT_done"], 1)
                pe.wait_ge(s["selw_ready"], n + 1)
                for t in range(T):
                    last = nc.tensor.transpose(bank[5][:, t * P:(t + 1) * P], SELW[:, t, :], ident)
                last.then_inc(s["swt_done"], 1)
                w = [weights(4), weights(5)]
                pe.wait_ge(s["hT_copied"], n + 1)
                for half, free, done in ((0, s["xg_lo"], s["y0_done"]), (1, s["xg_hi"], s["y1_done"])):
                    pe.wait_ge(free, g + 2)
                    for j in range(FE // P):
                        for e in range(2):
                            last = nc.tensor.matmul(bank[6 + half][64 * e:64 * e + 64, :],
                                                    HT[:, j, 64 * e:64 * e + 64],
                                                    w[e][:, j, 512 * half:512 * half + 512],
                                                    start=(j == 0), stop=(j == FE // P - 1))
                    last.then_inc(done, 1)
                pe.wait_ge(s["swt_copied"], n + 1)
                for half, copied in ((0, s["y0_copied"]), (1, s["y1_copied"])):
                    pe.wait_ge(copied, n + 1)
                    for t in range(T):
                        last = nc.tensor.matmul(bank[2 * t + half][:, :], SWT[:, t, :],
                                                Y[:, 512 * half:512 * half + 512],
                                                start=False, stop=False, skip_group_check=True)
                if used is not None:
                    last.then_inc(used, 1)

            def moe_layer(l):
                for t in range(T):
                    for c in range(C):
                        last = nc.tensor.matmul(bank[4][:, t * 64:t * 64 + ROUTE], x_tile(c, t), WR[:, l, c, :],
                                                start=(c == 0), stop=(c == C - 1))
                last.then_inc(logits_done, 1)
                for b in range(4):
                    nc.tensor.matmul(bank[b][:, :], zeros, XT[:, 0:2, :].rearrange("p a b -> p (a b)"),
                                     start=True, stop=False, skip_group_check=True)
                pe.wait_ge(r_one, l + 1)
                for t in range(T):
                    if t:
                        nc.tensor.matmul(bank[4][:, t * 64:t * 64 + EXPERTS], ones, ELOG[:, 0, :],
                                         start=True, stop=False)
                    last = nc.tensor.matmul(bank[4][:, t * 64:t * 64 + EXPERTS], earlier, ELOG[:, t, :],
                                            start=(t == 0), stop=True)
                last.then_inc(rank_done, 1)
                pe.wait_ge(r_top, l + 1)
                nc.tensor.transpose(bank[5][0:1, 0:P], rtop, ident).then_inc(top_done, 1)
                pe.wait_ge(moe["sel_ready"], (PAIRS + 1) * l + 1)
                gather(moe)
                with pe.Fori(0, PAIRS) as p:
                    experts(l, moe, p + PAIRS * l, p + (PAIRS + 1) * l, slot_loaded,
                            lambda i: (p + i // RING + 1) * 16)
                pe.wait_ge(flag_ready, l + 1)
                more = pe.value_load(FLAG[0:1, l:l + 1], min_val=0, max_val=1)
                with pe.If(more > 0):
                    s = over[l]
                    pe.drain().then_inc(over_free[l], 1)
                    with pe.Fori(0, ROUNDS_MORE) as r:
                        pe.wait_ge(s["sel_ready"], r * (PAIRS + 1) + 1)
                        gather(s)
                        with pe.Fori(0, PAIRS) as p:
                            n = r * PAIRS + p
                            experts(l, s, n, r * (PAIRS + 1) + p, over_loaded[l], lambda i: (r * PAIRS + p + 1) * 16,
                                    over_free[l])
                pe.drain().then_inc(acc_done, 1)

            pe.wait_ge(x_loaded, 16)
            pe.wait_ge(const_loaded, 16 * 4)
            transposes("x", lambda b, t: X[:, t, b * P:(b + 1) * P])
            transposed("x")
            for n in range(4):
                w = min(512, EVEN_IN - 512 * n)
                project(G_EIN + n, I_EIN[n], x_tile, lambda c: slot(I_EIN[n], C, w)[:, c, :], C)
            pe.wait_ge(rope_ready, 1)
            transposes("qk", lambda b, t: E[:, t, b * P:(b + 1) * P])
            pe.wait_ge(rank_ready, 1)
            transposes("c", lambda b, t: E[:, t, CQ0 + b * P:CQ0 + (b + 1) * P], blocks=3)
            transposed("c")
            for n in range(2):
                project(G_UQ + n, I_UQ, lambda c, t: CT[:, c, t * P:(t + 1) * P],
                        lambda c: slot(I_UQ, 2, 768)[:, c, 384 * n:384 * n + 384], 2)
            for n in range(2):
                project(G_UKV + n, I_UKV, lambda c, t: CT[:, 2, t * P:(t + 1) * P],
                        lambda c: slot(I_UKV, 1, 1024)[:, 0, 512 * n:512 * n + 512], 1)
            for i in range(A_HEADS + 2):
                if i < A_HEADS:
                    if i >= 2:
                        pe.wait_ge(d_exp, 2 * (i - 1))
                    for m in range(2):
                        half = slice(m * A_DIM, (m + 1) * A_DIM)
                        for t in range(T):
                            last = nc.tensor.matmul(bank[4 + 2 * (i % 2) + m][:, t * SEQ:(t + 1) * SEQ],
                                                    QKT[half, i, t * P:(t + 1) * P], QKT[half, 4 + i, :],
                                                    start=True, stop=True)
                        last.then_inc(d_score, 1)
                if 0 <= i - 1 < A_HEADS:
                    h = i - 1
                    pe.wait_ge(d_w, h + 1)
                    if h >= 2:
                        pe.wait_ge(d_ptc, h - 1)
                    for t in range(T):
                        for kt in range(T):
                            last = nc.tensor.transpose(bank[h % 2][:, kt * SEQ + t * P:kt * SEQ + (t + 1) * P],
                                                       PB[2 * (h % 2)][:, t, kt * P:(kt + 1) * P], ident)
                    last.then_inc(d_pt, 1)
                if i >= 2:
                    h = i - 2
                    pe.wait_ge(d_ptc, h + 1)
                    if h >= 2:
                        pe.wait_ge(d_o, h - 1)
                    for t in range(T):
                        for kt in range(T):
                            last = nc.tensor.matmul(bank[2 + h % 2][:, t * P:(t + 1) * P],
                                                    PT[h % 2][:, kt, t * P:(t + 1) * P],
                                                    E[:, kt, VA0 + h * P:VA0 + (h + 1) * P],
                                                    start=(kt == 0), stop=(kt == T - 1))
                    last.then_inc(d_pv, 1)
            pe.wait_ge(mla_ready, 1)
            pe.wait_ge(d_o, A_HEADS)
            transposes("qb", lambda b, t: QB[:, t, b * B_QK:(b + 1) * B_QK], B_QK)
            transposes("kb", lambda b, t: KC[:, t, b * B_QK:(b + 1) * B_QK], B_QK)
            transposed("kb")
            attention(N_MLA0, B_HEADS, lambda h, t: QBT[0:B_QK, h, t * P:(t + 1) * P], lambda h: KBT[0:B_QK, h, :],
                      lambda h, kt: KV[:, kt, h * 128 + B_NOPE:(h + 1) * 128], PB, PT, a_exp)
            pe.wait_ge(ao_ready, 1)
            transposes("ao", lambda b, t: AO[:, t, b * P:(b + 1) * P])
            transposed("ao")
            pe.wait_ge(a_o, B_HEADS // 2)
            for n in range(2):
                project(G_EO + n, I_EO[n], mixed_tile, lambda c: slot(I_EO[n], C, 512)[:, c, :], C)
            pe.wait_ge(x_ready, 1)
            transposes("ln0", lambda b, t: X[:, t, b * P:(b + 1) * P])
            transposed("ln0")
            moe_layer(0)

            pe.wait_ge(x_ready, 2)
            transposes("ln1", lambda b, t: X[:, t, b * P:(b + 1) * P])
            transposed("ln1")
            for n in range(4):
                project_t(G_QKV + n, I_QKV[n])
            for n in range(4, 6):
                project(G_QKV + n, I_QKV[n], x_tile, lambda c: slot(I_QKV[n], C, 512)[:, c, :], C)
            for t in range(2):
                pe.wait_ge(pj_free[t], G_OO)

            def head_rows(h):
                return slice(h % 2 * C_DIM, h % 2 * C_DIM + C_DIM)

            attention(N_NA0, C_HEADS, lambda h, t: OQ[head_rows(h), h // 2, t * P:(t + 1) * P],
                      lambda h: OK[head_rows(h), h // 2, :],
                      lambda h, kt: OV[:, kt, h * C_DIM:(h + 1) * C_DIM], PN, PTN, a_free)
            pe.wait_ge(a_o, (B_HEADS + C_HEADS) // 2)
            for n in range(2):
                project(G_OO + n, I_OO[n], mixed_tile, lambda c: slot(I_OO[n], C, 512)[:, c, :], C)
            pe.wait_ge(x_ready, 3)
            transposes("ln2", lambda b, t: X[:, t, b * P:(b + 1) * P])
            transposed("ln2")
            moe_layer(1)

            pe.wait_ge(xn_ready, 1)
            transposes("n1", lambda b, t: XN[:, t, b * P:(b + 1) * P])
            transposed("n1")
            for n in range(2):
                project_t(G_IN2 + n, I_IN2[n])
            for n in range(2, 6):
                project(G_IN2 + n, I_IN2[n], x_tile, lambda c: slot(I_IN2[n], C, 512)[:, c, :], C)
            pe.wait_ge(table2_loaded, 32)
            pe.wait_ge(lru_cvd, LRU_T)
            for m in range(2):
                for half in range(2):
                    for f in range(2):
                        c = 2 * half + f
                        last = nc.tensor.matmul(bank[4 + 2 * m + half][:, f * SEQ:(f + 1) * SEQ],
                                                GATE[:, m, c * P:(c + 1) * P], LX[:, c, :], start=True, stop=True)
                    last.then_inc(lru_gm, 1)
            pe.wait_ge(lru_sq, 1)
            for c in range(LRU_T):
                last = nc.tensor.matmul(bank[0][:, 0:SEQ], ones, LT_[:, c, :], start=(c == 0), stop=(c == LRU_T - 1))
            last.then_inc(lru_sqr, 1)
            pe.wait_ge(r_rope, 1)
            pe.wait_ge(lru_g, 4)
            transposes("rqk", lambda b, t: TOK[:, t, b * P:(b + 1) * P])
            transposed("rqk")
            for h in range(RET_HEADS):
                nc.tensor.matmul(bank[4 + h][:, 0:SEQ], RQK[:, 4 + h, 0:P], RQK[:, h, :], start=True, stop=True)
                nc.tensor.matmul(bank[4 + h][:, SEQ:DEC_W], RQK[:, 4 + h, P:SEQ], RQK[:, h, P:SEQ],
                                 start=True, stop=True).then_inc(r_sc, 1)
            for h in range(RET_HEADS):
                pe.wait_ge(r_scd, h + 1)
                if h >= 2:
                    pe.wait_ge(r_oc, h - 1)
                b = bank[2 + h % 2]
                v = [TOK[:, t, 1024 + h * P:1024 + (h + 1) * P] for t in range(T)]
                nc.tensor.matmul(b[:, 0:P], RS[:, h, 0:P], v[0], start=True, stop=True)
                nc.tensor.matmul(b[:, P:SEQ], RS[:, h, P:SEQ], v[0], start=True, stop=False)
                nc.tensor.matmul(b[:, P:SEQ], RS[:, h, SEQ:DEC_W], v[1], start=False, stop=True).then_inc(r_o, 1)
            pe.wait_ge(r_y, 1)
            transposes("yr", lambda b, t: YR[:, t, b * P:(b + 1) * P])
            transposed("yr")
            pe.wait_ge(lru_y, 1)
            for n in range(2):
                project(G_OUT2 + n, I_OUT2[n], mixed_tile, lambda c: slot(I_OUT2[n], C, 512)[:, c, :], C)
            pe.wait_ge(xn_ready, 2)
            transposes("n2", lambda b, t: XN[:, t, b * P:(b + 1) * P])
            transposed("n2")
            for f in range(FF2_T):
                i = I_UP[f // 4]
                if f % 4 == 0:
                    pe.wait_ge(*arrived(i))
                if f >= 4:
                    pe.wait_ge(f_cv, f - 3)
                for c in range(C):
                    last = nc.tensor.matmul(bank[f % 4][:, 0:SEQ], slot(i, C, 512)[:, c, f % 4 * P:(f % 4 + 1) * P],
                                            XT[:, c, :], start=(c == 0), stop=(c == C - 1))
                last.then_inc(f_up, 1)
            for n in range(6):
                i = I_DN[n]
                pe.wait_ge(*arrived(i))
                pe.wait_ge(f_act, 4 * n + 4)
                for c in range(4):
                    for t in range(T):
                        for half in range(2):
                            last = nc.tensor.matmul(bank[4 + 2 * t + half][:, :],
                                                    ACTT[:, 4 * n + c, t * P:(t + 1) * P],
                                                    slot(i, 4, D)[:, c, 512 * half:512 * half + 512],
                                                    start=(n == 0 and c == 0), stop=(n == 5 and c == 3))
                last.then_inc(f_down, 1)

        @block.scalar
        def _(act):
            act.dma_start(KT[:, :], table).then_inc(const_loaded, 16)
            act.dma_start(COLS[:, :], cols).then_inc(const_loaded, 16)
            act.dma_start(ROWS[:, :], rows[0, :].partition_broadcast(P)).then_inc(const_loaded, 16)
            act.dma_start(WR[:, :, :, :], w_route).then_inc(const_loaded, 16)

            def evac_transposes(name, dest, width=P, blocks=None, gain=None):
                k0, groups = TR[name]
                blocks = 2 * groups if blocks is None else blocks
                for g in range(groups):
                    k = k0 + g
                    if k % 2:
                        continue
                    act.wait_ge(tr_done, k + 1)
                    n = min(2, blocks - 2 * g)
                    if gain is None:
                        last = nc.scalar.copy(dest(2 * g, n), bank[4 + k % 4][0:width, 0:n * SEQ].rearrange(
                            "p (a b) -> p a b", b=SEQ))
                    else:
                        for b in range(n):
                            last = nc.scalar.activation(dest(2 * g + b, 1), bank[4 + k % 4][0:width, b * SEQ:(b + 1) * SEQ],
                                                        ACT.Copy, scale=gain(2 * g + b))
                    last.then_inc(tr_act, 1)

            def evac_chunk(g, dest):
                act.wait_ge(pj_done, 2 * g + 1)
                nc.scalar.copy(dest, bank[g % 2 * 2][:, 0:dest.free_size()].rearrange("p (a b) -> p a b", b=dest.shape[2])
                               if len(dest.shape) == 3 else bank[g % 2 * 2][:, 0:dest.shape[1]]).then_inc(pj_free[0], 1)

            roots = [0]

            def root(v):
                roots[0] += 1
                act.wait_ge(var_ready, roots[0])
                nc.scalar.activation(v, v, ACT.Sqrt).then_inc(std_ready, 1)

            def attention(a0, n, probs, probs_t, scale):
                for i in range(n + 2):
                    if i < n:
                        a = a0 + i
                        act.wait_ge(a_nb, a + 1)
                        if a >= 3 and scale is not None:
                            act.wait_ge(a_pt, a - 2)
                        for t in range(T):
                            src = bank[4 + a % 3][:, t * SEQ:(t + 1) * SEQ] if scale is not None else probs[a % 3][:, t, :]
                            last = nc.scalar.activation(probs[a % 3][:, t, :], src, ACT.Exp, bias=nb[:, a % 4, t:t + 1],
                                                        scale=1.0 if scale is None else scale,
                                                        accum_out=sm[:, a % 4, t:t + 1])
                        last.then_inc(a_exp, 1)
                    if i >= 2:
                        a = a0 + i - 2
                        act.wait_ge(a_pt, a + 1)
                        if a >= 2:
                            act.wait_ge(a_pv, a - 1)
                        nc.scalar.copy(probs_t[a % 2][:, :, :], bank[a % 2][:, :].rearrange("p (a b) -> p a b", b=SEQ))\
                            .then_inc(a_ptc, 1)

            def experts(s, n, g):
                act.wait_ge(s["gate_done"], n + 1)
                nc.scalar.activation(SG, bank[4][:, :], ACT.Silu).then_inc(s["silu_done"], 1)
                act.wait_ge(s["gather_lo"], g + 2)
                nc.scalar.copy(XG[:, 0:4, :], bank[6][:, :].rearrange("p (a b) -> p a b", b=P)).then_inc(s["xg_lo"], 1)
                act.wait_ge(s["hT_done"], n + 1)
                nc.scalar.copy(HT[:, :, :], bank[4][:, :].rearrange("p (a b) -> p a b", b=P)).then_inc(s["hT_copied"], 1)
                act.wait_ge(s["swt_done"], n + 1)
                nc.scalar.copy(SWT[:, :, :], bank[5][:, 0:SEQ].rearrange("p (a b) -> p a b", b=P)).then_inc(s["swt_copied"], 1)
                act.wait_ge(s["y0_done"], n + 1)
                nc.scalar.copy(Y[:, 0:512], bank[6][:, :]).then_inc(s["y0_copied"], 1)

            def first_tokens(s, g):
                act.wait_ge(s["gather_lo"], g + 1)
                nc.scalar.copy(XG[:, 0:4, :], bank[6][:, :].rearrange("p (a b) -> p a b", b=P)).then_inc(s["xg_lo"], 1)

            def moe_layer(l):
                act.wait_ge(r_gmax, l + 1)
                for t in range(T):
                    last = nc.scalar.activation(rg[:, t, 0:GROUPS], LOG[:, t, 0:GROUPS], ACT.Exp, bias=gmn[:, t:t + 1],
                                                accum_out=gsum[:, t:t + 1])
                last.then_inc(r_gexp, 1)
                act.wait_ge(r_d, l + 1)
                nc.scalar.activation(p2, p2, ACT.Exp).then_inc(r_p2, 1)
                first_tokens(moe, (PAIRS + 1) * l)
                with act.Fori(0, PAIRS) as p:
                    experts(moe, p + PAIRS * l, p + (PAIRS + 1) * l)
                act.wait_ge(flag_ready, l + 1)
                more = act.value_load(FLAG[0:1, l:l + 1], min_val=0, max_val=1)
                with act.If(more > 0):
                    with act.Fori(0, ROUNDS_MORE) as r:
                        first_tokens(over[l], r * (PAIRS + 1))
                        with act.Fori(0, PAIRS) as p:
                            experts(over[l], r * PAIRS + p, r * (PAIRS + 1) + p)

            act.wait_ge(const_loaded, 64)
            evac_transposes("x", lambda b, n: XT[:, b:b + n, :])
            for n in range(4):
                evac_chunk(G_EIN + n, E[:, 0, 512 * n:min(512 * n + 512, EVEN_IN)])
            act.wait_ge(lam_ready, 1)
            nc.scalar.activation(lamv, lamv, ACT.Exp).then_inc(lam_exp, 1)
            root(var_b[:, :, :])
            evac_transposes("qk", lambda b, n: QKT[:, b:b + n, :])
            evac_transposes("c", lambda b, n: CT[:, b, :], blocks=3, gain=lambda b: COLS[:, Q_QN + b:Q_QN + b + 1])
            for n in range(2):
                evac_chunk(G_UQ + n, QB[:, 0, 384 * n:384 * n + 384])
            for n in range(2):
                evac_chunk(G_UKV + n, KV[:, 0, 512 * n:512 * n + 512])
            for i in range(A_HEADS + 1):
                if i < A_HEADS:
                    for m in range(2):
                        act.wait_ge(d_nb, 2 * i + m + 1)
                        if i >= 2:
                            act.wait_ge(d_pt, i - 1)
                        for t in range(T):
                            last = nc.scalar.activation(PB[2 * (i % 2) + m][:, t, :],
                                                        bank[4 + 2 * (i % 2) + m][:, t * SEQ:(t + 1) * SEQ], ACT.Exp,
                                                        bias=dnb[:, i % 2, m, t:t + 1], scale=A_DIM ** -0.5,
                                                        accum_out=dsm[:, i % 2, m, t:t + 1])
                        last.then_inc(d_exp, 1)
                if i >= 1:
                    h = i - 1
                    act.wait_ge(d_pt, h + 1)
                    if h >= 2:
                        act.wait_ge(d_pv, h - 1)
                    nc.scalar.copy(PT[h % 2][:, :, :], bank[h % 2][:, :].rearrange("p (a b) -> p a b", b=SEQ))\
                        .then_inc(d_ptc, 1)
            evac_transposes("qb", lambda b, n: QBT[0:B_QK, b:b + n, :], B_QK)
            evac_transposes("kb", lambda b, n: KBT[0:B_QK, b:b + n, :], B_QK)
            root(var_a[:, :, :])
            attention(N_MLA0, B_HEADS, PB, PT, B_QK ** -0.5)
            evac_transposes("ao", lambda b, n: MT[:, b:b + n, :])
            root(var_l)
            evac_transposes("ln0", lambda b, n: XT[:, b:b + n, :])
            moe_layer(0)
            root(var_l)
            evac_transposes("ln1", lambda b, n: XT[:, b:b + n, :])
            for n in range(4):
                evac_chunk(G_QKV + n, (OQ if n < 2 else OK)[:, 4 * (n % 2):4 * (n % 2) + 2, :])
            for n in range(2):
                evac_chunk(G_QKV + 4 + n, OV[:, 0, 512 * n:512 * n + 512])
            attention(N_NA0, C_HEADS, PN, PTN, None)
            root(var_l)
            evac_transposes("ln2", lambda b, n: XT[:, b:b + n, :])
            moe_layer(1)
            root(var_l)
            root(var_l)
            evac_transposes("n1", lambda b, n: XT[:, b, :], gain=lambda b: COLS[:, Q_N1 + b:Q_N1 + b + 1])
            evac_chunk(G_IN2, XL[:, 0:2, :])
            act.wait_ge(pj_done, 2 * (G_IN2 + 1) + 1)
            nc.scalar.activation(GL[:, 0:2, :], bank[(G_IN2 + 1) % 2 * 2][:, :].rearrange("p (a b) -> p a b", b=SEQ),
                                 ACT.Gelu_apprx_tanh).then_inc(pj_free[0], 1)
            act.wait_ge(pj_done, 2 * (G_IN2 + 1) + 2)
            act.wait_ge(pj_free[1], G_IN2 + 1)
            nc.scalar.activation(GL[:, 2:4, :], bank[(G_IN2 + 1) % 2 * 2 + 1][:, :].rearrange("p (a b) -> p a b", b=SEQ),
                                 ACT.Gelu_apprx_tanh).then_inc(pj_free[1], 1)
            for n in range(4):
                evac_chunk(G_IN2 + 2 + n, TOK[:, 0, 512 * n:512 * n + 512])
            act.wait_ge(sp_in, 1)
            nc.scalar.activation(spl[1], spl[1], ACT.Exp).then_inc(sp_exp, 1)
            for c in range(LRU_T):
                for m, dst, bcol in ((0, LA, Q_BA), (1, LI, Q_BX)):
                    act.wait_ge(lru_gm, 2 * m + c // 2 + 1)
                    act.wait_ge(sp_in, 2)
                    last = nc.scalar.activation(dst[:, c, :], bank[4 + 2 * m + c // 2][:, c % 2 * SEQ:(c % 2 + 1) * SEQ],
                                                ACT.Tanh, scale=0.5, bias=spl[3 + m][:, c:c + 1])
                last.then_inc(lru_g, 1)
            act.wait_ge(lru_t, 1)
            nc.scalar.activation(LT_[:, :, :], LA[:, :, :], ACT.Tanh, scale=-1.0).then_inc(lru_a, 1)
            nc.scalar.activation(LA[:, :, :], LA[:, :, :], ACT.Exp).then_inc(lru_a, 1)
            root(LT_[:, :, :])
            evac_transposes("rqk", lambda b, n: RQK[:, b:b + n, :])
            root(LI[:, 0, :])
            for t in range(T):
                last = nc.scalar.activation(TOK[:, t, 1536:2048], TOK[:, t, 1536:2048], ACT.Silu)
            last.then_inc(r_silu, 1)
            root(var_h[:, :, :])
            evac_transposes("yr", lambda b, n: MT[:, 4 + b:4 + b + n, :])
            root(var_l)
            evac_transposes("n2", lambda b, n: XT[:, b, :], gain=lambda b: COLS[:, Q_N2 + b:Q_N2 + b + 1])
            for f in range(FF2_T + 2):
                if f < FF2_T:
                    act.wait_ge(f_up, f + 1)
                    if f >= 4:
                        act.wait_ge(f_gelu if f - 4 < DOWN_T else f_act, f - 3 if f - 4 < DOWN_T else f - 3 - DOWN_T)
                    nc.scalar.activation(CV[f % 4], bank[f % 4][:, 0:SEQ], ACT.Identity,
                                         scale=COLS[:, Q_FW + 2 * FF2_T + f:Q_FW + 2 * FF2_T + f + 1],
                                         bias=COLS[:, Q_FB + f:Q_FB + f + 1]).then_inc(f_cv0, 1)
                if 2 <= f < DOWN_T + 2:
                    act.wait_ge(f_cv, f - 1)
                    nc.scalar.activation(ACTT[:, f - 2, :], CV[(f - 2) % 4], ACT.Gelu_apprx_tanh).then_inc(f_gelu, 1)
            root(var_l)

        @block.vector
        def _(dve):
            v = nc.vector
            steps = [0]

            def link(ins):
                steps[0] += 1
                ins.then_inc(dve_step, 1)
                dve.wait_ge(dve_step, steps[0])

            def evac_transposes(name, dest, width=P, blocks=None, gain=None):
                k0, groups = TR[name]
                blocks = 2 * groups if blocks is None else blocks
                for g in range(groups):
                    k = k0 + g
                    if k % 2 == 0:
                        continue
                    dve.wait_ge(tr_done, k + 1)
                    n = min(2, blocks - 2 * g)
                    if gain is None:
                        last = v.tensor_copy(dest(2 * g, n), bank[4 + k % 4][0:width, 0:n * SEQ].rearrange(
                            "p (a b) -> p a b", b=SEQ))
                    else:
                        for b in range(n):
                            last = v.tensor_scalar(dest(2 * g + b, 1), bank[4 + k % 4][0:width, b * SEQ:(b + 1) * SEQ],
                                                   gain(2 * g + b), None, ALU.mult)
                    last.then_inc(tr_dve, 1)

            def evac_chunk(g, dest):
                dve.wait_ge(pj_done, 2 * g + 2)
                src = bank[g % 2 * 2 + 1]
                v.tensor_copy(dest, src[:, 0:dest.free_size()].rearrange("p (a b) -> p a b", b=dest.shape[2])
                              if len(dest.shape) == 3 else src[:, 0:dest.shape[1]]).then_inc(pj_free[1], 1)

            def add_chunk(g, n, alpha):
                for t in range(T):
                    dve.wait_ge(pj_done, 2 * g + 1 + t)
                    xs = X[:, t, 512 * n:512 * n + 512]
                    v.scalar_tensor_tensor(xs, xs, alpha, bank[g % 2 * 2 + t][:, :], ALU.mult, ALU.add)\
                        .then_inc(pj_free[t], 1)

            roots = [0]

            def inverse_root(var, out_):
                dve.wait_ge(std_ready, roots[0])
                link(v.reciprocal(out_, var))

            def ask_root(ins):
                roots[0] += 1
                ins.then_inc(var_ready, 1)

            norms = [0]

            def layer_norm(chunks):
                if chunks:
                    dve.wait_ge(pj_free[0], chunks)
                    dve.wait_ge(pj_free[1], chunks)
                for t in range(T):
                    for h in range(2):
                        last = v.bn_stats(bst[:, t, h, :], X[:, t, 512 * h:512 * h + 512])
                link(last)
                for t in range(T):
                    last = v.bn_aggr(mv[:, t, :], bst[:, t, :, :].rearrange("p a b -> p (a b)"))
                link(last)
                ask_root(v.tensor_scalar(var_l, mv[:, :, 1], LN_EPS, None, ALU.add))
                inverse_root(var_l, rs_l)
                for t in range(T):
                    last = v.tensor_scalar(X[:, t, :], X[:, t, :], mv[:, t, 0:1], rs_l[:, t:t + 1], ALU.subtract, ALU.mult)
                link(last)
                norms[0] += 1
                dve.wait_ge(ln_loaded, 16 * norms[0])
                for t in range(T):
                    last = v.tensor_tensor(X[:, t, :], X[:, t, :], LNR[:, 0, :], ALU.mult)
                link(last)
                for t in range(T):
                    last = v.tensor_tensor(X[:, t, :], X[:, t, :], LNR[:, 1, :], ALU.add)
                last.then_inc(x_ready, 1)
                dve.wait_ge(x_ready, norms[0])

            def token_rms(dest, scratch):
                for t in range(T):
                    last = v.tensor_tensor(scratch[:, t, :], X[:, t, :], X[:, t, :], ALU.mult)
                link(last)
                link(v.tensor_reduce(var_l, scratch, AX, ALU.add))
                ask_root(v.tensor_scalar(var_l, var_l, 1.0 / D, RMS_EPS, ALU.mult, ALU.add))
                inverse_root(var_l, rs_l)
                for t in range(T):
                    last = v.tensor_scalar(dest[:, t, :], X[:, t, :], rs_l[:, t:t + 1], None, ALU.mult)
                return last

            def rope(x4, rot, half, heads, tmp):
                for t in range(T):
                    x1, x2 = x4[:, t, :, 0:half], x4[:, t, :, half:2 * half]
                    cos = rot[:, 0, t, :].unsqueeze(1).broadcast_to([P, heads, half])
                    sin = rot[:, 1, t, :].unsqueeze(1).broadcast_to([P, heads, half])
                    n = heads * half
                    a, b, c, d = (m[:, 0:n].rearrange("p (h f) -> p h f", f=half) for m in tmp)
                    v.tensor_tensor(a, x1, cos, ALU.mult)
                    v.tensor_tensor(b, x2, sin, ALU.mult)
                    v.tensor_tensor(c, x2, cos, ALU.mult)
                    link(v.tensor_tensor(d, x1, sin, ALU.mult))
                    v.tensor_tensor(x1, a, b, ALU.subtract)
                    last = v.tensor_tensor(x2, c, d, ALU.add)
                    if t == 0:
                        link(last)
                return last

            def attention(a0, n, probs, dest, scale, bias):
                for i in range(n + 4):
                    if i < n:
                        a = a0 + i
                        dve.wait_ge(a_score, a + 1)
                        ps = bank[4 + a % 3][:, :].rearrange("p (t k) -> p t k", t=T)
                        if bias is None:
                            link(v.tensor_reduce(mx[:, a % 4, :], ps, AX, ALU.max))
                            v.tensor_scalar(nb[:, a % 4, :], mx[:, a % 4, :], -scale, None, ALU.mult).then_inc(a_nb, 1)
                        else:
                            if a >= 3:
                                dve.wait_ge(a_pt, a - 2)
                            for t in range(T):
                                last = v.scalar_tensor_tensor(probs[a % 3][:, t, :], ps[:, t, :], scale, bias(i, t),
                                                              ALU.mult, ALU.add)
                            last.then_inc(a_free, 1)
                            dve.wait_ge(a_free, i + 1)
                            v.tensor_reduce(nb[:, a % 4, :], probs[a % 3][:, :, :], AX, ALU.max, negate=True)\
                                .then_inc(a_nb, 1)
                    if 0 <= i - 1 < n:
                        a = a0 + i - 1
                        dve.wait_ge(a_exp, a + 1)
                        link(v.reciprocal(sm[:, a % 4, :], sm[:, a % 4, :]))
                        for t in range(T):
                            last = v.tensor_scalar(probs[a % 3][:, t, :], probs[a % 3][:, t, :], sm[:, a % 4, t:t + 1], None,
                                                   ALU.mult)
                        last.then_inc(a_p, 1)
                    if i >= 4 and (i - 4) % 2 == 1:
                        pair = (a0 + i - 4) // 2
                        dve.wait_ge(a_pv, 2 * pair + 2)
                        v.tensor_copy(dest(pair - a0 // 2), bank[2 + pair % 2][:, 0:SEQ]).then_inc(a_o, 1)

            def select(s, pair, g):
                io = iota_s.unsqueeze(1).broadcast_to([P, 2, SLOTS])
                for t in range(T):
                    last = v.tensor_tensor(SEL[:, t, :].rearrange("p (e s) -> p e s", e=2), io,
                                           RANK[:, t, bass.ds(pair * 2, 2)].unsqueeze(2).broadcast_to([P, 2, SLOTS]),
                                           ALU.is_equal)
                last.then_inc(s["sel_ready"], 1)

            def first_tokens(s, g):
                dve.wait_ge(s["gather_hi"], g + 1)
                v.tensor_copy(XG[:, 4:8, :], bank[7][:, :].rearrange("p (a b) -> p a b", b=P)).then_inc(s["xg_hi"], 1)

            def experts(s, pair, n, g):
                dve.wait_ge(s["sel_ready"], g + 1)
                for t in range(T):
                    last = v.tensor_tensor(SELW[:, t, :].rearrange("p (e s) -> p e s", e=2),
                                           SEL[:, t, :].rearrange("p (e s) -> p e s", e=2),
                                           WGT[:, t, bass.ds(pair * 2, 2)].unsqueeze(2).broadcast_to([P, 2, SLOTS]),
                                           ALU.mult)
                last.then_inc(s["selw_ready"], 1)
                dve.wait_ge(s["selw_ready"], n + 1)
                dve.wait_ge(s["gather_hi"], g + 1)
                select(s, pair + 1, g)
                dve.wait_ge(s["silu_done"], n + 1)
                dve.wait_ge(s["up_done"], n + 1)
                v.tensor_tensor(H, SG, bank[5][:, :], ALU.mult).then_inc(s["h_ready"], 1)
                dve.wait_ge(s["gather_hi"], g + 2)
                v.tensor_copy(XG[:, 4:8, :], bank[7][:, :].rearrange("p (a b) -> p a b", b=P)).then_inc(s["xg_hi"], 1)
                dve.wait_ge(s["y1_done"], n + 1)
                v.tensor_copy(Y[:, 512:1024], bank[7][:, :]).then_inc(s["y1_copied"], 1)

            def moe_layer(l):
                dve.wait_ge(logits_done, l + 1)
                lg = bank[4][:, 0:128].rearrange("p (t f) -> p t f", t=T)[:, :, 0:ROUTE]
                br = ROWS[:, R_BR + l * ROUTE:R_BR + (l + 1) * ROUTE].unsqueeze(1).broadcast_to([P, T, ROUTE])
                link(v.tensor_tensor(LOG[:, :, :], lg, br, ALU.add))

                def first_of(vals, top, width, at, cand, one):
                    bc = top.unsqueeze(2).broadcast_to([P, T, width])
                    io = iota_e[:, 0:width].unsqueeze(1).broadcast_to([P, T, width])
                    link(v.tensor_tensor(cand, vals, bc, ALU.is_equal))
                    link(v.tensor_tensor(cand, cand, io, ALU.mult))
                    link(v.tensor_reduce(at, cand, AX, ALU.min))
                    link(v.tensor_tensor(one, io, at.unsqueeze(2).broadcast_to([P, T, width]), ALU.is_equal))

                lgr = LOG[:, :, 0:GROUPS]
                link(v.tensor_reduce(m1, lgr, AX, ALU.max))
                v.tensor_scalar(gmn, m1, -1.0, None, ALU.mult).then_inc(r_gmax, 1)
                first_of(lgr, m1, GROUPS, i1, ru[:, :, 0:GROUPS], ru[:, :, 4:4 + GROUPS])
                link(v.tensor_scalar(ru[:, :, 4:8], ru[:, :, 4:8], -1.0, -NEG, ALU.add, ALU.mult))
                for t in range(T):
                    last = v.tensor_tensor(ELOG[:, t, :].rearrange("p (g e) -> p g e", g=GROUPS),
                                           LOG[:, t, GROUPS:ROUTE].rearrange("p (g e) -> p g e", g=GROUPS),
                                           ru[:, t, 4:8].unsqueeze(2).broadcast_to([P, GROUPS, PER_GROUP]), ALU.add)
                link(last)
                link(v.tensor_reduce(m1, ELOG[:, :, :], AX, ALU.max))
                first_of(ELOG[:, :, :], m1, EXPERTS, i1, RANK[:, :, 0:EXPERTS], ONE1[:, :, :])
                link(v.scalar_tensor_tensor(ELOG[:, :, :], ONE1[:, :, :], 3 * NEG, ELOG[:, :, :], ALU.mult, ALU.add))
                link(v.tensor_reduce(m2, ELOG[:, :, :], AX, ALU.max))
                v.tensor_tensor(p2, m2, m1, ALU.subtract).then_inc(r_d, 1)
                first_of(ELOG[:, :, :], m2, EXPERTS, i2, RANK[:, :, 0:EXPERTS], ONE2[:, :, :])
                v.tensor_tensor(ELOG[:, :, :], ONE1[:, :, :], ONE2[:, :, :], ALU.add).then_inc(r_one, 1)
                dve.wait_ge(r_gexp, l + 1)
                link(v.reciprocal(gw, gsum))
                dve.wait_ge(r_p2, l + 1)
                link(v.tensor_scalar(g2, p2, 1.0, None, ALU.add))
                link(v.reciprocal(g1, g2))
                link(v.tensor_tensor(g1, g1, gw, ALU.mult))
                link(v.tensor_tensor(g2, g1, p2, ALU.mult))
                link(v.tensor_tensor(ONE1[:, :, :], ONE1[:, :, :], g1.unsqueeze(2).broadcast_to([P, T, EXPERTS]), ALU.mult))
                link(v.tensor_tensor(ONE2[:, :, :], ONE2[:, :, :], g2.unsqueeze(2).broadcast_to([P, T, EXPERTS]), ALU.mult))
                link(v.tensor_tensor(WGT[:, :, 0:EXPERTS], ONE1[:, :, :], ONE2[:, :, :], ALU.add))
                dve.wait_ge(rank_done, l + 1)
                dve.wait_ge(r_one, l + 1)
                rk = bank[4][:, 0:128].rearrange("p (t f) -> p t f", t=T)[:, :, 0:EXPERTS]
                link(v.scalar_tensor_tensor(RANK[:, :, 0:EXPERTS], rk, 1.0, ELOG[:, :, :], ALU.add, ALU.mult))
                link(v.tensor_scalar(RANK[:, :, 0:EXPERTS], RANK[:, :, 0:EXPERTS], -1.0, None, ALU.add))
                v.tensor_reduce(rtop, RANK[:, :, :].rearrange("p t e -> p (t e)"), AX, ALU.max).then_inc(r_top, 1)
                if l:
                    dve.wait_ge(moe["gather_hi"], (PAIRS + 1) * l)
                select(moe, 0, 0)
                dve.wait_ge(top_done, l + 1)
                link(v.tensor_reduce(rtop2[0:1, :], bank[5][0:1, 0:P], AX, ALU.max))
                v.tensor_scalar(FLAG[0:1, l:l + 1], rtop2[0:1, :], SLOTS - 0.5, None, ALU.is_ge).then_inc(flag_ready, 1)
                first_tokens(moe, (PAIRS + 1) * l)
                with dve.Fori(0, PAIRS) as p:
                    experts(moe, p, p + PAIRS * l, p + (PAIRS + 1) * l)
                dve.wait_ge(flag_ready, l + 1)
                more = dve.value_load(FLAG[0:1, l:l + 1], min_val=0, max_val=1)
                with dve.If(more > 0):
                    s = over[l]
                    dve.wait_ge(moe["gather_hi"], (PAIRS + 1) * (l + 1))
                    with dve.Fori(0, ROUNDS_MORE) as r:
                        v.tensor_scalar(RANK[:, :, 0:EXPERTS], RANK[:, :, 0:EXPERTS], float(-SLOTS), None, ALU.add)\
                            .then_inc(over_shift[l], 1)
                        dve.wait_ge(over_shift[l], r + 1)
                        select(s, 0, 0)
                        first_tokens(s, r * (PAIRS + 1))
                        with dve.Fori(0, PAIRS) as p:
                            experts(s, p, r * PAIRS + p, r * (PAIRS + 1) + p)
                dve.wait_ge(acc_done, l + 1)
                for t in range(T):
                    for h in range(2):
                        xs = X[:, t, 512 * h:512 * h + 512]
                        last = v.scalar_tensor_tensor(xs, xs, ALPHA, bank[2 * t + h][:, :], ALU.mult, ALU.add)
                link(last)

            v.memset(RANK[:, :, :], -1.0)
            link(v.memset(WGT[:, :, :], 0.0))
            dve.wait_ge(const_loaded, 64)
            lam = ROWS[:, R_LAM:R_LAM + 4 * A_DIM].rearrange("p (a b f) -> p a b f", a=2, b=2)
            lt = ROT[3][:, 0:2 * A_DIM].rearrange("p (a f) -> p a f", a=2)
            link(v.tensor_tensor(lt, lam[:, :, 0, :], lam[:, :, 1, :], ALU.mult))
            v.tensor_reduce(lamv, lt, AX, ALU.add).then_inc(lam_ready, 1)
            evac_transposes("x", lambda b, n: XT[:, b:b + n, :])
            for n in range(4):
                evac_chunk(G_EIN + n, E[:, 1, 512 * n:min(512 * n + 512, EVEN_IN)])
            dve.wait_ge(lam_exp, 1)
            link(v.scalar_tensor_tensor(nlam, lamv[:, 1:2], -LAMBDA_INIT, lamv[:, 0:1], ALU.add, ALU.subtract))
            dve.wait_ge(pj_free[0], 4)
            dve.wait_ge(pj_free[1], 4)
            sq = SQA[:, :, 0:Q_RANK + KV_RANK]
            link(v.tensor_tensor(sq, E[:, :, CQ0:KR0], E[:, :, CQ0:KR0], ALU.mult))
            v.tensor_reduce(var_b[:, :, 0], sq[:, :, 0:Q_RANK], AX, ALU.add)
            link(v.tensor_reduce(var_b[:, :, 1], sq[:, :, Q_RANK:Q_RANK + KV_RANK], AX, ALU.add))
            v.tensor_scalar(var_b[:, :, 0], var_b[:, :, 0], 1.0 / Q_RANK, RMS_EPS, ALU.mult, ALU.add)
            ask_root(v.tensor_scalar(var_b[:, :, 1], var_b[:, :, 1], 1.0 / KV_RANK, RMS_EPS, ALU.mult, ALU.add))
            rope(E[:, :, 0:1024].rearrange("p t (h f) -> p t h f", f=A_DIM), rot_a, A_HALF, 16, ROT).then_inc(rope_ready, 1)
            inverse_root(var_b[:, :, :], rs_b[:, :, :])
            for t in range(T):
                v.tensor_scalar(E[:, t, CQ0:CKV0], E[:, t, CQ0:CKV0], rs_b[:, t, 0:1], None, ALU.mult)
                last = v.tensor_scalar(E[:, t, CKV0:KR0], E[:, t, CKV0:KR0], rs_b[:, t, 1:2], None, ALU.mult)
            last.then_inc(rank_ready, 1)
            evac_transposes("qk", lambda b, n: QKT[:, b:b + n, :])
            evac_transposes("c", lambda b, n: CT[:, b, :], blocks=3, gain=lambda b: COLS[:, Q_QN + b:Q_QN + b + 1])
            for n in range(2):
                evac_chunk(G_UQ + n, QB[:, 1, 384 * n:384 * n + 384])
            for n in range(2):
                evac_chunk(G_UKV + n, KV[:, 1, 512 * n:512 * n + 512])
            for t in range(T):
                dve.wait_ge(pj_free[t], G_EO)
            q4 = QB[:, :, :].rearrange("p t (h f) -> p t h f", f=B_QK)
            link(rope(q4[:, :, :, B_NOPE:B_QK], rot_b, B_HALF, B_HEADS, ROT))
            link(rope(E[:, :, KR0:EVEN_IN].unsqueeze(2), rot_b, B_HALF, 1, ROT))
            kv4 = KV[:, :, :].rearrange("p t (h f) -> p t h f", f=B_NOPE + B_V)
            kc4 = KC.rearrange("p t (h f) -> p t h f", f=B_QK)
            for t in range(T):
                v.tensor_copy(kc4[:, t, :, 0:B_NOPE], kv4[:, t, :, 0:B_NOPE])
                last = v.tensor_copy(kc4[:, t, :, B_NOPE:B_QK],
                                     E[:, t, KR0:EVEN_IN].unsqueeze(1).broadcast_to([P, B_HEADS, B_ROPE]))
            last.then_inc(mla_ready, 1)
            for i in range(A_HEADS + 2):
                if i < A_HEADS:
                    for m in range(2):
                        dve.wait_ge(d_score, 2 * i + m + 1)
                        ps = bank[4 + 2 * (i % 2) + m][:, :].rearrange("p (t k) -> p t k", t=T)
                        link(v.tensor_reduce(dmx[:, i % 2, m, :], ps, AX, ALU.max))
                        v.tensor_scalar(dnb[:, i % 2, m, :], dmx[:, i % 2, m, :], -(A_DIM ** -0.5), None, ALU.mult)\
                            .then_inc(d_nb, 1)
                if 0 <= i - 1 < A_HEADS:
                    h = i - 1
                    dve.wait_ge(d_exp, 2 * h + 2)
                    s4 = dsm[:, h % 2, :, :]
                    link(v.reciprocal(s4, s4))
                    link(v.tensor_scalar(s4[:, 1, :], s4[:, 1, :], nlam, None, ALU.mult))
                    e0, e1 = PB[2 * (h % 2)], PB[2 * (h % 2) + 1]
                    for t in range(T):
                        last = v.tensor_scalar(e0[:, t, :], e0[:, t, :], s4[:, 0, t:t + 1], None, ALU.mult)
                    link(last)
                    for t in range(T):
                        last = v.scalar_tensor_tensor(e0[:, t, :], e1[:, t, :], s4[:, 1, t:t + 1], e0[:, t, :], ALU.mult, ALU.add)
                    last.then_inc(d_w, 1)
                if i >= 2:
                    h = i - 2
                    dve.wait_ge(d_pv, h + 1)
                    v.tensor_copy(AO[:, :, h * P:(h + 1) * P], bank[2 + h % 2][:, 0:SEQ].rearrange("p (t e) -> p t e", t=T))\
                        .then_inc(d_o, 1)
            dve.wait_ge(d_o, A_HEADS)
            link(v.tensor_tensor(SQA, AO, AO, ALU.mult))
            evac_transposes("qb", lambda b, n: QBT[0:B_QK, b:b + n, :], B_QK)
            evac_transposes("kb", lambda b, n: KBT[0:B_QK, b:b + n, :], B_QK)
            link(v.tensor_reduce(var_a[:, :, :], SQA.rearrange("p t (h e) -> p t h e", h=A_HEADS), AX, ALU.add))
            ask_root(v.tensor_scalar(var_a[:, :, :], var_a[:, :, :], 1.0 / (2 * A_DIM), RMS_EPS, ALU.mult, ALU.add))
            inverse_root(var_a[:, :, :], rs_a[:, :, :])
            link(v.tensor_scalar(rs_a[:, :, :], rs_a[:, :, :], 1.0 - LAMBDA_INIT, None, ALU.mult))
            sub = ROWS[:, R_SUB:R_SUB + P].unsqueeze(1).broadcast_to([P, A_HEADS, P])
            for t in range(T):
                ao = AO[:, t, :].rearrange("p (h e) -> p h e", h=A_HEADS)
                link(v.tensor_tensor(ao, ao, rs_a[:, t, :].unsqueeze(2).broadcast_to([P, A_HEADS, P]), ALU.mult))
                last = v.tensor_tensor(ao, ao, sub, ALU.mult)
            last.then_inc(ao_ready, 1)
            attention(N_MLA0, B_HEADS, PB, lambda pair: MT[:, 4 + pair, :], B_QK ** -0.5, None)
            evac_transposes("ao", lambda b, n: MT[:, b:b + n, :])
            for n in range(2):
                add_chunk(G_EO + n, n, ALPHA)
            layer_norm(G_QKV)
            evac_transposes("ln0", lambda b, n: XT[:, b:b + n, :])
            moe_layer(0)
            layer_norm(None)
            evac_transposes("ln1", lambda b, n: XT[:, b:b + n, :])
            for n in range(4):
                evac_chunk(G_QKV + n, (OQ if n < 2 else OK)[:, 4 * (n % 2) + 2:4 * (n % 2) + 4, :])
            for n in range(2):
                evac_chunk(G_QKV + 4 + n, OV[:, 1, 512 * n:512 * n + 512])
            dve.wait_ge(bias_loaded, 16)
            attention(N_NA0, C_HEADS, PN, lambda pair: MT[:, pair, :], C_DIM ** -0.5,
                      lambda h, t: G[:, h, (2 - 2 * t) * GRID_W:(2 - 2 * t) * GRID_W + SEQ])
            for n in range(2):
                add_chunk(G_OO + n, n, ALPHA)
            layer_norm(G_IN2)
            evac_transposes("ln2", lambda b, n: XT[:, b:b + n, :])
            moe_layer(1)
            layer_norm(None)
            token_rms(XN, XN).then_inc(xn_ready, 1)
            ll = COLS[:, Q_LAM:Q_LAM + LRU_T]
            link(v.tensor_scalar(spl[0], ll, -1.0, 0.0, ALU.mult, ALU.max))
            link(v.tensor_scalar(spl[1], ll, -1.0, None, ALU.mult))
            v.tensor_tensor(spl[1], spl[1], ll, ALU.min).then_inc(sp_in, 1)
            v.tensor_scalar(spl[3], COLS[:, Q_BA:Q_BA + LRU_T], 0.5, None, ALU.mult)
            v.tensor_scalar(spl[4], COLS[:, Q_BX:Q_BX + LRU_T], 0.5, None, ALU.mult).then_inc(sp_in, 1)
            evac_transposes("n1", lambda b, n: XT[:, b, :], gain=lambda b: COLS[:, Q_N1 + b:Q_N1 + b + 1])
            evac_chunk(G_IN2, XL[:, 2:4, :])
            dve.wait_ge(pj_free[0], G_IN2 + 1)
            dve.wait_ge(pj_free[1], G_IN2 + 1)

            def tap(j, c):
                return COLS[:, Q_CW + j * LRU_T + c:Q_CW + j * LRU_T + c + 1]

            for c in range(LRU_T):
                last = v.tensor_scalar(LX[:, c, :], XL[:, c, :], tap(3, c), COLS[:, Q_CB + c:Q_CB + c + 1], ALU.mult, ALU.add)
            link(last)
            for j in range(1, LRU_CONV):
                for c in range(LRU_T):
                    last = v.scalar_tensor_tensor(LX[:, c, j:SEQ], XL[:, c, 0:SEQ - j], tap(3 - j, c), LX[:, c, j:SEQ],
                                                  ALU.mult, ALU.add)
                    if j == LRU_CONV - 1:
                        last.then_inc(lru_cvd, 1)
                if j < LRU_CONV - 1:
                    link(last)
            dve.wait_ge(pj_free[1], G_IN2 + 2)
            for n in range(4):
                evac_chunk(G_IN2 + 2 + n, TOK[:, 1, 512 * n:512 * n + 512])
            dve.wait_ge(sp_exp, 1)
            link(v.tensor_scalar(spl[2], spl[1], 2.0, None, ALU.add))
            link(v.reciprocal(spl[2], spl[2]))
            link(v.tensor_tensor(spl[1], spl[1], spl[2], ALU.mult))
            link(v.tensor_tensor(spl[2], spl[1], spl[1], ALU.mult))
            ser = spl_series
            link(v.tensor_scalar(ser, spl[2], 1.0 / 19, 1.0 / 17, ALU.mult, ALU.add))
            for k in (15, 13, 11, 9, 7, 5, 3, 1):
                link(v.tensor_tensor(ser, ser, spl[2], ALU.mult))
                link(v.tensor_scalar(ser, ser, 1.0 / k, None, ALU.add))
            link(v.tensor_tensor(ser, ser, spl[1], ALU.mult))
            link(v.scalar_tensor_tensor(spl[0], ser, 2.0, spl[0], ALU.mult, ALU.add))
            link(v.tensor_scalar(spl[0], spl[0], -4.0, None, ALU.mult))
            dve.wait_ge(lru_g, LRU_T)
            for c in range(LRU_T):
                last = v.tensor_scalar(LA[:, c, :], LA[:, c, :], 1.0, spl[0][:, c:c + 1], ALU.add, ALU.mult)
            last.then_inc(lru_t, 1)
            link(v.tensor_scalar(LI[:, :, :], LI[:, :, :], 0.5, 0.5, ALU.mult, ALU.add))
            link(v.tensor_tensor(LI[:, :, :], LI[:, :, :], LX[:, :, :], ALU.mult))
            dve.wait_ge(lru_a, 1)
            link(v.tensor_scalar(XL[:, :, :], LT_[:, :, :], 1.0, None, ALU.add))
            link(v.reciprocal(XL[:, :, :], XL[:, :, :]))
            ask_root(v.scalar_tensor_tensor(LT_[:, :, :], LT_[:, :, :], 2.0, XL[:, :, :], ALU.mult, ALU.mult))
            dve.wait_ge(pj_free[0], G_OUT2)
            dve.wait_ge(pj_free[1], G_OUT2)
            dve.wait_ge(table2_loaded, 32)
            rope(TOK[:, :, 0:1024].rearrange("p t (h f) -> p t h f", f=RET_DIM), rot_c, RET_DIM // 2, 8, ROT2)\
                .then_inc(r_rope, 1)
            dve.wait_ge(std_ready, roots[0])
            link(v.tensor_tensor(LI[:, :, :], LI[:, :, :], LT_[:, :, :], ALU.mult))
            dve.wait_ge(lru_a, 2)
            for c in range(LRU_T):
                last = v.tensor_tensor_scan(LX[:, c, :], LA[:, c, :], LI[:, c, :], 0.0, ALU.mult, ALU.add)
            link(last)
            link(v.tensor_tensor(LX[:, :, :], LX[:, :, :], GL[:, :, :], ALU.mult))
            v.tensor_tensor(LT_[:, :, :], LX[:, :, :], LX[:, :, :], ALU.mult).then_inc(lru_sq, 1)
            evac_transposes("rqk", lambda b, n: RQK[:, b:b + n, :])
            dve.wait_ge(lru_sqr, 1)
            ask_root(v.tensor_scalar(LI[:, 0, :], bank[0][:, 0:SEQ], 1.0 / LRU, RMS_EPS, ALU.mult, ALU.add))
            inverse_root(LI[:, 0, :], LI[:, 1, :])
            for c in range(LRU_T):
                last = v.scalar_tensor_tensor(MT[:, c, :], LX[:, c, :], COLS[:, Q_LN + c:Q_LN + c + 1], LI[:, 1, :],
                                              ALU.mult, ALU.mult)
            last.then_inc(lru_y, 1)
            for h in range(RET_HEADS):
                dve.wait_ge(r_sc, h + 1)
                v.tensor_tensor(RS[:, h, :], bank[4 + h][:, 0:DEC_W], KT2[:, L_DEC + h * DEC_W:L_DEC + (h + 1) * DEC_W],
                                ALU.mult).then_inc(r_scd, 1)
            for h in range(RET_HEADS):
                dve.wait_ge(r_o, h + 1)
                v.tensor_copy(YR[:, :, h * P:(h + 1) * P], bank[2 + h % 2][:, 0:SEQ].rearrange("p (t e) -> p t e", t=T))\
                    .then_inc(r_oc, 1)
            dve.wait_ge(r_oc, RET_HEADS)
            for t in range(T):
                for h in range(RET_HEADS):
                    last = v.bn_stats(hst[:, t, h, :], YR[:, t, h * P:(h + 1) * P])
            link(last)
            for t in range(T):
                for h in range(RET_HEADS):
                    last = v.bn_aggr(hmv[:, t, h, :], hst[:, t, h, :])
            link(last)
            ask_root(v.tensor_scalar(var_h[:, :, :], hmv[:, :, :, 1], RMS_EPS, None, ALU.add))
            inverse_root(var_h[:, :, :], rs_h[:, :, :])
            for t in range(T):
                for h in range(RET_HEADS):
                    last = v.tensor_scalar(YR[:, t, h * P:(h + 1) * P], YR[:, t, h * P:(h + 1) * P], hmv[:, t, h, 0:1],
                                           rs_h[:, t, h:h + 1], ALU.subtract, ALU.mult)
            link(last)
            dve.wait_ge(ln_loaded, 16 * 5)
            for t in range(T):
                last = v.tensor_tensor(YR[:, t, :], YR[:, t, :], LNR[:, 0, 0:RET_HEADS * RET_DIM], ALU.mult)
            link(last)
            dve.wait_ge(r_silu, 1)
            for t in range(T):
                last = v.tensor_tensor(YR[:, t, :], YR[:, t, :], TOK[:, t, 1536:2048], ALU.mult)
            last.then_inc(r_y, 1)
            evac_transposes("yr", lambda b, n: MT[:, 4 + b:4 + b + n, :])
            for n in range(2):
                add_chunk(G_OUT2 + n, n, 1.0)
            dve.wait_ge(pj_free[0], G_OUT2 + 2)
            dve.wait_ge(pj_free[1], G_OUT2 + 2)
            token_rms(XN, XN).then_inc(xn_ready, 1)
            evac_transposes("n2", lambda b, n: XT[:, b, :], gain=lambda b: COLS[:, Q_N2 + b:Q_N2 + b + 1])
            for f in range(FF2_T):
                dve.wait_ge(f_cv0, f + 1)
                for j in (1, 2):
                    wj = COLS[:, Q_FW + (2 - j) * FF2_T + f:Q_FW + (2 - j) * FF2_T + f + 1]
                    ins = v.scalar_tensor_tensor(CV[f % 4][:, j:SEQ], bank[f % 4][:, 0:SEQ - j], wj, CV[f % 4][:, j:SEQ],
                                                 ALU.mult, ALU.add)
                    if j == 1:
                        link(ins)
                    else:
                        ins.then_inc(f_cv, 1)
                if f >= DOWN_T:
                    g = f - DOWN_T
                    dve.wait_ge(f_gelu, g + 1)
                    dve.wait_ge(f_cv, f + 1)
                    v.tensor_tensor(ACTT[:, g, :], ACTT[:, g, :], CV[f % 4], ALU.mult).then_inc(f_act, 1)
            dve.wait_ge(f_down, 6)
            for t in range(T):
                for h in range(2):
                    xs = X[:, t, 512 * h:512 * h + 512]
                    last = v.tensor_tensor(xs, xs, bank[4 + 2 * t + h][:, :], ALU.add)
            link(last)
            link(token_rms(X, XN))
            dve.wait_ge(ln_loaded, 16 * 6)
            for t in range(T):
                last = v.tensor_tensor(X[:, t, :], X[:, t, :], LNR[:, 0, :], ALU.mult)
            last.then_inc(out_ready, 1)


def lay_out(i):
    table, table2 = shape_constants()

    def feature_columns(a):
        a = a.reshape(-1, a.shape[-1] // P, P)
        return a.transpose(2, 0, 1).reshape(P, -1)

    cols = np.concatenate([feature_columns(a) for a in (
        i["norm1_gain_2"], i["lru_conv_w_2"][0], i["lru_conv_b_2"], i["lru_gate_a_b_2"], i["lru_gate_x_b_2"],
        i["lru_lambda_2"], i["lru_norm_gain_2"], i["norm2_gain_2"], i["ffn_conv_w_2"][0], i["ffn_conv_b_2"],
        i["even_q_norm_g"], i["even_kv_norm_g"])], 1)
    rows = np.concatenate([i["even_subln_g"][0], i["even_lam_q1"][0], i["even_lam_k1"][0], i["even_lam_q2"][0],
                           i["even_lam_k2"][0]] +
                          [a for l in range(DEPTH) for a in (i["b_router_group"][l], i["b_router_expert"][l])])[None]
    ln_rows = np.zeros((6, 2 * D), np.float32)
    for l in range(DEPTH):
        for n, name in enumerate(("ln1", "ln2")):
            ln_rows[2 * l + n, :D] = i[f"{name}_g"][l]
            ln_rows[2 * l + n, D:] = i[f"{name}_b"][l]
    ln_rows[4, :RET_HEADS * RET_DIM] = i["ret_norm_gain_2"][0]
    ln_rows[5, :D] = i["final_norm_gain_2"]
    route = np.concatenate([i["w_router_group"], i["w_router_expert"]], 2)
    route = route.reshape(DEPTH, C, P, ROUTE).transpose(2, 0, 1, 3)
    rr, cc, m, j = np.meshgrid(np.arange(2), np.arange(GRID_W), np.arange(BIAS_ROWS), np.arange(GRID_W), indexing="ij")
    start = np.clip(cc - NA_COLS // 2, 0, GRID_W - NA_COLS)
    inside = (j >= start) & (j < start + NA_COLS)
    col = np.clip(j - cc + NA_COLS - 1, 0, 2 * NA_COLS - 2)
    bias = i["odd_rel_bias"][0][:, m + 5 - rr, col]
    bias = np.where(inside[None], bias, np.float32(NEG))
    bias = bias.transpose(1, 2, 0, 3, 4).reshape(P, C_HEADS, BIAS_ROWS * GRID_W)
    gates = np.zeros((P, 2, LRU_T, P), np.float32)
    for n, name in enumerate(("lru_gate_a_w_2", "lru_gate_x_w_2")):
        for h in range(8):
            o = h % 2 * 64
            gates[o:o + 64, n, h // 2, o:o + 64] = i[name][0, h]
    return {
        "x": i["x"][0], "w_in": i["even_w_in"][0], "w_uq": i["even_w_uq"][0], "w_ukv": i["even_w_ukv"][0],
        "w_o": i["even_w_o"][0], "w_qkv": i["odd_w_qkv"][0], "na_bias": bias, "w_o2": i["odd_w_o"][0],
        "ln_rows": ln_rows, "rows": rows, "cols": cols, "w_route": route, "w_gate": i["w_gate"], "w_up": i["w_up"],
        "w_down": i["w_down"], "w_in2": i["w_in_2"][0], "gates": gates.reshape(P, 2, LRU_T * P),
        "w_out2": i["w_out_2"][0], "ffn_up": i["ffn_up_w_2"][0], "ffn_down": i["ffn_down_w_2"][0],
        "table": table, "table2": table2,
    }


def kernel(**inputs):
    import concourse.bacc as bacc
    from concourse.bass_utils import run_bass_kernel_spmd

    laid = lay_out({k: np.asarray(a) for k, a in inputs.items()})
    nc = bacc.Bacc("TRN2", target_bir_lowering=False, num_devices=1)
    arrays, args = {}, []
    for name, a in laid.items():
        a = np.ascontiguousarray(a)
        arrays[f"in_{name}"] = a
        args.append(nc.dram_tensor(f"in_{name}", a.shape, mybir.dt.from_np(a.dtype), kind="ExternalInput").ap())
    out = nc.dram_tensor("out", (SEQ, D), F32, kind="ExternalOutput").ap()
    bass_two_blocks(nc, *args, out)
    r = run_bass_kernel_spmd(nc, [arrays], core_ids=[0])
    return np.asarray(r.results[0]["out"]).reshape(1, SEQ, D)
```

```python
import math
from contextlib import ExitStack

import numpy as np
import concourse.bass as bass
from concourse import mybir

F32 = mybir.dt.float32
I32 = mybir.dt.int32
ALU = mybir.AluOpType
ACT = mybir.ActivationFunctionType
AX = mybir.AxisListType.X

P = 128
SEQ, D = 256, 1024
T = SEQ // P
C = D // P
DEPTH = 2
ALPHA = (2 * DEPTH) ** 0.25
LN_EPS, RMS_EPS = 1e-5, 1e-6
NEG = -1e30

A_HEADS, A_DIM = 4, 64
A_HALF = A_DIM // 4 // 2
LAMBDA_INIT = 0.8 - 0.6 * math.exp(-0.3 * 0)
B_HEADS, B_NOPE, B_ROPE, B_V = 8, 64, 32, 64
B_QK = B_NOPE + B_ROPE
B_HALF = B_ROPE // 2
Q_RANK, KV_RANK = 256, 128
VA0 = 1024
CQ0, CKV0, KR0, EVEN_IN = 1536, 1792, 1920, 1952
C_HEADS, C_DIM = 16, 64
GRID_W, NA_COLS = 64, 16
GRID_R = SEQ // GRID_W
BIAS_ROWS = 6
GROUPS, PER_GROUP, EXPERTS, FE = 4, 8, 32, 512
SLOTS = 64
PAIRS = EXPERTS // 2
ROUNDS_MORE = SEQ // SLOTS - 1
ROUTE = GROUPS + EXPERTS
LRU, LRU_T, LRU_CONV = 512, 4, 4
RET_HEADS, RET_DIM = 4, 128
FF2, FF2_T, FF_CONV = 6144, 48, 3
DOWN_T = FF2_T // 2

RING = 6
EARLY = 3
SLOT = 4096


def shape_constants():
    f = np.float32

    def rotation(theta, rot):
        inv = f(theta) ** (-np.arange(0, rot, 2, dtype=f) / f(rot))
        ang = np.arange(SEQ, dtype=f)[:, None] * inv[None].astype(f)
        both = np.stack([np.cos(ang), np.sin(ang)]).astype(f)
        return both.reshape(2, T, P, -1).transpose(2, 0, 1, 3).reshape(P, -1)

    first = [
        np.eye(P, dtype=f),
        np.triu(np.ones((P, P), f), 1),
        np.ones((P, P), f),
        np.zeros((P, P), f),
        np.tile(np.arange(SLOTS, dtype=f), (P, 1)),
        np.tile(np.arange(EXPERTS, dtype=f) - 64, (P, 1)),
        rotation(500000.0, 2 * A_HALF),
        rotation(500000.0, B_ROPE),
    ]
    log_g = np.log1p(-np.exp2(-5.0 - np.arange(RET_HEADS, dtype=np.float64)))
    diff = np.arange(SEQ)[None] - np.arange(P)[:, None]
    decay = np.where(diff >= 0, np.exp(np.maximum(diff, 0) * log_g[:, None, None]), 0.0) * RET_DIM ** -0.5
    decay = np.concatenate([decay, decay[:, :, :P]], axis=2)
    later = [rotation(10000.0, RET_DIM), decay.transpose(1, 0, 2).reshape(P, -1).astype(f)]
    return np.concatenate(first, 1).astype(f), np.concatenate(later, 1).astype(f)


K_ID, K_LT, K_ONE, K_ZERO, K_IO = 0, 128, 256, 384, 512
K_IE = K_IO + SLOTS
K_RA = K_IE + EXPERTS
K_RB = K_RA + 2 * T * A_HALF
K_W = K_RB + 2 * T * B_HALF
L_ROT, L_DEC = 0, 2 * T * (RET_DIM // 2)
DEC_W = SEQ + P
L_W = L_DEC + RET_HEADS * DEC_W
R_SUB, R_LAM, R_BR = 0, 128, 128 + 256
R_W = R_BR + DEPTH * ROUTE
Q_N1, Q_CW, Q_CB, Q_BA, Q_BX, Q_LAM, Q_LN, Q_N2 = 0, 8, 24, 28, 32, 36, 40, 44
Q_FW, Q_FB = 52, 52 + FF_CONV * FF2_T
Q_QN = Q_FB + FF2_T
Q_KVN = Q_QN + 2
Q_W = Q_KVN + 1


def bass_two_blocks(nc, x, w_in, w_uq, w_ukv, w_o, w_qkv, na_bias, w_o2, ln_rows, rows, cols, w_route,
                    w_gate, w_up, w_down, w_in2, gates, w_out2, ffn_up, ffn_down, table, table2, out):
    with ExitStack() as ctx:
        def sb(name, shape, dt=F32):
            return ctx.enter_context(nc.sbuf_tensor(name, shape, dt))

        def sem(name):
            return ctx.enter_context(nc.semaphore(name))

        ring = sb("ring", [P, RING, SLOT])
        X = sb("X", [P, T, D])
        XT = sb("XT", [P, C, SEQ])
        MT = sb("MT", [P, C, SEQ])
        LNR = sb("LNR", [P, 2, D])
        KT = sb("KT", [P, K_W])
        ROWS = sb("ROWS", [P, R_W])
        COLS = sb("COLS", [P, Q_W])
        WR = sb("WR", [P, DEPTH, C, ROUTE])
        ST = sb("ST", [P, 512])
        FLAG = sb("FLAG", [1, DEPTH], I32)
        ARENA_W = 16896
        arena = sb("arena", [P, ARENA_W])
        bank = [ctx.enter_context(nc.psum_tensor(f"bank{i}", [P, 512], F32)) for i in range(8)]

        def cut(off, *shape):
            n = int(np.prod(shape))
            assert off + n <= ARENA_W, (off, shape)
            v = arena[:, off:off + n]
            if len(shape) == 2:
                v = v.rearrange("p (a b) -> p a b", b=shape[1])
            if len(shape) == 3:
                v = v.rearrange("p (a b c) -> p a b c", b=shape[1], c=shape[2])
            return v

        stat_at = [0]

        def stat(*shape):
            n = int(np.prod(shape))
            v = ST[:, stat_at[0]:stat_at[0] + n]
            stat_at[0] += n
            assert stat_at[0] <= 512
            if len(shape) == 2:
                v = v.rearrange("p (a b) -> p a b", b=shape[1])
            if len(shape) == 3:
                v = v.rearrange("p (a b c) -> p a b c", b=shape[1], c=shape[2])
            return v

        ident, earlier = KT[:, K_ID:K_ID + P], KT[:, K_LT:K_LT + P]
        ones, zeros = KT[:, K_ONE:K_ONE + P], KT[:, K_ZERO:K_ZERO + P]
        iota_s, iota_e = KT[:, K_IO:K_IO + SLOTS], KT[:, K_IE:K_IE + EXPERTS]
        rot_a = KT[:, K_RA:K_RB].rearrange("p (s t f) -> p s t f", s=2, t=T)
        rot_b = KT[:, K_RB:K_W].rearrange("p (s t f) -> p s t f", s=2, t=T)

        E = cut(0, T, EVEN_IN)
        QKT = cut(3904, C, SEQ)
        QBT, KBT = QKT, XT
        PB = [cut(5952 + 512 * i, T, SEQ) for i in range(4)]
        ROT = [cut(5952 + 512 * i, 512) for i in range(4)]
        PT = [cut(8000 + 512 * i, T, SEQ) for i in range(2)]
        QB = cut(9024, T, B_HEADS * B_QK)
        KV = cut(10560, T, B_HEADS * (B_NOPE + B_V))
        KC = E[:, :, 0:B_HEADS * B_QK]
        CT = cut(12608, 3, SEQ)
        AO = cut(13376, T, A_HEADS * 2 * A_DIM)
        SQA = cut(14400, T, A_HEADS * 2 * A_DIM)
        ROTB = [cut(15424 + B_HEADS * B_HALF * i, B_HEADS * B_HALF) for i in range(4)]
        SEL = cut(0, T, 2 * SLOTS)
        SELW = cut(256, T, 2 * SLOTS)
        SWT = cut(512, T, P)
        XG = cut(768, C, 2 * SLOTS)
        SG = cut(1792, FE)
        H = cut(2304, FE)
        HT = cut(2816, FE // P, 2 * SLOTS)
        Y = cut(3328, D)
        FIRST = [cut(4352 + SLOT * i, SLOT) for i in range(EARLY)]
        G = cut(4352, C_HEADS, BIAS_ROWS * GRID_W)
        OQ, OK, OV = cut(10496, C, SEQ), cut(12544, C, SEQ), cut(14592, T, D)
        PN = [cut(512 * i, T, SEQ) for i in range(3)]
        PTN = [cut(1536 + 512 * i, T, SEQ) for i in range(2)]
        XL, GL, LX, LA = (cut(1024 * i, LRU_T, SEQ) for i in range(4))
        KT2 = cut(4352, L_W)
        rot_c = KT2[:, L_ROT:L_DEC].rearrange("p (s t f) -> p s t f", s=2, t=T)
        GATE = cut(6144, 2, LRU_T * P)
        LI, LT_ = cut(7168, LRU_T, SEQ), cut(8192, LRU_T, SEQ)
        TOK = cut(9216, T, 4 * RET_HEADS * RET_DIM)
        RQK = cut(13312, C, SEQ)
        ROT2 = [cut(13312 + 512 * i, 512) for i in range(4)]
        RS = cut(15360, RET_HEADS, DEC_W)
        YR = TOK[:, :, 0:RET_HEADS * RET_DIM]
        ACTT = cut(0, DOWN_T, SEQ)
        CV = [cut(9216 + 256 * i, SEQ) for i in range(4)]
        XN = MT[:, :, :].rearrange("p c s -> p (c s)").rearrange("p (t d) -> p t d", t=T)
        XN2 = cut(13312, T, D)

        mx, nb, sm = stat(4, T), stat(4, T), stat(4, T)
        dmx, dnb, dsm = stat(2, 2, T), stat(2, 2, T), stat(2, 2, T)
        lamv, nlam = stat(2), stat(1)
        var_b, rs_b = stat(T, 2), stat(T, 2)
        var_a, rs_a = stat(T, A_HEADS), stat(T, A_HEADS)
        bst, mv = stat(T, 2, 6), stat(T, 2)
        var_l, rs_l = stat(T), stat(T)
        rg, ru = stat(T, 8), stat(T, 8)
        gmn, gsum, gw = stat(T), stat(T), stat(T)
        m1, m2, i1, i2, p2, g1, g2 = (stat(T) for _ in range(7))
        rtop, rtop2 = stat(1), stat(1)
        hst, hmv = stat(T, RET_HEADS, 6), stat(T, RET_HEADS, 2)
        var_h, rs_h = stat(T, RET_HEADS), stat(T, RET_HEADS)
        spl = [stat(LRU_T) for _ in range(5)]
        spl_series = stat(LRU_T)
        LOG = sb("LOG", [P, T, ROUTE])
        ONE1, ONE2, ELOG = sb("ONE1", [P, T, EXPERTS]), sb("ONE2", [P, T, EXPERTS]), sb("ELOG", [P, T, EXPERTS])
        RANK, WGT = sb("RANK", [P, T, EXPERTS + 2]), sb("WGT", [P, T, EXPERTS + 2])

        x_loaded, table_loaded, const_loaded, table2_loaded, bias_loaded = (sem(n) for n in (
            "x_loaded", "table_loaded", "const_loaded", "table2_loaded", "bias_loaded"))
        early_loaded = [sem(f"early_loaded{i}") for i in range(EARLY)]
        ln_loaded = sem("ln_loaded")
        slot_loaded = [sem(f"slot_loaded{i}") for i in range(RING)]
        x_ready, xn_ready = sem("x_ready"), sem("xn_ready")
        dve_step = sem("dve_step")
        tr_done, tr_act, tr_dve = sem("tr_done"), sem("tr_act"), sem("tr_dve")
        pj_done, pj_free = sem("pj_done"), [sem("pj_free0"), sem("pj_free1")]
        var_ready, std_ready = sem("var_ready"), sem("std_ready")
        rope_ready, rank_ready, mla_ready, lam_ready, lam_exp = (sem(n) for n in (
            "rope_ready", "rank_normed", "mla_ready", "lam_ready", "lam_exp"))
        d_score, d_nb, d_exp, d_w, d_pt, d_ptc, d_pv, d_o = (sem(n) for n in (
            "d_score_done", "d_nb_ready", "d_exp_done", "d_w_ready", "d_pT_done", "d_pT_copied", "d_pv_done",
            "d_o_copied"))
        d_sq, ao_scale, ao_ready, pool_step, a_rec = (sem(n) for n in (
            "d_squares_done", "ao_scale_ready", "ao_ready", "pool_step", "reciprocal_ready"))
        a_score, a_free, a_nb, a_exp, a_p, a_pt, a_ptc, a_pv, a_o = (sem(n) for n in (
            "score_done", "score_free", "nb_ready", "exp_done", "prob_ready", "pT_done", "pT_copied", "pv_done",
            "o_copied"))
        logits_done, r_gmax, r_gexp, r_d, r_p2, r_one, rank_done, r_top, top_done, flag_ready, route_ready = (
            sem(n) for n in ("logits_done", "group_max", "group_exp", "top_gap", "second_exp", "chosen_ready",
                             "rank_done", "rank_top", "top_done", "flag_ready", "route_ready"))

        def signals(tag):
            return {n: sem(f"{tag}_{n}") for n in (
                "sel_ready", "selw_ready", "gather_lo", "gather_hi", "xg_lo", "xg_hi", "gate_done", "up_done",
                          "silu_done", "h_ready", "hT_done", "hT_copied", "swt_done", "swt_copied", "y0_done",
                          "y1_done", "y0_copied", "y1_copied")}

        moe = signals("moe")
        over = [signals(f"over{l}") for l in range(DEPTH)]
        over_loaded = [sem(f"over{l}_loaded") for l in range(DEPTH)]
        over_free = [sem(f"over{l}_slots_free") for l in range(DEPTH)]
        over_shift = [sem(f"over{l}_shifted") for l in range(DEPTH)]
        acc_done = sem("acc_done")
        lru_cvd, lru_gm, lru_g, lru_t, lru_a, lru_sq, lru_sqr, lru_y = (sem(n) for n in (
            "lru_conv", "lru_gate_mm", "lru_gates", "lru_tanh", "lru_decay", 
            "lru_squares", "lru_sum", "lru_out"))
        sp_exp, sp_in = sem("softplus_exp"), sem("softplus_in")
        r_rope, r_sc, r_scd, r_o, r_oc, r_y, r_silu = (sem(n) for n in (
            "ret_rope", "ret_score", "ret_decayed", "ret_out", "ret_out_copied", "ret_y", "ret_silu"))
        f_up, f_cv0, f_cv, f_act, f_gelu, f_down = (sem(n) for n in (
            "ffn_up_done", "ffn_conv0", "ffn_conv", "ffn_act", "ffn_gelu", "ffn_down_done"))
        out_ready, stored = sem("out_ready"), sem("stored")

        def columns(w, n, width=512):
            return w[:, n * 512:n * 512 + width].rearrange("(c p) f -> p c f", p=P)

        def slot(i, a, b):
            return ring[:, i % RING, 0:a * b].rearrange("p (a b) -> p a b", b=b)

        items = []

        def item(src, a, b, used, value):
            items.append((src, slot(len(items), a, b), used, value))
            return len(items) - 1

        G_EIN, G_UQ, G_UKV, G_EO, G_QKV, G_OO, G_IN2, G_OUT2 = 0, 4, 6, 8, 10, 16, 18, 24
        EIN = [0, 1, 3, 2]
        I_EIN = [item(columns(w_in, n, min(512, EVEN_IN - 512 * n)), C, min(512, EVEN_IN - 512 * n), pj_done,
                      2 * g + 2) for g, n in enumerate(EIN)]
        I_UQ = item(w_uq.rearrange("(c p) f -> p c f", p=P), 2, 768, pj_done, 2 * G_UKV)
        I_UKV = item(w_ukv.rearrange("(c p) f -> p c f", p=P), 1, 1024, pj_done, 2 * G_EO)

        def out_items(w, g):
            return [item(columns(w, n), C, 512, pj_done, 2 * g + 3 + n) for n in range(2)]

        I_EO = out_items(w_o, G_EO)

        def expert_source(l, e, k):
            if k < 2:
                return w_gate[l, bass.ds(e, 1)].rearrange("o (c p) f -> p (o c) f", p=P)
            if k < 4:
                return w_up[l, bass.ds(e, 1)].rearrange("o (c p) f -> p (o c) f", p=P)
            return w_down[l, bass.ds(e, 1)].rearrange("o (j p) f -> p (o j) f", p=P)

        def as_expert(v, k):
            return v.rearrange("p (a b) -> p a b", b=FE if k < 4 else D)

        def expert_items(l):
            first = len(items)
            for p in range(PAIRS):
                for k in range(EARLY if p == 0 else 0, 6):
                    used = (moe["gate_done"], moe["up_done"], moe["y1_done"])[k // 2]
                    items.append((None, None, used, PAIRS * l + p + 1))
            return first

        I_MOE = [expert_items(0)]
        I_QKV = [item(columns(w_qkv, n), C, 512, pj_done, 2 * (G_QKV + n) + 2) for n in range(6)]
        I_OO = out_items(w_o2, G_OO)
        I_MOE.append(expert_items(1))
        I_IN2 = [item(columns(w_in2, n), C, 512, pj_done, 2 * (G_IN2 + n) + 2) for n in range(6)]
        I_OUT2 = out_items(w_out2, G_OUT2)
        I_UP = [item(columns(ffn_up, n), C, 512, f_up, 4 * n + 4) for n in range(FF2 // 512)]
        I_DN = [item(ffn_down[512 * n:512 * (n + 1), :].rearrange("(c p) f -> p c f", p=P), 4, D, f_down, n + 1)
                for n in range(6)]

        def ring_item(l, k):
            return I_MOE[l] + 6 - EARLY + k

        def arrived(i):
            return slot_loaded[i % RING], 16 * (i // RING + 1)

        TR = {}
        tr_groups = 0
        for name, groups in (("x", 4), ("qk", 4), ("c", 2), ("qb", 4), ("kb", 4), ("ao", 2), ("ln0", 4), ("ln1", 4),
                             ("ln2", 4), ("n1", 4), ("rqk", 4), ("yr", 2), ("n2", 4)):
            TR[name] = (tr_groups, groups)
            tr_groups += groups

        N_MLA0, N_NA0 = 0, B_HEADS

        def counted(eng, steps):
            n = [0]

            def link(ins):
                n[0] += 1
                ins.then_inc(steps, 1)
                eng.wait_ge(steps, n[0])
            return link

        def rope(e, link, x4, rot, half, heads, tmp):
            for t in range(T):
                x1, x2 = x4[:, t, :, 0:half], x4[:, t, :, half:2 * half]
                cos = rot[:, 0, t, :].unsqueeze(1).broadcast_to([P, heads, half])
                sin = rot[:, 1, t, :].unsqueeze(1).broadcast_to([P, heads, half])
                a, b, c, d = (m[:, 0:heads * half].rearrange("p (h f) -> p h f", f=half) for m in tmp)
                e.tensor_tensor(a, x1, cos, ALU.mult)
                e.tensor_tensor(b, x2, sin, ALU.mult)
                e.tensor_tensor(c, x2, cos, ALU.mult)
                link(e.tensor_tensor(d, x1, sin, ALU.mult))
                e.tensor_tensor(x1, a, b, ALU.subtract)
                last = e.tensor_tensor(x2, c, d, ALU.add)
                if t == 0:
                    link(last)
            return last

        block = ctx.enter_context(nc.Block())

        @block.sync
        def _(sp):
            sp.dma_start(X[:, :, :], x.rearrange("(t p) d -> p t d", p=P)).then_inc(x_loaded, 16)
            sp.dma_start(KT[:, :], table).then_inc(table_loaded, 16)

            def load(i):
                src, view, _, _ = items[i]
                if i >= RING:
                    sp.wait_ge(items[i - RING][2], items[i - RING][3])
                sp.dma_start(view, src).then_inc(slot_loaded[i % RING], 16)

            def load_expert(l, k, e, loaded=None):
                slot_no = ring_item(l, k) % RING
                signal = slot_loaded[slot_no] if loaded is None else loaded
                sp.dma_start(as_expert(ring[:, slot_no, :], k), expert_source(l, e, k)).then_inc(signal, 16)

            def load_experts(l, arena_free):
                for k in range(EARLY, 6):
                    i = ring_item(l, k - 6)
                    sp.wait_ge(items[i - RING][2], items[i - RING][3])
                    load_expert(l, k, k % 2)
                i = ring_item(l, 0)
                sp.wait_ge(items[i - RING][2], items[i - RING][3])
                load_expert(l, 0, 2)
                sp.wait_ge(pj_done, arena_free)
                for k in range(EARLY):
                    sp.dma_start(as_expert(FIRST[k], k), expert_source(l, k % 2, k)).then_inc(early_loaded[k], 16)
                for k in range(1, 6):
                    i = ring_item(l, k)
                    sp.wait_ge(items[i - RING][2], items[i - RING][3])
                    load_expert(l, k, 2 + k % 2)
                with sp.Fori(2, PAIRS) as p:
                    for k in range(6):
                        used = (moe["gate_done"], moe["up_done"], moe["y1_done"])[k // 2]
                        sp.wait_ge(used, p + PAIRS * l)
                        load_expert(l, k, p * 2 + k % 2)
                sp.wait_ge(flag_ready, l + 1)
                more = sp.value_load(FLAG[0:1, l:l + 1], min_val=0, max_val=1)
                with sp.If(more > 0):
                    with sp.Fori(0, ROUNDS_MORE) as r:
                        with sp.Fori(0, PAIRS) as p:
                            sp.wait_ge(over_free[l], r * PAIRS + p + 1)
                            for k in range(6):
                                load_expert(l, k, p * 2 + k % 2, over_loaded[l])
                    sp.wait_ge(over_free[l], ROUNDS_MORE * PAIRS + 1)

            for i in I_EIN:
                load(i)
                if i == 0:
                    sp.dma_start(COLS[:, :], cols).then_inc(const_loaded, 16)
                    sp.dma_start(ROWS[:, :], rows[0, :].partition_broadcast(P)).then_inc(const_loaded, 16)
            sp.dma_start(WR[:, :, :, :], w_route).then_inc(const_loaded, 16)
            for i in [I_UQ, I_UKV] + I_EO:
                load(i)
            load_experts(0, 2 * G_EO + 1)
            for i in I_QKV + I_OO:
                load(i)
                if i == I_QKV[0]:
                    sp.dma_start(G[:, :, :], na_bias).then_inc(bias_loaded, 16)
            load_experts(1, 2 * G_OO + 1)
            for i in I_IN2 + I_OUT2 + I_UP + I_DN:
                load(i)
                if i == I_IN2[1]:
                    sp.dma_start(KT2[:, :], table2).then_inc(table2_loaded, 16)
                    sp.dma_start(GATE[:, :, :], gates).then_inc(table2_loaded, 16)
            for t in range(T):
                sp.wait_ge(out_ready, t + 1)
                sp.dma_start(out[t * P:(t + 1) * P, :], X[:, t, :]).then_inc(stored, 16)
            sp.wait_ge(stored, 16 * T)

        @block.gpsimd
        def _(pool):
            def norm_rows(n):
                pool.dma_start(LNR[:, :, :].rearrange("p a d -> p (a d)"),
                               ln_rows[n, :].partition_broadcast(P)).then_inc(ln_loaded, 16)

            link = counted(pool, pool_step)
            pool.wait_ge(rope_ready, 1)
            norm_rows(0)
            for t in range(T):
                pool.wait_ge(pj_free[t], G_EO)
            q4 = QB[:, :, :].rearrange("p t (h f) -> p t h f", f=B_QK)
            link(rope(nc.gpsimd, link, q4[:, :, :, B_NOPE:B_QK], rot_b, B_HALF, B_HEADS, ROTB))
            link(rope(nc.gpsimd, link, E[:, :, KR0:EVEN_IN].unsqueeze(2), rot_b, B_HALF, 1, ROTB))
            kv4 = KV[:, :, :].rearrange("p t (h f) -> p t h f", f=B_NOPE + B_V)
            kc4 = KC.rearrange("p t (h f) -> p t h f", f=B_QK)
            pool.wait_ge(tr_done, sum(TR["qk"]))
            for t in range(T):
                nc.gpsimd.tensor_copy(kc4[:, t, :, 0:B_NOPE], kv4[:, t, :, 0:B_NOPE])
                last = nc.gpsimd.tensor_copy(kc4[:, t, :, B_NOPE:B_QK],
                                             E[:, t, KR0:EVEN_IN].unsqueeze(1).broadcast_to([P, B_HEADS, B_ROPE]))
            last.then_inc(mla_ready, 1)
            pool.wait_ge(ao_scale, 1)
            pool.wait_ge(const_loaded, 48)
            sub = ROWS[:, R_SUB:R_SUB + P].unsqueeze(1).broadcast_to([P, A_HEADS, P])
            ao = [AO[:, t, :].rearrange("p (h e) -> p h e", h=A_HEADS) for t in range(T)]
            for t in range(T):
                last = nc.gpsimd.tensor_tensor(ao[t], ao[t], rs_a[:, t, :].unsqueeze(2).broadcast_to([P, A_HEADS, P]),
                                               ALU.mult)
            link(last)
            for t in range(T):
                last = nc.gpsimd.tensor_tensor(ao[t], ao[t], sub, ALU.mult)
            last.then_inc(ao_ready, 1)
            pool.wait_ge(x_ready, 2)
            norm_rows(1)
            pool.wait_ge(x_ready, 4)
            norm_rows(2)
            for a in range(N_NA0, N_NA0 + C_HEADS):
                pool.wait_ge(a_rec, a - N_NA0 + 1)
                for t in range(T):
                    last = nc.gpsimd.tensor_scalar(PN[a % 3][:, t, :], PN[a % 3][:, t, :], sm[:, a % 4, t:t + 1], None,
                                                   ALU.mult)
                last.then_inc(a_p, 1)
            pool.wait_ge(x_ready, 6)
            norm_rows(3)
            pool.wait_ge(x_ready, 8)
            norm_rows(4)
            pool.wait_ge(r_y, 1)
            norm_rows(5)

        @block.tensor
        def _(pe):
            def transposes(name, source, width=P, blocks=None):
                k0, groups = TR[name]
                blocks = 2 * groups if blocks is None else blocks
                for g in range(groups):
                    k = k0 + g
                    if k >= 4:
                        pe.wait_ge(tr_dve if k % 2 else tr_act, (k - 4) // 2 + 1)
                    for b in range(2 * g, min(2 * g + 2, blocks)):
                        for t in range(T):
                            last = nc.tensor.transpose(
                                bank[4 + k % 4][0:width, (b % 2) * SEQ + t * P:(b % 2) * SEQ + (t + 1) * P],
                                source(b, t), ident)
                    last.then_inc(tr_done, 1)

            def transposes_by_token(name, source, ready=None, n0=0):
                k0 = TR[name][0]
                for t in range(T):
                    if ready is not None:
                        pe.wait_ge(ready, n0 + t + 1)
                    for h in range(2):
                        k = k0 + 2 * t + h
                        if k >= 4:
                            pe.wait_ge(tr_dve if k % 2 else tr_act, (k - 4) // 2 + 1)
                        for j in range(4):
                            c = 4 * h + j
                            last = nc.tensor.transpose(bank[4 + k % 4][:, j * P:(j + 1) * P],
                                                       source[:, t, c * P:(c + 1) * P], ident)
                        last.then_inc(tr_done, 1)

            def transposed(name):
                k = sum(TR[name])
                pe.wait_ge(tr_act, k // 2)
                pe.wait_ge(tr_dve, k // 2)

            def project(g, i, lhsT, rhs, kt):
                pe.wait_ge(*arrived(i))
                for t in range(T):
                    if g >= 2:
                        pe.wait_ge(pj_free[t], g - 1)
                    width = rhs(0).shape[1]
                    for c in range(kt):
                        last = nc.tensor.matmul(bank[g % 2 * 2 + t][:, 0:width], lhsT(c, t), rhs(c),
                                                start=(c == 0), stop=(c == kt - 1))
                    last.then_inc(pj_done, 1)

            def project_out(g0, i):
                for t in range(T):
                    for n in range(2):
                        if t == 0:
                            pe.wait_ge(*arrived(i[n]))
                        pe.wait_ge(pj_free[t], g0 + n - 1)
                        for c in range(C):
                            last = nc.tensor.matmul(bank[(g0 + n) % 2 * 2 + t][:, :], mixed_tile(c, t),
                                                    slot(i[n], C, 512)[:, c, :], start=(c == 0), stop=(c == C - 1))
                        last.then_inc(pj_done, 1)

            def project_t(g, i):
                pe.wait_ge(*arrived(i))
                for half in range(2):
                    if g >= 2:
                        pe.wait_ge(pj_free[half], g - 1)
                    for f in range(2):
                        for c in range(C):
                            last = nc.tensor.matmul(
                                bank[g % 2 * 2 + half][:, f * SEQ:(f + 1) * SEQ],
                                slot(i, C, 512)[:, c, (2 * half + f) * P:(2 * half + f + 1) * P],
                                XT[:, c, :], start=(c == 0), stop=(c == C - 1))
                    last.then_inc(pj_done, 1)

            def x_tile(c, t):
                return XT[:, c, t * P:(t + 1) * P]

            def mixed_tile(c, t):
                return MT[:, c, t * P:(t + 1) * P]

            def attention(a0, n, q, k, v, probs, probs_t, free):
                for i in range(n + 3):
                    if i < n:
                        a = a0 + i
                        if i >= 3:
                            pe.wait_ge(free, i - 2)
                        for t in range(T):
                            last = nc.tensor.matmul(bank[4 + a % 3][:, t * SEQ:(t + 1) * SEQ], q(i, t), k(i),
                                                    start=True, stop=True)
                        last.then_inc(a_score, 1)
                    if 0 <= i - 2 < n:
                        a = a0 + i - 2
                        pe.wait_ge(a_p, a + 1)
                        if a >= 2:
                            pe.wait_ge(a_ptc, a - 1)
                        for t in range(T):
                            for kt in range(T):
                                last = nc.tensor.transpose(
                                    bank[a % 2][:, kt * SEQ + t * P:kt * SEQ + (t + 1) * P],
                                    probs[a % 3][:, t, kt * P:(kt + 1) * P], ident)
                        last.then_inc(a_pt, 1)
                    if 0 <= i - 3 < n:
                        a = a0 + i - 3
                        pair = a // 2
                        pe.wait_ge(a_ptc, a + 1)
                        if a % 2 == 0 and pair >= 2:
                            pe.wait_ge(a_o, pair - 1)
                        for kt in range(T):
                            last = nc.tensor.matmul(bank[2 + pair % 2][(a % 2) * 64:(a % 2) * 64 + 64, 0:SEQ],
                                                    v(i - 3, kt), probs_t[a % 2][:, kt, :],
                                                    start=(kt == 0), stop=(kt == T - 1))
                        last.then_inc(a_pv, 1)

            def gather(s):
                for c in range(C):
                    for t in range(T):
                        last = nc.tensor.matmul(bank[6 + c // 4][:, c % 4 * P:(c % 4 + 1) * P],
                                                X[:, t, c * P:(c + 1) * P], SEL[:, t, :],
                                                start=(t == 0), stop=(t == T - 1))
                    if c == C // 2 - 1:
                        last.then_inc(s["gather_lo"], 1)
                last.then_inc(s["gather_hi"], 1)

            def experts(s, n, g, matrix, used=None):
                pe.wait_ge(s["xg_lo"], g + 1)
                pe.wait_ge(s["xg_hi"], g + 1)
                for m, done in ((0, s["gate_done"]), (1, s["up_done"])):
                    w = [matrix(2 * m), matrix(2 * m + 1)]
                    for c in range(C):
                        for e in range(2):
                            last = nc.tensor.matmul(bank[4 + m][64 * e:64 * e + 64, :],
                                                    XG[:, c, 64 * e:64 * e + 64], w[e][:, c, :],
                                                    start=(c == 0), stop=(c == C - 1))
                    last.then_inc(done, 1)
                pe.wait_ge(s["sel_ready"], g + 2)
                gather(s)
                pe.wait_ge(s["h_ready"], n + 1)
                for j in range(FE // P):
                    last = nc.tensor.transpose(bank[4][:, j * P:(j + 1) * P], H[:, j * P:(j + 1) * P], ident)
                last.then_inc(s["hT_done"], 1)
                pe.wait_ge(s["selw_ready"], n + 1)
                for t in range(T):
                    last = nc.tensor.transpose(bank[5][:, t * P:(t + 1) * P], SELW[:, t, :], ident)
                last.then_inc(s["swt_done"], 1)
                w = [matrix(4), matrix(5)]
                pe.wait_ge(s["hT_copied"], n + 1)
                for half, free, done in ((0, s["xg_lo"], s["y0_done"]), (1, s["xg_hi"], s["y1_done"])):
                    pe.wait_ge(free, g + 2)
                    for j in range(FE // P):
                        for e in range(2):
                            last = nc.tensor.matmul(bank[6 + half][64 * e:64 * e + 64, :],
                                                    HT[:, j, 64 * e:64 * e + 64],
                                                    w[e][:, j, 512 * half:512 * half + 512],
                                                    start=(j == 0), stop=(j == FE // P - 1))
                    last.then_inc(done, 1)
                pe.wait_ge(s["swt_copied"], n + 1)
                for half, copied in ((0, s["y0_copied"]), (1, s["y1_copied"])):
                    pe.wait_ge(copied, n + 1)
                    for t in range(T):
                        last = nc.tensor.matmul(bank[2 * t + half][:, :], SWT[:, t, :],
                                                Y[:, 512 * half:512 * half + 512],
                                                start=False, stop=False, skip_group_check=True)
                if used is not None:
                    last.then_inc(used, 1)

            def moe_layer(l):
                for t in range(T):
                    for c in range(C):
                        last = nc.tensor.matmul(bank[4][:, t * 64:t * 64 + ROUTE], x_tile(c, t), WR[:, l, c, :],
                                                start=(c == 0), stop=(c == C - 1))
                last.then_inc(logits_done, 1)
                for b in range(4):
                    nc.tensor.matmul(bank[b][:, :], zeros, XT[:, 0:2, :].rearrange("p a b -> p (a b)"),
                                     start=True, stop=False, skip_group_check=True)
                pe.wait_ge(r_one, l + 1)
                for t in range(T):
                    if t:
                        nc.tensor.matmul(bank[4][:, t * 64:t * 64 + EXPERTS], ones, ELOG[:, 0, :],
                                         start=True, stop=False)
                    last = nc.tensor.matmul(bank[4][:, t * 64:t * 64 + EXPERTS], earlier, ELOG[:, t, :],
                                            start=(t == 0), stop=True)
                last.then_inc(rank_done, 1)
                pe.wait_ge(r_top, l + 1)
                nc.tensor.transpose(bank[5][0:1, 0:P], rtop, ident).then_inc(top_done, 1)
                pe.wait_ge(moe["sel_ready"], (PAIRS + 1) * l + 1)
                gather(moe)

                def ring_matrix(k, count, loaded=None):
                    slot_no = ring_item(l, k) % RING
                    pe.wait_ge(slot_loaded[slot_no] if loaded is None else loaded, count)
                    return as_expert(ring[:, slot_no, :], k)

                def first_matrix(k):
                    if k >= EARLY:
                        return ring_matrix(k, arrived(ring_item(l, k - 6))[1])
                    pe.wait_ge(early_loaded[k], 16 * (l + 1))
                    return as_expert(FIRST[k], k)

                experts(moe, PAIRS * l, (PAIRS + 1) * l, first_matrix)
                with pe.Fori(1, PAIRS) as p:
                    experts(moe, p + PAIRS * l, p + (PAIRS + 1) * l,
                            lambda k: ring_matrix(k, (p + ring_item(l, k) // RING) * 16))
                pe.wait_ge(flag_ready, l + 1)
                more = pe.value_load(FLAG[0:1, l:l + 1], min_val=0, max_val=1)
                with pe.If(more > 0):
                    s = over[l]
                    pe.drain().then_inc(over_free[l], 1)
                    with pe.Fori(0, ROUNDS_MORE) as r:
                        pe.wait_ge(s["sel_ready"], r * (PAIRS + 1) + 1)
                        gather(s)
                        with pe.Fori(0, PAIRS) as p:
                            n = r * PAIRS + p
                            experts(s, n, r * (PAIRS + 1) + p,
                                    lambda k: ring_matrix(k, (n + 1) * 96, over_loaded[l]), over_free[l])
                pe.drain().then_inc(acc_done, 1)

            pe.wait_ge(x_loaded, 16)
            pe.wait_ge(table_loaded, 16)
            transposes_by_token("x", X)
            transposed("x")
            for g, n in enumerate(EIN):
                w = min(512, EVEN_IN - 512 * n)
                project(G_EIN + g, I_EIN[g], x_tile, lambda c: slot(I_EIN[g], C, w)[:, c, :], C)
            pe.wait_ge(rope_ready, 1)
            transposes("qk", lambda b, t: E[:, t, b * P:(b + 1) * P])
            pe.wait_ge(rank_ready, 1)
            transposes("c", lambda b, t: E[:, t, CQ0 + b * P:CQ0 + (b + 1) * P], blocks=3)
            transposed("c")
            for n in range(2):
                project(G_UQ + n, I_UQ, lambda c, t: CT[:, c, t * P:(t + 1) * P],
                        lambda c: slot(I_UQ, 2, 768)[:, c, 384 * n:384 * n + 384], 2)
            for n in range(2):
                project(G_UKV + n, I_UKV, lambda c, t: CT[:, 2, t * P:(t + 1) * P],
                        lambda c: slot(I_UKV, 1, 1024)[:, 0, 512 * n:512 * n + 512], 1)
            for i in range(A_HEADS + 2):
                if i < A_HEADS:
                    if i >= 2:
                        pe.wait_ge(d_exp, 2 * (i - 1))
                    for m in range(2):
                        half = slice(m * A_DIM, (m + 1) * A_DIM)
                        for t in range(T):
                            last = nc.tensor.matmul(bank[4 + 2 * (i % 2) + m][:, t * SEQ:(t + 1) * SEQ],
                                                    QKT[half, i, t * P:(t + 1) * P], QKT[half, 4 + i, :],
                                                    start=True, stop=True)
                        last.then_inc(d_score, 1)
                if 0 <= i - 1 < A_HEADS:
                    h = i - 1
                    pe.wait_ge(d_w, h + 1)
                    if h >= 2:
                        pe.wait_ge(d_ptc, h - 1)
                    for t in range(T):
                        for kt in range(T):
                            last = nc.tensor.transpose(bank[h % 2][:, kt * SEQ + t * P:kt * SEQ + (t + 1) * P],
                                                       PB[2 * (h % 2)][:, t, kt * P:(kt + 1) * P], ident)
                    last.then_inc(d_pt, 1)
                if i >= 2:
                    h = i - 2
                    pe.wait_ge(d_ptc, h + 1)
                    if h >= 2:
                        pe.wait_ge(d_o, h - 1)
                        pe.wait_ge(d_sq, h - 1)
                    for t in range(T):
                        for kt in range(T):
                            last = nc.tensor.matmul(bank[2 + h % 2][:, t * P:(t + 1) * P],
                                                    PT[h % 2][:, kt, t * P:(t + 1) * P],
                                                    E[:, kt, VA0 + h * P:VA0 + (h + 1) * P],
                                                    start=(kt == 0), stop=(kt == T - 1))
                    last.then_inc(d_pv, 1)
            pe.wait_ge(mla_ready, 1)
            pe.wait_ge(d_o, A_HEADS)
            pe.wait_ge(d_sq, A_HEADS)
            transposes("qb", lambda b, t: QB[:, t, b * B_QK:(b + 1) * B_QK], B_QK)
            transposes("kb", lambda b, t: KC[:, t, b * B_QK:(b + 1) * B_QK], B_QK)
            transposed("kb")
            attention(N_MLA0, B_HEADS, lambda h, t: QBT[0:B_QK, h, t * P:(t + 1) * P], lambda h: KBT[0:B_QK, h, :],
                      lambda h, kt: KV[:, kt, h * 128 + B_NOPE:(h + 1) * 128], PB, PT, a_exp)
            pe.wait_ge(ao_ready, 1)
            transposes("ao", lambda b, t: AO[:, t, b * P:(b + 1) * P])
            transposed("ao")
            pe.wait_ge(a_o, B_HEADS // 2)
            project_out(G_EO, I_EO)
            transposes_by_token("ln0", X, x_ready, 0)
            transposed("ln0")
            moe_layer(0)

            transposes_by_token("ln1", X, x_ready, 2)
            transposed("ln1")
            for n in range(4):
                project_t(G_QKV + n, I_QKV[n])
            for n in range(4, 6):
                project(G_QKV + n, I_QKV[n], x_tile, lambda c: slot(I_QKV[n], C, 512)[:, c, :], C)
            for t in range(2):
                pe.wait_ge(pj_free[t], G_OO)

            def head_rows(h):
                return slice(h % 2 * C_DIM, h % 2 * C_DIM + C_DIM)

            attention(N_NA0, C_HEADS, lambda h, t: OQ[head_rows(h), h // 2, t * P:(t + 1) * P],
                      lambda h: OK[head_rows(h), h // 2, :],
                      lambda h, kt: OV[:, kt, h * C_DIM:(h + 1) * C_DIM], PN, PTN, a_free)
            pe.wait_ge(a_o, (B_HEADS + C_HEADS) // 2)
            project_out(G_OO, I_OO)
            transposes_by_token("ln2", X, x_ready, 4)
            transposed("ln2")
            moe_layer(1)

            transposes_by_token("n1", XN, xn_ready, 0)
            transposed("n1")

            def project_2(n):
                project(G_IN2 + n, I_IN2[n], x_tile, lambda c: slot(I_IN2[n], C, 512)[:, c, :], C)

            for n in range(2):
                project_t(G_IN2 + n, I_IN2[n])
            project_2(2)
            pe.wait_ge(table2_loaded, 32)
            pe.wait_ge(lru_cvd, LRU_T)
            for m in range(2):
                for half in range(2):
                    for f in range(2):
                        c = 2 * half + f
                        last = nc.tensor.matmul(bank[4 + 2 * m + half][:, f * SEQ:(f + 1) * SEQ],
                                                GATE[:, m, c * P:(c + 1) * P], LX[:, c, :], start=True, stop=True)
                    last.then_inc(lru_gm, 1)
            project_2(3)
            project_2(4)
            pe.wait_ge(r_rope, 1)
            pe.wait_ge(lru_g, 4)
            transposes("rqk", lambda b, t: TOK[:, t, b * P:(b + 1) * P])
            project_2(5)
            transposed("rqk")
            for h in range(RET_HEADS):
                nc.tensor.matmul(bank[4 + h][:, 0:SEQ], RQK[:, 4 + h, 0:P], RQK[:, h, :], start=True, stop=True)
                nc.tensor.matmul(bank[4 + h][:, SEQ:DEC_W], RQK[:, 4 + h, P:SEQ], RQK[:, h, P:SEQ],
                                 start=True, stop=True).then_inc(r_sc, 1)
            pe.wait_ge(pj_free[0], G_OUT2)
            pe.wait_ge(pj_free[1], G_OUT2)
            pe.wait_ge(lru_sq, 1)
            for c in range(LRU_T):
                last = nc.tensor.matmul(bank[2][:, 0:SEQ], ones, LT_[:, c, :], start=(c == 0), stop=(c == LRU_T - 1))
            last.then_inc(lru_sqr, 1)
            for h in range(RET_HEADS):
                pe.wait_ge(r_scd, h + 1)
                if h >= 2:
                    pe.wait_ge(r_oc, h - 1)
                b = bank[h % 2]
                v = [TOK[:, t, 1024 + h * P:1024 + (h + 1) * P] for t in range(T)]
                nc.tensor.matmul(b[:, 0:P], RS[:, h, 0:P], v[0], start=True, stop=True)
                nc.tensor.matmul(b[:, P:SEQ], RS[:, h, P:SEQ], v[0], start=True, stop=False)
                nc.tensor.matmul(b[:, P:SEQ], RS[:, h, SEQ:DEC_W], v[1], start=False, stop=True).then_inc(r_o, 1)
            pe.wait_ge(r_y, 1)
            transposes("yr", lambda b, t: YR[:, t, b * P:(b + 1) * P])
            transposed("yr")
            pe.wait_ge(lru_y, 1)
            project_out(G_OUT2, I_OUT2)
            transposes_by_token("n2", XN2, xn_ready, 2)
            transposed("n2")
            for f in range(FF2_T):
                i = I_UP[f // 4]
                if f % 4 == 0:
                    pe.wait_ge(*arrived(i))
                if f >= 4:
                    pe.wait_ge(f_cv, f - 3)
                for c in range(C):
                    last = nc.tensor.matmul(bank[f % 4][:, 0:SEQ], slot(i, C, 512)[:, c, f % 4 * P:(f % 4 + 1) * P],
                                            XT[:, c, :], start=(c == 0), stop=(c == C - 1))
                last.then_inc(f_up, 1)
            for t in range(T):
                for n in range(6):
                    i = I_DN[n]
                    if t == 0:
                        pe.wait_ge(*arrived(i))
                        pe.wait_ge(f_act, 4 * n + 4)
                    for c in range(4):
                        for half in range(2):
                            last = nc.tensor.matmul(bank[4 + 2 * t + half][:, :],
                                                    ACTT[:, 4 * n + c, t * P:(t + 1) * P],
                                                    slot(i, 4, D)[:, c, 512 * half:512 * half + 512],
                                                    start=(n == 0 and c == 0), stop=(n == 5 and c == 3))
                last.then_inc(f_down, 1)

        @block.scalar
        def _(act):
            def evac_transposes(name, dest, width=P, blocks=None, gain=None):
                k0, groups = TR[name]
                blocks = 2 * groups if blocks is None else blocks
                for g in range(groups):
                    k = k0 + g
                    if k % 2:
                        continue
                    act.wait_ge(tr_done, k + 1)
                    n = min(2, blocks - 2 * g)
                    if gain is None:
                        last = nc.scalar.copy(dest(2 * g, n), bank[4 + k % 4][0:width, 0:n * SEQ].rearrange(
                            "p (a b) -> p a b", b=SEQ))
                    else:
                        for b in range(n):
                            last = nc.scalar.activation(dest(2 * g + b, 1), bank[4 + k % 4][0:width, b * SEQ:(b + 1) * SEQ],
                                                        ACT.Copy, scale=gain(2 * g + b))
                    last.then_inc(tr_act, 1)

            def evac_by_token(name, gain=None):
                for t in range(T):
                    k = TR[name][0] + 2 * t
                    act.wait_ge(tr_done, k + 1)
                    src = bank[4 + k % 4][:, :].rearrange("p (c s) -> p c s", s=P)
                    if gain is None:
                        last = nc.scalar.copy(XT[:, 0:4, t * P:(t + 1) * P], src)
                    else:
                        for c in range(4):
                            last = nc.scalar.activation(XT[:, c, t * P:(t + 1) * P], src[:, c, :], ACT.Copy,
                                                        scale=COLS[:, gain + c:gain + c + 1])
                    last.then_inc(tr_act, 1)

            def evac_chunk(g, dest):
                act.wait_ge(pj_done, 2 * g + 1)
                nc.scalar.copy(dest, bank[g % 2 * 2][:, 0:dest.free_size()].rearrange("p (a b) -> p a b", b=dest.shape[2])
                               if len(dest.shape) == 3 else bank[g % 2 * 2][:, 0:dest.shape[1]]).then_inc(pj_free[0], 1)

            roots = [0]

            def root(v):
                roots[0] += 1
                act.wait_ge(var_ready, roots[0])
                nc.scalar.activation(v, v, ACT.Sqrt).then_inc(std_ready, 1)

            def token_roots():
                for t in range(T):
                    root(var_l[:, t:t + 1])

            def attention(a0, n, probs, probs_t, scale):
                for i in range(n + 2):
                    if i < n:
                        a = a0 + i
                        act.wait_ge(a_nb, a + 1)
                        if a >= 3 and scale is not None:
                            act.wait_ge(a_pt, a - 2)
                        for t in range(T):
                            src = bank[4 + a % 3][:, t * SEQ:(t + 1) * SEQ] if scale is not None else probs[a % 3][:, t, :]
                            last = nc.scalar.activation(probs[a % 3][:, t, :], src, ACT.Exp, bias=nb[:, a % 4, t:t + 1],
                                                        scale=1.0 if scale is None else scale,
                                                        accum_out=sm[:, a % 4, t:t + 1])
                        last.then_inc(a_exp, 1)
                    if i >= 2:
                        a = a0 + i - 2
                        act.wait_ge(a_pt, a + 1)
                        if a >= 2:
                            act.wait_ge(a_pv, a - 1)
                        nc.scalar.copy(probs_t[a % 2][:, :, :], bank[a % 2][:, :].rearrange("p (a b) -> p a b", b=SEQ))\
                            .then_inc(a_ptc, 1)

            def experts(s, n, g):
                act.wait_ge(s["gate_done"], n + 1)
                nc.scalar.activation(SG, bank[4][:, :], ACT.Silu).then_inc(s["silu_done"], 1)
                act.wait_ge(s["gather_lo"], g + 2)
                nc.scalar.copy(XG[:, 0:4, :], bank[6][:, :].rearrange("p (a b) -> p a b", b=P)).then_inc(s["xg_lo"], 1)
                act.wait_ge(s["hT_done"], n + 1)
                nc.scalar.copy(HT[:, :, :], bank[4][:, :].rearrange("p (a b) -> p a b", b=P)).then_inc(s["hT_copied"], 1)
                act.wait_ge(s["swt_done"], n + 1)
                nc.scalar.copy(SWT[:, :, :], bank[5][:, 0:SEQ].rearrange("p (a b) -> p a b", b=P)).then_inc(s["swt_copied"], 1)
                act.wait_ge(s["y0_done"], n + 1)
                nc.scalar.copy(Y[:, 0:512], bank[6][:, :]).then_inc(s["y0_copied"], 1)

            def first_tokens(s, g):
                act.wait_ge(s["gather_lo"], g + 1)
                nc.scalar.copy(XG[:, 0:4, :], bank[6][:, :].rearrange("p (a b) -> p a b", b=P)).then_inc(s["xg_lo"], 1)

            def moe_layer(l):
                act.wait_ge(r_gmax, l + 1)
                for t in range(T):
                    last = nc.scalar.activation(rg[:, t, 0:GROUPS], LOG[:, t, 0:GROUPS], ACT.Exp, bias=gmn[:, t:t + 1],
                                                accum_out=gsum[:, t:t + 1])
                last.then_inc(r_gexp, 1)
                act.wait_ge(r_d, l + 1)
                nc.scalar.activation(p2, p2, ACT.Exp).then_inc(r_p2, 1)
                first_tokens(moe, (PAIRS + 1) * l)
                with act.Fori(0, PAIRS) as p:
                    experts(moe, p + PAIRS * l, p + (PAIRS + 1) * l)
                act.wait_ge(flag_ready, l + 1)
                more = act.value_load(FLAG[0:1, l:l + 1], min_val=0, max_val=1)
                with act.If(more > 0):
                    with act.Fori(0, ROUNDS_MORE) as r:
                        first_tokens(over[l], r * (PAIRS + 1))
                        with act.Fori(0, PAIRS) as p:
                            experts(over[l], r * PAIRS + p, r * (PAIRS + 1) + p)

            evac_by_token("x")
            for g, n in enumerate(EIN):
                if g == 3:
                    root(var_b[:, :, :])
                evac_chunk(G_EIN + g, E[:, 0, 512 * n:min(512 * n + 512, EVEN_IN)])
            act.wait_ge(const_loaded, 48)
            act.wait_ge(lam_ready, 1)
            nc.scalar.activation(lamv, lamv, ACT.Exp).then_inc(lam_exp, 1)
            evac_transposes("qk", lambda b, n: QKT[:, b:b + n, :])
            evac_transposes("c", lambda b, n: CT[:, b, :], blocks=3, gain=lambda b: COLS[:, Q_QN + b:Q_QN + b + 1])
            for n in range(2):
                evac_chunk(G_UQ + n, QB[:, 0, 384 * n:384 * n + 384])
            for n in range(2):
                evac_chunk(G_UKV + n, KV[:, 0, 512 * n:512 * n + 512])
            for i in range(A_HEADS + 2):
                if i < A_HEADS:
                    for m in range(2):
                        act.wait_ge(d_nb, 2 * i + m + 1)
                        if i >= 2:
                            act.wait_ge(d_pt, i - 1)
                        for t in range(T):
                            last = nc.scalar.activation(PB[2 * (i % 2) + m][:, t, :],
                                                        bank[4 + 2 * (i % 2) + m][:, t * SEQ:(t + 1) * SEQ], ACT.Exp,
                                                        bias=dnb[:, i % 2, m, t:t + 1], scale=A_DIM ** -0.5,
                                                        accum_out=dsm[:, i % 2, m, t:t + 1])
                        last.then_inc(d_exp, 1)
                if 0 <= i - 1 < A_HEADS:
                    h = i - 1
                    act.wait_ge(d_pt, h + 1)
                    if h >= 2:
                        act.wait_ge(d_pv, h - 1)
                    nc.scalar.copy(PT[h % 2][:, :, :], bank[h % 2][:, :].rearrange("p (a b) -> p a b", b=SEQ))\
                        .then_inc(d_ptc, 1)
                if i >= 2:
                    h = i - 2
                    act.wait_ge(d_o, h + 1)
                    for t in range(T):
                        last = nc.scalar.activation(SQA[:, t, h * P:(h + 1) * P], AO[:, t, h * P:(h + 1) * P],
                                                    ACT.Square, accum_out=var_a[:, t, h:h + 1])
                    last.then_inc(d_sq, 1)
            root(var_a[:, :, :])
            evac_transposes("qb", lambda b, n: QBT[0:B_QK, b:b + n, :], B_QK)
            evac_transposes("kb", lambda b, n: KBT[0:B_QK, b:b + n, :], B_QK)
            attention(N_MLA0, B_HEADS, PB, PT, B_QK ** -0.5)
            evac_transposes("ao", lambda b, n: MT[:, b:b + n, :])
            token_roots()
            evac_by_token("ln0")
            moe_layer(0)
            token_roots()
            evac_by_token("ln1")
            for n in range(4):
                evac_chunk(G_QKV + n, (OQ if n < 2 else OK)[:, 4 * (n % 2):4 * (n % 2) + 2, :])
            for n in range(2):
                evac_chunk(G_QKV + 4 + n, OV[:, 0, 512 * n:512 * n + 512])
            attention(N_NA0, C_HEADS, PN, PTN, None)
            token_roots()
            evac_by_token("ln2")
            moe_layer(1)
            token_roots()
            token_roots()
            evac_by_token("n1", Q_N1)
            evac_chunk(G_IN2, XL[:, 0:2, :])
            act.wait_ge(pj_done, 2 * (G_IN2 + 1) + 1)
            nc.scalar.activation(GL[:, 0:2, :], bank[(G_IN2 + 1) % 2 * 2][:, :].rearrange("p (a b) -> p a b", b=SEQ),
                                 ACT.Gelu_apprx_tanh).then_inc(pj_free[0], 1)
            act.wait_ge(pj_done, 2 * (G_IN2 + 1) + 2)
            act.wait_ge(pj_free[1], G_IN2 + 1)
            nc.scalar.activation(GL[:, 2:4, :], bank[(G_IN2 + 1) % 2 * 2 + 1][:, :].rearrange("p (a b) -> p a b", b=SEQ),
                                 ACT.Gelu_apprx_tanh).then_inc(pj_free[1], 1)
            def evac_2(n):
                evac_chunk(G_IN2 + n, TOK[:, 0, 512 * (n - 2):512 * (n - 1)])

            act.wait_ge(sp_in, 1)
            nc.scalar.activation(spl[1], spl[1], ACT.Exp).then_inc(sp_exp, 1)
            evac_2(2)
            act.wait_ge(sp_in, 2)
            for c in range(LRU_T):
                for m, dst in ((0, LA), (1, LI)):
                    act.wait_ge(lru_gm, 2 * m + c // 2 + 1)
                    last = nc.scalar.activation(dst[:, c, :], bank[4 + 2 * m + c // 2][:, c % 2 * SEQ:(c % 2 + 1) * SEQ],
                                                ACT.Tanh, scale=0.5, bias=spl[3 + m][:, c:c + 1])
                last.then_inc(lru_g, 1)
            act.wait_ge(lru_t, 1)
            nc.scalar.activation(LT_[:, :, :], LA[:, :, :], ACT.Tanh, scale=-1.0).then_inc(lru_a, 1)
            nc.scalar.activation(LA[:, :, :], LA[:, :, :], ACT.Exp).then_inc(lru_a, 1)
            root(LT_[:, :, :])
            evac_2(3)
            evac_2(4)
            evac_transposes("rqk", lambda b, n: RQK[:, b:b + n, :])
            evac_2(5)
            for t in range(T):
                if t:
                    act.wait_ge(pj_free[1], G_OUT2)
                else:
                    act.wait_ge(pj_free[0], G_OUT2)
                last = nc.scalar.activation(TOK[:, t, 1536:2048], TOK[:, t, 1536:2048], ACT.Silu)
            last.then_inc(r_silu, 1)
            root(LI[:, 0, :])
            root(var_h[:, :, :])
            evac_transposes("yr", lambda b, n: MT[:, 4 + b:4 + b + n, :])
            token_roots()
            evac_by_token("n2", Q_N2)
            for f in range(FF2_T + 2):
                if f < FF2_T:
                    act.wait_ge(f_up, f + 1)
                    if f >= 4:
                        act.wait_ge(f_gelu if f - 4 < DOWN_T else f_act, f - 3 if f - 4 < DOWN_T else f - 3 - DOWN_T)
                    nc.scalar.activation(CV[f % 4], bank[f % 4][:, 0:SEQ], ACT.Identity,
                                         scale=COLS[:, Q_FW + 2 * FF2_T + f:Q_FW + 2 * FF2_T + f + 1],
                                         bias=COLS[:, Q_FB + f:Q_FB + f + 1]).then_inc(f_cv0, 1)
                if 2 <= f < DOWN_T + 2:
                    act.wait_ge(f_cv, f - 1)
                    nc.scalar.activation(ACTT[:, f - 2, :], CV[(f - 2) % 4], ACT.Gelu_apprx_tanh).then_inc(f_gelu, 1)
            token_roots()

        @block.vector
        def _(dve):
            v = nc.vector
            link = counted(dve, dve_step)

            def evac_transposes(name, dest, width=P, blocks=None, gain=None):
                k0, groups = TR[name]
                blocks = 2 * groups if blocks is None else blocks
                for g in range(groups):
                    k = k0 + g
                    if k % 2 == 0:
                        continue
                    dve.wait_ge(tr_done, k + 1)
                    n = min(2, blocks - 2 * g)
                    if gain is None:
                        last = v.tensor_copy(dest(2 * g, n), bank[4 + k % 4][0:width, 0:n * SEQ].rearrange(
                            "p (a b) -> p a b", b=SEQ))
                    else:
                        for b in range(n):
                            last = v.tensor_scalar(dest(2 * g + b, 1), bank[4 + k % 4][0:width, b * SEQ:(b + 1) * SEQ],
                                                   gain(2 * g + b), None, ALU.mult)
                    last.then_inc(tr_dve, 1)

            def evac_by_token(name, gain=None):
                for t in range(T):
                    k = TR[name][0] + 2 * t + 1
                    dve.wait_ge(tr_done, k + 1)
                    dst = XT[:, 4:8, t * P:(t + 1) * P]
                    src = bank[4 + k % 4][:, :].rearrange("p (c s) -> p c s", s=P)
                    if gain is None:
                        last = v.tensor_copy(dst, src)
                    else:
                        last = v.tensor_tensor(dst, src, COLS[:, gain + 4:gain + 8].unsqueeze(2).broadcast_to([P, 4, P]),
                                               ALU.mult)
                    last.then_inc(tr_dve, 1)

            def evac_chunk(g, dest):
                dve.wait_ge(pj_done, 2 * g + 2)
                src = bank[g % 2 * 2 + 1]
                v.tensor_copy(dest, src[:, 0:dest.free_size()].rearrange("p (a b) -> p a b", b=dest.shape[2])
                              if len(dest.shape) == 3 else src[:, 0:dest.shape[1]]).then_inc(pj_free[1], 1)

            def add_out(g0, t, alpha):
                for n in range(2):
                    dve.wait_ge(pj_done, 2 * g0 + 2 * t + n + 1)
                    xs = X[:, t, 512 * n:512 * n + 512]
                    v.scalar_tensor_tensor(xs, xs, alpha, bank[(g0 + n) % 2 * 2 + t][:, :], ALU.mult, ALU.add)\
                        .then_inc(pj_free[t], 1)
                dve.wait_ge(pj_free[t], g0 + 2)

            def add_experts(t):
                for h in range(2):
                    xs = X[:, t, 512 * h:512 * h + 512]
                    last = v.scalar_tensor_tensor(xs, xs, ALPHA, bank[2 * t + h][:, :], ALU.mult, ALU.add)
                link(last)

            roots = [0]

            def inverse_root(var, out_):
                dve.wait_ge(std_ready, roots[0])
                link(v.reciprocal(out_, var))

            def ask_root(ins):
                roots[0] += 1
                ins.then_inc(var_ready, 1)

            norms = [0]

            def layer_norm(add):
                for t in range(T):
                    add(t)
                    for h in range(2):
                        last = v.bn_stats(bst[:, t, h, :], X[:, t, 512 * h:512 * h + 512])
                    link(last)
                    link(v.bn_aggr(mv[:, t, :], bst[:, t, :, :].rearrange("p a b -> p (a b)")))
                    ask_root(v.tensor_scalar(var_l[:, t:t + 1], mv[:, t, 1:2], LN_EPS, None, ALU.add))
                    dve.wait_ge(ln_loaded, 16 * (norms[0] + 1))
                    link(v.scalar_tensor_tensor(X[:, t, :], X[:, t, :], mv[:, t, 0:1], LNR[:, 0, :], ALU.subtract, ALU.mult))
                    inverse_root(var_l[:, t:t + 1], rs_l[:, t:t + 1])
                    v.scalar_tensor_tensor(X[:, t, :], X[:, t, :], rs_l[:, t:t + 1], LNR[:, 1, :], ALU.mult, ALU.add)\
                        .then_inc(x_ready, 1)
                norms[0] += 1
                dve.wait_ge(x_ready, T * norms[0])

            def token_rms(t, xn):
                link(v.tensor_tensor_reduce(xn[:, t, :], X[:, t, :], X[:, t, :], 1.0, 0.0, ALU.mult, ALU.add,
                                            var_l[:, t:t + 1]))
                ask_root(v.tensor_scalar(var_l[:, t:t + 1], var_l[:, t:t + 1], 1.0 / D, RMS_EPS, ALU.mult, ALU.add))
                inverse_root(var_l[:, t:t + 1], rs_l[:, t:t + 1])

            def normed(t, xn):
                token_rms(t, xn)
                v.tensor_scalar(xn[:, t, :], X[:, t, :], rs_l[:, t:t + 1], None, ALU.mult).then_inc(xn_ready, 1)

            def continue_pair(i, a0, dest):
                if i >= 4 and (i - 4) % 2 == 1:
                    pair = (a0 + i - 4) // 2
                    dve.wait_ge(a_pv, 2 * pair + 2)
                    v.tensor_copy(dest(pair - a0 // 2), bank[2 + pair % 2][:, 0:SEQ]).then_inc(a_o, 1)

            def attention(a0, n, probs, dest, scale, bias):
                for i in range(n + 4):
                    if i < n:
                        a = a0 + i
                        dve.wait_ge(a_score, a + 1)
                        ps = bank[4 + a % 3][:, :].rearrange("p (t k) -> p t k", t=T)
                        if bias is None:
                            link(v.tensor_reduce(mx[:, a % 4, :], ps, AX, ALU.max))
                            v.tensor_scalar(nb[:, a % 4, :], mx[:, a % 4, :], -scale, None, ALU.mult).then_inc(a_nb, 1)
                        else:
                            if a >= 3:
                                dve.wait_ge(a_pt, a - 2)
                            for t in range(T):
                                last = v.scalar_tensor_tensor(probs[a % 3][:, t, :], ps[:, t, :], scale, bias(i, t),
                                                              ALU.mult, ALU.add)
                            last.then_inc(a_free, 1)
                            dve.wait_ge(a_free, i + 1)
                            v.tensor_reduce(nb[:, a % 4, :], probs[a % 3][:, :, :], AX, ALU.max, negate=True)\
                                .then_inc(a_nb, 1)
                    if 0 <= i - 1 < n:
                        a = a0 + i - 1
                        dve.wait_ge(a_exp, a + 1)
                        if bias is not None:
                            v.reciprocal(sm[:, a % 4, :], sm[:, a % 4, :]).then_inc(a_rec, 1)
                            continue_pair(i, a0, dest)
                            continue
                        link(v.reciprocal(sm[:, a % 4, :], sm[:, a % 4, :]))
                        for t in range(T):
                            last = v.tensor_scalar(probs[a % 3][:, t, :], probs[a % 3][:, t, :], sm[:, a % 4, t:t + 1], None,
                                                   ALU.mult)
                        last.then_inc(a_p, 1)
                    continue_pair(i, a0, dest)

            def select(s, pair, g):
                io = iota_s.unsqueeze(1).broadcast_to([P, 2, SLOTS])
                for t in range(T):
                    last = v.tensor_tensor(SEL[:, t, :].rearrange("p (e s) -> p e s", e=2), io,
                                           RANK[:, t, bass.ds(pair * 2, 2)].unsqueeze(2).broadcast_to([P, 2, SLOTS]),
                                           ALU.is_equal)
                last.then_inc(s["sel_ready"], 1)

            def first_tokens(s, g):
                dve.wait_ge(s["gather_hi"], g + 1)
                v.tensor_copy(XG[:, 4:8, :], bank[7][:, :].rearrange("p (a b) -> p a b", b=P)).then_inc(s["xg_hi"], 1)

            def experts(s, pair, n, g):
                dve.wait_ge(s["sel_ready"], g + 1)
                for t in range(T):
                    last = v.tensor_tensor(SELW[:, t, :].rearrange("p (e s) -> p e s", e=2),
                                           SEL[:, t, :].rearrange("p (e s) -> p e s", e=2),
                                           WGT[:, t, bass.ds(pair * 2, 2)].unsqueeze(2).broadcast_to([P, 2, SLOTS]),
                                           ALU.mult)
                last.then_inc(s["selw_ready"], 1)
                dve.wait_ge(s["selw_ready"], n + 1)
                dve.wait_ge(s["gather_hi"], g + 1)
                select(s, pair + 1, g)
                dve.wait_ge(s["silu_done"], n + 1)
                dve.wait_ge(s["up_done"], n + 1)
                v.tensor_tensor(H, SG, bank[5][:, :], ALU.mult).then_inc(s["h_ready"], 1)
                dve.wait_ge(s["gather_hi"], g + 2)
                v.tensor_copy(XG[:, 4:8, :], bank[7][:, :].rearrange("p (a b) -> p a b", b=P)).then_inc(s["xg_hi"], 1)
                dve.wait_ge(s["y1_done"], n + 1)
                v.tensor_copy(Y[:, 512:1024], bank[7][:, :]).then_inc(s["y1_copied"], 1)

            def moe_layer(l):
                dve.wait_ge(logits_done, l + 1)
                lg = bank[4][:, 0:128].rearrange("p (t f) -> p t f", t=T)[:, :, 0:ROUTE]
                br = ROWS[:, R_BR + l * ROUTE:R_BR + (l + 1) * ROUTE].unsqueeze(1).broadcast_to([P, T, ROUTE])
                link(v.tensor_tensor(LOG[:, :, :], lg, br, ALU.add))

                def first_of(vals, top, width, at, cand, one):
                    bc = top.unsqueeze(2).broadcast_to([P, T, width])
                    io = iota_e[:, 0:width].unsqueeze(1).broadcast_to([P, T, width])
                    link(v.tensor_tensor(cand, vals, bc, ALU.is_equal))
                    link(v.tensor_tensor(cand, cand, io, ALU.mult))
                    link(v.tensor_reduce(at, cand, AX, ALU.min))
                    link(v.tensor_tensor(one, io, at.unsqueeze(2).broadcast_to([P, T, width]), ALU.is_equal))

                lgr = LOG[:, :, 0:GROUPS]
                link(v.tensor_reduce(m1, lgr, AX, ALU.max))
                v.tensor_scalar(gmn, m1, -1.0, None, ALU.mult).then_inc(r_gmax, 1)
                first_of(lgr, m1, GROUPS, i1, ru[:, :, 0:GROUPS], ru[:, :, 4:4 + GROUPS])
                link(v.tensor_scalar(ru[:, :, 4:8], ru[:, :, 4:8], -1.0, -NEG, ALU.add, ALU.mult))
                for t in range(T):
                    last = v.tensor_tensor(ELOG[:, t, :].rearrange("p (g e) -> p g e", g=GROUPS),
                                           LOG[:, t, GROUPS:ROUTE].rearrange("p (g e) -> p g e", g=GROUPS),
                                           ru[:, t, 4:8].unsqueeze(2).broadcast_to([P, GROUPS, PER_GROUP]), ALU.add)
                link(last)
                link(v.tensor_reduce(m1, ELOG[:, :, :], AX, ALU.max))
                first_of(ELOG[:, :, :], m1, EXPERTS, i1, RANK[:, :, 0:EXPERTS], ONE1[:, :, :])
                link(v.scalar_tensor_tensor(ELOG[:, :, :], ONE1[:, :, :], 3 * NEG, ELOG[:, :, :], ALU.mult, ALU.add))
                link(v.tensor_reduce(m2, ELOG[:, :, :], AX, ALU.max))
                v.tensor_tensor(p2, m2, m1, ALU.subtract).then_inc(r_d, 1)
                first_of(ELOG[:, :, :], m2, EXPERTS, i2, RANK[:, :, 0:EXPERTS], ONE2[:, :, :])
                v.tensor_tensor(ELOG[:, :, :], ONE1[:, :, :], ONE2[:, :, :], ALU.add).then_inc(r_one, 1)
                dve.wait_ge(r_gexp, l + 1)
                link(v.reciprocal(gw, gsum))
                dve.wait_ge(r_p2, l + 1)
                link(v.tensor_scalar(g2, p2, 1.0, None, ALU.add))
                link(v.reciprocal(g1, g2))
                link(v.tensor_tensor(g1, g1, gw, ALU.mult))
                link(v.tensor_tensor(g2, g1, p2, ALU.mult))
                link(v.tensor_tensor(ONE1[:, :, :], ONE1[:, :, :], g1.unsqueeze(2).broadcast_to([P, T, EXPERTS]), ALU.mult))
                link(v.tensor_tensor(ONE2[:, :, :], ONE2[:, :, :], g2.unsqueeze(2).broadcast_to([P, T, EXPERTS]), ALU.mult))
                link(v.tensor_tensor(WGT[:, :, 0:EXPERTS], ONE1[:, :, :], ONE2[:, :, :], ALU.add))
                dve.wait_ge(rank_done, l + 1)
                dve.wait_ge(r_one, l + 1)
                rk = bank[4][:, 0:128].rearrange("p (t f) -> p t f", t=T)[:, :, 0:EXPERTS]
                link(v.scalar_tensor_tensor(RANK[:, :, 0:EXPERTS], rk, 1.0, ELOG[:, :, :], ALU.add, ALU.mult))
                link(v.tensor_scalar(RANK[:, :, 0:EXPERTS], RANK[:, :, 0:EXPERTS], -1.0, None, ALU.add))
                v.tensor_reduce(rtop, RANK[:, :, :].rearrange("p t e -> p (t e)"), AX, ALU.max).then_inc(r_top, 1)
                if l:
                    dve.wait_ge(moe["gather_hi"], (PAIRS + 1) * l)
                select(moe, 0, 0)
                dve.wait_ge(top_done, l + 1)
                link(v.tensor_reduce(rtop2[0:1, :], bank[5][0:1, 0:P], AX, ALU.max))
                v.tensor_scalar(FLAG[0:1, l:l + 1], rtop2[0:1, :], SLOTS - 0.5, None, ALU.is_ge).then_inc(flag_ready, 1)
                first_tokens(moe, (PAIRS + 1) * l)
                with dve.Fori(0, PAIRS) as p:
                    experts(moe, p, p + PAIRS * l, p + (PAIRS + 1) * l)
                dve.wait_ge(flag_ready, l + 1)
                more = dve.value_load(FLAG[0:1, l:l + 1], min_val=0, max_val=1)
                with dve.If(more > 0):
                    s = over[l]
                    dve.wait_ge(moe["gather_hi"], (PAIRS + 1) * (l + 1))
                    with dve.Fori(0, ROUNDS_MORE) as r:
                        v.tensor_scalar(RANK[:, :, 0:EXPERTS], RANK[:, :, 0:EXPERTS], float(-SLOTS), None, ALU.add)\
                            .then_inc(over_shift[l], 1)
                        dve.wait_ge(over_shift[l], r + 1)
                        select(s, 0, 0)
                        first_tokens(s, r * (PAIRS + 1))
                        with dve.Fori(0, PAIRS) as p:
                            experts(s, p, r * PAIRS + p, r * (PAIRS + 1) + p)
                dve.wait_ge(acc_done, l + 1)
                layer_norm(add_experts)

            v.memset(RANK[:, :, :], -1.0)
            link(v.memset(WGT[:, :, :], 0.0))
            evac_by_token("x")
            for g, n in enumerate(EIN[0:3]):
                evac_chunk(G_EIN + g, E[:, 1, 512 * n:min(512 * n + 512, EVEN_IN)])
            dve.wait_ge(pj_free[0], 3)
            dve.wait_ge(pj_free[1], 3)
            sq = SQA[:, :, 0:Q_RANK + KV_RANK]
            link(v.tensor_tensor(sq, E[:, :, CQ0:KR0], E[:, :, CQ0:KR0], ALU.mult))
            v.tensor_reduce(var_b[:, :, 0], sq[:, :, 0:Q_RANK], AX, ALU.add)
            link(v.tensor_reduce(var_b[:, :, 1], sq[:, :, Q_RANK:Q_RANK + KV_RANK], AX, ALU.add))
            v.tensor_scalar(var_b[:, :, 0], var_b[:, :, 0], 1.0 / Q_RANK, RMS_EPS, ALU.mult, ALU.add)
            ask_root(v.tensor_scalar(var_b[:, :, 1], var_b[:, :, 1], 1.0 / KV_RANK, RMS_EPS, ALU.mult, ALU.add))
            rope(v, link, E[:, :, 0:1024].rearrange("p t (h f) -> p t h f", f=A_DIM), rot_a, A_HALF, 16, ROT)\
                .then_inc(rope_ready, 1)
            inverse_root(var_b[:, :, :], rs_b[:, :, :])
            for t in range(T):
                v.tensor_scalar(E[:, t, CQ0:CKV0], E[:, t, CQ0:CKV0], rs_b[:, t, 0:1], None, ALU.mult)
                last = v.tensor_scalar(E[:, t, CKV0:KR0], E[:, t, CKV0:KR0], rs_b[:, t, 1:2], None, ALU.mult)
            last.then_inc(rank_ready, 1)
            dve.wait_ge(const_loaded, 48)
            dve.wait_ge(rope_ready, 1)
            lam = ROWS[:, R_LAM:R_LAM + 4 * A_DIM].rearrange("p (a b f) -> p a b f", a=2, b=2)
            lt = ROT[3][:, 0:2 * A_DIM].rearrange("p (a f) -> p a f", a=2)
            link(v.tensor_tensor(lt, lam[:, :, 0, :], lam[:, :, 1, :], ALU.mult))
            v.tensor_reduce(lamv, lt, AX, ALU.add).then_inc(lam_ready, 1)
            evac_chunk(G_EIN + 3, E[:, 1, 1024:1536])
            dve.wait_ge(lam_exp, 1)
            link(v.scalar_tensor_tensor(nlam, lamv[:, 1:2], -LAMBDA_INIT, lamv[:, 0:1], ALU.add, ALU.subtract))
            dve.wait_ge(pj_free[0], 4)
            evac_transposes("qk", lambda b, n: QKT[:, b:b + n, :])
            evac_transposes("c", lambda b, n: CT[:, b, :], blocks=3, gain=lambda b: COLS[:, Q_QN + b:Q_QN + b + 1])
            for n in range(2):
                evac_chunk(G_UQ + n, QB[:, 1, 384 * n:384 * n + 384])
            for n in range(2):
                evac_chunk(G_UKV + n, KV[:, 1, 512 * n:512 * n + 512])
            for i in range(A_HEADS + 2):
                if i < A_HEADS:
                    for m in range(2):
                        dve.wait_ge(d_score, 2 * i + m + 1)
                        ps = bank[4 + 2 * (i % 2) + m][:, :].rearrange("p (t k) -> p t k", t=T)
                        link(v.tensor_reduce(dmx[:, i % 2, m, :], ps, AX, ALU.max))
                        v.tensor_scalar(dnb[:, i % 2, m, :], dmx[:, i % 2, m, :], -(A_DIM ** -0.5), None, ALU.mult)\
                            .then_inc(d_nb, 1)
                if 0 <= i - 1 < A_HEADS:
                    h = i - 1
                    dve.wait_ge(d_exp, 2 * h + 2)
                    s4 = dsm[:, h % 2, :, :]
                    link(v.reciprocal(s4, s4))
                    link(v.tensor_scalar(s4[:, 1, :], s4[:, 1, :], nlam, None, ALU.mult))
                    e0, e1 = PB[2 * (h % 2)], PB[2 * (h % 2) + 1]
                    for t in range(T):
                        last = v.tensor_scalar(e0[:, t, :], e0[:, t, :], s4[:, 0, t:t + 1], None, ALU.mult)
                    link(last)
                    for t in range(T):
                        last = v.scalar_tensor_tensor(e0[:, t, :], e1[:, t, :], s4[:, 1, t:t + 1], e0[:, t, :], ALU.mult, ALU.add)
                    last.then_inc(d_w, 1)
                if i >= 2:
                    h = i - 2
                    dve.wait_ge(d_pv, h + 1)
                    v.tensor_copy(AO[:, :, h * P:(h + 1) * P], bank[2 + h % 2][:, 0:SEQ].rearrange("p (t e) -> p t e", t=T))\
                        .then_inc(d_o, 1)
            dve.wait_ge(d_sq, A_HEADS)
            ask_root(v.tensor_scalar(var_a[:, :, :], var_a[:, :, :], 1.0 / (2 * A_DIM), RMS_EPS, ALU.mult, ALU.add))
            evac_transposes("qb", lambda b, n: QBT[0:B_QK, b:b + n, :], B_QK)
            inverse_root(var_a[:, :, :], rs_a[:, :, :])
            v.tensor_scalar(rs_a[:, :, :], rs_a[:, :, :], 1.0 - LAMBDA_INIT, None, ALU.mult).then_inc(ao_scale, 1)
            evac_transposes("kb", lambda b, n: KBT[0:B_QK, b:b + n, :], B_QK)
            attention(N_MLA0, B_HEADS, PB, lambda pair: MT[:, 4 + pair, :], B_QK ** -0.5, None)
            evac_transposes("ao", lambda b, n: MT[:, b:b + n, :])
            layer_norm(lambda t: add_out(G_EO, t, ALPHA))
            evac_by_token("ln0")
            moe_layer(0)
            evac_by_token("ln1")
            for n in range(4):
                evac_chunk(G_QKV + n, (OQ if n < 2 else OK)[:, 4 * (n % 2) + 2:4 * (n % 2) + 4, :])
            for n in range(2):
                evac_chunk(G_QKV + 4 + n, OV[:, 1, 512 * n:512 * n + 512])
            dve.wait_ge(bias_loaded, 16)
            attention(N_NA0, C_HEADS, PN, lambda pair: MT[:, pair, :], C_DIM ** -0.5,
                      lambda h, t: G[:, h, (2 - 2 * t) * GRID_W:(2 - 2 * t) * GRID_W + SEQ])
            layer_norm(lambda t: add_out(G_OO, t, ALPHA))
            evac_by_token("ln2")
            moe_layer(1)
            for t in range(T):
                normed(t, XN)
            ll = COLS[:, Q_LAM:Q_LAM + LRU_T]
            link(v.tensor_scalar(spl[0], ll, -1.0, 0.0, ALU.mult, ALU.max))
            link(v.tensor_scalar(spl[1], ll, -1.0, None, ALU.mult))
            v.tensor_tensor(spl[1], spl[1], ll, ALU.min).then_inc(sp_in, 1)
            v.tensor_scalar(spl[3], COLS[:, Q_BA:Q_BA + LRU_T], 0.5, None, ALU.mult)
            v.tensor_scalar(spl[4], COLS[:, Q_BX:Q_BX + LRU_T], 0.5, None, ALU.mult).then_inc(sp_in, 1)
            evac_by_token("n1", Q_N1)
            evac_chunk(G_IN2, XL[:, 2:4, :])
            dve.wait_ge(pj_free[0], G_IN2 + 1)
            dve.wait_ge(pj_free[1], G_IN2 + 1)

            def tap(j, c):
                return COLS[:, Q_CW + j * LRU_T + c:Q_CW + j * LRU_T + c + 1]

            for c in range(LRU_T):
                last = v.tensor_scalar(LX[:, c, :], XL[:, c, :], tap(3, c), COLS[:, Q_CB + c:Q_CB + c + 1], ALU.mult, ALU.add)
            link(last)
            for j in range(1, LRU_CONV):
                for c in range(LRU_T):
                    last = v.scalar_tensor_tensor(LX[:, c, j:SEQ], XL[:, c, 0:SEQ - j], tap(3 - j, c), LX[:, c, j:SEQ],
                                                  ALU.mult, ALU.add)
                    if j == LRU_CONV - 1:
                        last.then_inc(lru_cvd, 1)
                if j < LRU_CONV - 1:
                    link(last)
            dve.wait_ge(sp_exp, 1)
            link(v.tensor_scalar(spl[2], spl[1], 2.0, None, ALU.add))
            link(v.reciprocal(spl[2], spl[2]))
            link(v.tensor_tensor(spl[1], spl[1], spl[2], ALU.mult))
            link(v.tensor_tensor(spl[2], spl[1], spl[1], ALU.mult))
            ser = spl_series
            link(v.tensor_scalar(ser, spl[2], 1.0 / 19, 1.0 / 17, ALU.mult, ALU.add))
            for k in (15, 13, 11, 9, 7, 5, 3, 1):
                link(v.tensor_tensor(ser, ser, spl[2], ALU.mult))
                link(v.tensor_scalar(ser, ser, 1.0 / k, None, ALU.add))
            link(v.tensor_tensor(ser, ser, spl[1], ALU.mult))
            link(v.scalar_tensor_tensor(spl[0], ser, 2.0, spl[0], ALU.mult, ALU.add))
            link(v.tensor_scalar(spl[0], spl[0], -4.0, None, ALU.mult))
            def evac_2(n):
                evac_chunk(G_IN2 + n, TOK[:, 1, 512 * (n - 2):512 * (n - 1)])

            dve.wait_ge(pj_free[1], G_IN2 + 2)
            evac_2(2)
            dve.wait_ge(lru_g, LRU_T)
            for c in range(LRU_T):
                last = v.tensor_scalar(LA[:, c, :], LA[:, c, :], 1.0, spl[0][:, c:c + 1], ALU.add, ALU.mult)
            last.then_inc(lru_t, 1)
            link(v.tensor_scalar(LI[:, :, :], LI[:, :, :], 0.5, 0.5, ALU.mult, ALU.add))
            link(v.tensor_tensor(LI[:, :, :], LI[:, :, :], LX[:, :, :], ALU.mult))
            dve.wait_ge(lru_a, 1)
            link(v.tensor_scalar(XL[:, :, :], LT_[:, :, :], 1.0, None, ALU.add))
            link(v.reciprocal(XL[:, :, :], XL[:, :, :]))
            ask_root(v.scalar_tensor_tensor(LT_[:, :, :], LT_[:, :, :], 2.0, XL[:, :, :], ALU.mult, ALU.mult))
            evac_2(3)
            dve.wait_ge(pj_free[0], G_IN2 + 4)
            dve.wait_ge(pj_free[1], G_IN2 + 4)
            dve.wait_ge(table2_loaded, 32)
            rope(v, link, TOK[:, :, 0:1024].rearrange("p t (h f) -> p t h f", f=RET_DIM), rot_c, RET_DIM // 2, 8, ROT2)\
                .then_inc(r_rope, 1)
            dve.wait_ge(std_ready, roots[0])
            link(v.tensor_tensor(LI[:, :, :], LI[:, :, :], LT_[:, :, :], ALU.mult))
            dve.wait_ge(lru_a, 2)
            for c in range(LRU_T):
                last = v.tensor_tensor_scan(LX[:, c, :], LA[:, c, :], LI[:, c, :], 0.0, ALU.mult, ALU.add)
            link(last)
            evac_2(4)
            link(v.tensor_tensor(LX[:, :, :], LX[:, :, :], GL[:, :, :], ALU.mult))
            v.tensor_tensor(LT_[:, :, :], LX[:, :, :], LX[:, :, :], ALU.mult).then_inc(lru_sq, 1)
            evac_transposes("rqk", lambda b, n: RQK[:, b:b + n, :])
            evac_2(5)
            for h in range(RET_HEADS):
                dve.wait_ge(r_sc, h + 1)
                v.tensor_tensor(RS[:, h, :], bank[4 + h][:, 0:DEC_W], KT2[:, L_DEC + h * DEC_W:L_DEC + (h + 1) * DEC_W],
                                ALU.mult).then_inc(r_scd, 1)
            dve.wait_ge(lru_sqr, 1)
            ask_root(v.tensor_scalar(LI[:, 0, :], bank[2][:, 0:SEQ], 1.0 / LRU, RMS_EPS, ALU.mult, ALU.add))
            for h in range(RET_HEADS):
                dve.wait_ge(r_o, h + 1)
                v.tensor_copy(YR[:, :, h * P:(h + 1) * P], bank[h % 2][:, 0:SEQ].rearrange("p (t e) -> p t e", t=T))\
                    .then_inc(r_oc, 1)
            inverse_root(LI[:, 0, :], LI[:, 1, :])
            for c in range(LRU_T):
                last = v.scalar_tensor_tensor(MT[:, c, :], LX[:, c, :], COLS[:, Q_LN + c:Q_LN + c + 1], LI[:, 1, :],
                                              ALU.mult, ALU.mult)
            last.then_inc(lru_y, 1)
            dve.wait_ge(r_oc, RET_HEADS)
            for t in range(T):
                for h in range(RET_HEADS):
                    last = v.bn_stats(hst[:, t, h, :], YR[:, t, h * P:(h + 1) * P])
            link(last)
            for t in range(T):
                for h in range(RET_HEADS):
                    last = v.bn_aggr(hmv[:, t, h, :], hst[:, t, h, :])
            link(last)
            ask_root(v.tensor_scalar(var_h[:, :, :], hmv[:, :, :, 1], RMS_EPS, None, ALU.add))
            inverse_root(var_h[:, :, :], rs_h[:, :, :])
            for t in range(T):
                for h in range(RET_HEADS):
                    last = v.tensor_scalar(YR[:, t, h * P:(h + 1) * P], YR[:, t, h * P:(h + 1) * P], hmv[:, t, h, 0:1],
                                           rs_h[:, t, h:h + 1], ALU.subtract, ALU.mult)
            link(last)
            dve.wait_ge(ln_loaded, 16 * 5)
            for t in range(T):
                last = v.tensor_tensor(YR[:, t, :], YR[:, t, :], LNR[:, 0, 0:RET_HEADS * RET_DIM], ALU.mult)
            link(last)
            dve.wait_ge(r_silu, 1)
            for t in range(T):
                last = v.tensor_tensor(YR[:, t, :], YR[:, t, :], TOK[:, t, 1536:2048], ALU.mult)
            last.then_inc(r_y, 1)
            evac_transposes("yr", lambda b, n: MT[:, 4 + b:4 + b + n, :])
            for t in range(T):
                add_out(G_OUT2, t, 1.0)
                normed(t, XN2)
            evac_by_token("n2", Q_N2)
            for f in range(FF2_T):
                dve.wait_ge(f_cv0, f + 1)
                for j in (1, 2):
                    wj = COLS[:, Q_FW + (2 - j) * FF2_T + f:Q_FW + (2 - j) * FF2_T + f + 1]
                    ins = v.scalar_tensor_tensor(CV[f % 4][:, j:SEQ], bank[f % 4][:, 0:SEQ - j], wj, CV[f % 4][:, j:SEQ],
                                                 ALU.mult, ALU.add)
                    if j == 1:
                        link(ins)
                    else:
                        ins.then_inc(f_cv, 1)
                if f >= DOWN_T:
                    g = f - DOWN_T
                    dve.wait_ge(f_gelu, g + 1)
                    dve.wait_ge(f_cv, f + 1)
                    v.tensor_tensor(ACTT[:, g, :], ACTT[:, g, :], CV[f % 4], ALU.mult).then_inc(f_act, 1)
            dve.wait_ge(ln_loaded, 16 * 6)
            for t in range(T):
                dve.wait_ge(f_down, t + 1)
                for h in range(2):
                    xs = X[:, t, 512 * h:512 * h + 512]
                    last = v.tensor_tensor(xs, xs, bank[4 + 2 * t + h][:, :], ALU.add)
                link(last)
                token_rms(t, XN2)
                v.scalar_tensor_tensor(X[:, t, :], X[:, t, :], rs_l[:, t:t + 1], LNR[:, 0, :], ALU.mult, ALU.mult)\
                    .then_inc(out_ready, 1)


def lay_out(i):
    table, table2 = shape_constants()

    def feature_columns(a):
        a = a.reshape(-1, a.shape[-1] // P, P)
        return a.transpose(2, 0, 1).reshape(P, -1)

    cols = np.concatenate([feature_columns(a) for a in (
        i["norm1_gain_2"], i["lru_conv_w_2"][0], i["lru_conv_b_2"], i["lru_gate_a_b_2"], i["lru_gate_x_b_2"],
        i["lru_lambda_2"], i["lru_norm_gain_2"], i["norm2_gain_2"], i["ffn_conv_w_2"][0], i["ffn_conv_b_2"],
        i["even_q_norm_g"], i["even_kv_norm_g"])], 1)
    rows = np.concatenate([i["even_subln_g"][0], i["even_lam_q1"][0], i["even_lam_k1"][0], i["even_lam_q2"][0],
                           i["even_lam_k2"][0]] +
                          [a for l in range(DEPTH) for a in (i["b_router_group"][l], i["b_router_expert"][l])])[None]
    ln_rows = np.zeros((6, 2 * D), np.float32)
    for l in range(DEPTH):
        for n, name in enumerate(("ln1", "ln2")):
            ln_rows[2 * l + n, :D] = i[f"{name}_g"][l]
            ln_rows[2 * l + n, D:] = i[f"{name}_b"][l]
    ln_rows[4, :RET_HEADS * RET_DIM] = i["ret_norm_gain_2"][0]
    ln_rows[5, :D] = i["final_norm_gain_2"]
    route = np.concatenate([i["w_router_group"], i["w_router_expert"]], 2)
    route = route.reshape(DEPTH, C, P, ROUTE).transpose(2, 0, 1, 3)
    rr, cc, m, j = np.meshgrid(np.arange(2), np.arange(GRID_W), np.arange(BIAS_ROWS), np.arange(GRID_W), indexing="ij")
    start = np.clip(cc - NA_COLS // 2, 0, GRID_W - NA_COLS)
    inside = (j >= start) & (j < start + NA_COLS)
    col = np.clip(j - cc + NA_COLS - 1, 0, 2 * NA_COLS - 2)
    bias = i["odd_rel_bias"][0][:, m + 5 - rr, col]
    bias = np.where(inside[None], bias, np.float32(NEG))
    bias = bias.transpose(1, 2, 0, 3, 4).reshape(P, C_HEADS, BIAS_ROWS * GRID_W)
    gates = np.zeros((P, 2, LRU_T, P), np.float32)
    for n, name in enumerate(("lru_gate_a_w_2", "lru_gate_x_w_2")):
        for h in range(8):
            o = h % 2 * 64
            gates[o:o + 64, n, h // 2, o:o + 64] = i[name][0, h]
    return {
        "x": i["x"][0], "w_in": i["even_w_in"][0], "w_uq": i["even_w_uq"][0], "w_ukv": i["even_w_ukv"][0],
        "w_o": i["even_w_o"][0], "w_qkv": i["odd_w_qkv"][0], "na_bias": bias, "w_o2": i["odd_w_o"][0],
        "ln_rows": ln_rows, "rows": rows, "cols": cols, "w_route": route, "w_gate": i["w_gate"], "w_up": i["w_up"],
        "w_down": i["w_down"], "w_in2": i["w_in_2"][0], "gates": gates.reshape(P, 2, LRU_T * P),
        "w_out2": i["w_out_2"][0], "ffn_up": i["ffn_up_w_2"][0], "ffn_down": i["ffn_down_w_2"][0],
        "table": table, "table2": table2,
    }


def kernel(**inputs):
    import concourse.bacc as bacc
    from concourse.bass_utils import run_bass_kernel_spmd

    laid = lay_out({k: np.asarray(a) for k, a in inputs.items()})
    nc = bacc.Bacc("TRN2", target_bir_lowering=False, num_devices=1)
    arrays, args = {}, []
    for name, a in laid.items():
        a = np.ascontiguousarray(a)
        arrays[f"in_{name}"] = a
        args.append(nc.dram_tensor(f"in_{name}", a.shape, mybir.dt.from_np(a.dtype), kind="ExternalInput").ap())
    out = nc.dram_tensor("out", (SEQ, D), F32, kind="ExternalOutput").ap()
    bass_two_blocks(nc, *args, out)
    r = run_bass_kernel_spmd(nc, [arrays], core_ids=[0])
    return np.asarray(r.results[0]["out"]).reshape(1, SEQ, D)
```

```python
import math
from contextlib import ExitStack

import numpy as np
import concourse.bass as bass
from concourse import mybir

F32 = mybir.dt.float32
F32R = mybir.dt.float32r
I32 = mybir.dt.int32
ALU = mybir.AluOpType
ACT = mybir.ActivationFunctionType
AX = mybir.AxisListType.X

P = 128
SEQ, D = 256, 1024
T = SEQ // P
C = D // P
DEPTH = 2
ALPHA = (2 * DEPTH) ** 0.25
LN_EPS, RMS_EPS = 1e-5, 1e-6
NEG = -1e30

A_HEADS, A_DIM = 4, 64
A_HALF = A_DIM // 4 // 2
LAMBDA_INIT = 0.8 - 0.6 * math.exp(-0.3 * 0)
B_HEADS, B_NOPE, B_ROPE, B_V = 8, 64, 32, 64
B_QK = B_NOPE + B_ROPE
B_HALF = B_ROPE // 2
Q_RANK, KV_RANK = 256, 128
VA0 = 1024
CQ0, CKV0, KR0, EVEN_IN = 1536, 1792, 1920, 1952
C_HEADS, C_DIM = 16, 64
GRID_W, NA_COLS = 64, 16
GRID_R = SEQ // GRID_W
BIAS_ROWS = 6
GROUPS, PER_GROUP, EXPERTS, FE = 4, 8, 32, 512
SLOTS = 64
PAIRS = EXPERTS // 2
ROUNDS_MORE = SEQ // SLOTS - 1
ROUTE = GROUPS + EXPERTS
LRU, LRU_T, LRU_CONV = 512, 4, 4
RET_HEADS, RET_DIM = 4, 128
FF2, FF2_T, FF_CONV = 6144, 48, 3
DOWN_T = FF2_T // 2
TILES = 4
WBUF = 3
EARLY_A = FF2_T - 8

RING = 6
EARLY = 4
AHEAD = 5
POOL = RING + EARLY
SLOT = 4096


def shape_constants():
    f = np.float32

    def rotation(theta, rot):
        inv = f(theta) ** (-np.arange(0, rot, 2, dtype=f) / f(rot))
        ang = np.arange(SEQ, dtype=f)[:, None] * inv[None].astype(f)
        both = np.stack([np.cos(ang), np.sin(ang)]).astype(f)
        return both.reshape(2, T, P, -1).transpose(2, 0, 1, 3).reshape(P, -1)

    first = [
        np.eye(P, dtype=f),
        np.triu(np.ones((P, P), f), 1),
        np.ones((P, P), f),
        np.zeros((P, P), f),
        np.tile(np.arange(SLOTS, dtype=f), (P, 1)),
        np.tile(np.arange(EXPERTS, dtype=f) - 64, (P, 1)),
        rotation(500000.0, 2 * A_HALF),
        rotation(500000.0, B_ROPE),
    ]
    log_g = np.log1p(-np.exp2(-5.0 - np.arange(RET_HEADS, dtype=np.float64)))
    diff = np.arange(SEQ)[None] - np.arange(P)[:, None]
    decay = np.where(diff >= 0, np.exp(np.maximum(diff, 0) * log_g[:, None, None]), 0.0) * RET_DIM ** -0.5
    decay = np.concatenate([decay, decay[:, :, :P]], axis=2)
    later = [rotation(10000.0, RET_DIM), decay.transpose(1, 0, 2).reshape(P, -1).astype(f)]
    return np.concatenate(first, 1).astype(f), np.concatenate(later, 1).astype(f)


K_ID, K_LT, K_ONE, K_ZERO, K_IO = 0, 128, 256, 384, 512
K_IE = K_IO + SLOTS
K_RA = K_IE + EXPERTS
K_RB = K_RA + 2 * T * A_HALF
K_W = K_RB + 2 * T * B_HALF
L_ROT, L_DEC = 0, 2 * T * (RET_DIM // 2)
DEC_W = SEQ + P
L_W = L_DEC + RET_HEADS * DEC_W
R_SUB, R_LAM, R_BR = 0, 128, 128 + 256
R_W = R_BR + DEPTH * ROUTE
Q_N1, Q_CW, Q_CB, Q_BA, Q_BX, Q_LAM, Q_LN, Q_N2 = 0, 8, 24, 28, 32, 36, 40, 44
Q_FW, Q_FB = 52, 52 + FF_CONV * FF2_T
Q_QN = Q_FB + FF2_T
Q_KVN = Q_QN + 2
Q_W = Q_KVN + 1


def bass_two_blocks(nc, x, w_in, w_uq, w_ukv, w_o, w_qkv, na_bias, w_o2, ln_rows, rows, cols, w_route,
                    w_gate, w_up, w_down, w_in2, gates, w_out2, ffn_up, ffn_down, table, table2, out):
    with ExitStack() as ctx:
        def sb(name, shape, dt=F32):
            return ctx.enter_context(nc.sbuf_tensor(name, shape, dt))

        def sem(name):
            return ctx.enter_context(nc.semaphore(name))

        offset = {}

        def placed(name, shape):
            buffer = sb(name, shape)
            offset[name] = nc.sbuf_base - 4 * int(np.prod(shape[1:]))
            return buffer

        def part(name, over, at, shape):
            return nc.alloc_sbuf_tensor_at(name, shape, F32R, offset=offset[over] + 4 * at)

        ring = placed("ring", [P, RING, SLOT])
        ARENA_W = 16896
        arena = placed("arena", [P, ARENA_W])
        X = sb("X", [P, T, D])
        XT = placed("XT", [P, C, SEQ])
        MT = placed("MT", [P, C, SEQ])
        LNR = sb("LNR", [P, 2, D])
        KT = sb("KT", [P, K_W])
        ROWS = sb("ROWS", [P, R_W])
        COLS = sb("COLS", [P, Q_W])
        WR = sb("WR", [P, DEPTH, C, ROUTE])
        ST = sb("ST", [P, 512])
        FLAG = sb("FLAG", [1, DEPTH], I32)
        bank = [ctx.enter_context(nc.psum_tensor(f"bank{i}", [P, 512], F32)) for i in range(8)]

        def cut(off, *shape):
            n = int(np.prod(shape))
            assert off + n <= ARENA_W, (off, shape)
            v = arena[:, off:off + n]
            if len(shape) == 2:
                v = v.rearrange("p (a b) -> p a b", b=shape[1])
            if len(shape) == 3:
                v = v.rearrange("p (a b c) -> p a b c", b=shape[1], c=shape[2])
            return v

        stat_at = [0]

        def stat(*shape):
            n = int(np.prod(shape))
            v = ST[:, stat_at[0]:stat_at[0] + n]
            stat_at[0] += n
            assert stat_at[0] <= 512
            if len(shape) == 2:
                v = v.rearrange("p (a b) -> p a b", b=shape[1])
            if len(shape) == 3:
                v = v.rearrange("p (a b c) -> p a b c", b=shape[1], c=shape[2])
            return v

        ident, earlier = KT[:, K_ID:K_ID + P], KT[:, K_LT:K_LT + P]
        ones, zeros = KT[:, K_ONE:K_ONE + P], KT[:, K_ZERO:K_ZERO + P]
        iota_s, iota_e = KT[:, K_IO:K_IO + SLOTS], KT[:, K_IE:K_IE + EXPERTS]
        rot_a = KT[:, K_RA:K_RB].rearrange("p (s t f) -> p s t f", s=2, t=T)
        rot_b = KT[:, K_RB:K_W].rearrange("p (s t f) -> p s t f", s=2, t=T)

        E = cut(0, T, EVEN_IN)
        QKT = cut(3904, C, SEQ)
        QBT, KBT = QKT, XT
        PB = [cut(5952 + 512 * i, T, SEQ) for i in range(4)]
        ROT = [cut(5952 + 512 * i, 512) for i in range(4)]
        PT = [cut(8000 + 512 * i, T, SEQ) for i in range(2)]
        QB = cut(9024, T, B_HEADS * B_QK)
        KV = cut(10560, T, B_HEADS * (B_NOPE + B_V))
        KC = E[:, :, 0:B_HEADS * B_QK]
        CT = cut(12608, 3, SEQ)
        AO = cut(13376, T, A_HEADS * 2 * A_DIM)
        SQA = cut(14400, T, A_HEADS * 2 * A_DIM)
        ROTB = [cut(15424 + B_HEADS * B_HALF * i, B_HEADS * B_HALF) for i in range(4)]
        SEL = cut(0, T, 2 * SLOTS)
        SELW = cut(256, T, 2 * SLOTS)
        SWT = cut(512, T, P)
        XG = cut(768, C, 2 * SLOTS)
        SG = cut(1792, FE)
        H = cut(2304, FE)
        HT = cut(2816, FE // P, 2 * SLOTS)
        Y = cut(3328, D)
        FIRST = [cut(4352 + SLOT * i, SLOT) for i in range(EARLY - 1)]
        FIRST.append(nc.alloc_sbuf_tensor_at("first_over_features", [P, SLOT], F32, offset=offset["XT"])[:, :])
        assert offset["MT"] == offset["XT"] + 4 * C * SEQ and SLOT == 2 * C * SEQ
        G = cut(4352, C_HEADS, BIAS_ROWS * GRID_W)
        OQ, OK, OV = cut(10496, C, SEQ), cut(12544, C, SEQ), cut(14592, T, D)
        PN = [cut(512 * i, T, SEQ) for i in range(4)]
        PTN = [cut(2048 + 512 * i, T, SEQ) for i in range(2)]
        XL, GL, LX, LA = (cut(1024 * i, LRU_T, SEQ) for i in range(4))
        KT2 = cut(4352, L_W)
        rot_c = KT2[:, L_ROT:L_DEC].rearrange("p (s t f) -> p s t f", s=2, t=T)
        GATE = cut(6144, 2, LRU_T * P)
        LI, LT_ = cut(7168, LRU_T, SEQ), cut(8192, LRU_T, SEQ)
        TOK = cut(9216, T, 4 * RET_HEADS * RET_DIM)
        RQK = cut(13312, C, SEQ)
        ROT2 = [cut(13312 + 512 * i, 512) for i in range(4)]
        RS = cut(15360, RET_HEADS, DEC_W)
        YR = TOK[:, :, 0:RET_HEADS * RET_DIM]
        ACTT = cut(0, DOWN_T, SEQ)
        CV = [cut(12288 + 256 * i, SEQ) for i in range(4)]
        XN = cut(0, T, D)
        WHI = [part(f"w_high{i}", "arena", 6144 + 2048 * i, [P, C, P]) for i in range(WBUF)]
        WLO = [part(f"w_low{i}", "arena", 7168 + 2048 * i, [P, C, P]) for i in range(WBUF)]
        AHI = [part(f"act_high{i}", "arena", 15360 + 512 * i, [P, SEQ]) for i in range(WBUF)]
        ALO = [part(f"act_low{i}", "arena", 15616 + 512 * i, [P, SEQ]) for i in range(WBUF)]
        XHI, XLO = part("x_high", "MT", 0, [P, C, SEQ]), part("x_low", "XT", 0, [P, C, SEQ])

        mx, nb, sm = stat(4, T), stat(4, T), stat(4, T)
        dmx, dnb, dsm = stat(2, 2, T), stat(2, 2, T), stat(2, 2, T)
        lamv, nlam = stat(2), stat(1)
        var_b, rs_b = stat(T, 2), stat(T, 2)
        var_a, rs_a = stat(T, A_HEADS), stat(T, A_HEADS)
        bst, mv = stat(T, 2, 6), stat(T, 2)
        var_l, rs_l = stat(T), stat(T)
        rg, ru = stat(T, 8), stat(T, 8)
        gmn, gsum, gw = stat(T), stat(T), stat(T)
        m1, m2, i1, i2, p2, g1, g2 = (stat(T) for _ in range(7))
        rtop, rtop2 = stat(1), stat(1)
        hst, hmv = stat(T, RET_HEADS, 6), stat(T, RET_HEADS, 2)
        var_h, rs_h = stat(T, RET_HEADS), stat(T, RET_HEADS)
        spl = [stat(LRU_T) for _ in range(5)]
        spl_series = stat(LRU_T)
        LOG = sb("LOG", [P, T, ROUTE])
        ONE1, ONE2, ELOG = sb("ONE1", [P, T, EXPERTS]), sb("ONE2", [P, T, EXPERTS]), sb("ELOG", [P, T, EXPERTS])
        RANK, WGT = sb("RANK", [P, T, EXPERTS + 2]), sb("WGT", [P, T, EXPERTS + 2])

        x_loaded, const_loaded, table2_loaded, bias_loaded = (sem(n) for n in (
            "x_loaded", "const_loaded", "table2_loaded", "bias_loaded"))
        early_loaded = [sem(f"early_loaded{i}") for i in range(EARLY)]
        ln_loaded = sem("ln_loaded")
        slot_loaded = [sem(f"slot_loaded{i}") for i in range(RING)]
        x_ready, xn_ready = sem("x_ready"), sem("xn_ready")
        dve_step = sem("dve_step")
        tr_done, tr_act, tr_dve = sem("tr_done"), sem("tr_act"), sem("tr_dve")
        pj_done, pj_free = sem("pj_done"), [sem("pj_free0"), sem("pj_free1")]
        var_ready, std_ready = sem("var_ready"), sem("std_ready")
        rope_ready, rank_ready, mla_ready, lam_ready, lam_exp = (sem(n) for n in (
            "rope_ready", "rank_normed", "mla_ready", "lam_ready", "lam_exp"))
        d_score, d_nb, d_exp, d_w, d_pt, d_ptc, d_pv, d_o = (sem(n) for n in (
            "d_score_done", "d_nb_ready", "d_exp_done", "d_w_ready", "d_pT_done", "d_pT_copied", "d_pv_done",
            "d_o_copied"))
        d_sq, ao_scale, ao_ready, pool_step, a_rec, a_p0 = (sem(n) for n in (
            "d_squares_done", "ao_scale_ready", "ao_ready", "pool_step", "reciprocal_ready", "prob0_ready"))
        a_score, a_free, a_nb, a_exp, a_p, a_pt, a_ptc, a_pv, a_o = (sem(n) for n in (
            "score_done", "score_free", "nb_ready", "exp_done", "prob_ready", "pT_done", "pT_copied", "pv_done",
            "o_copied"))
        logits_done, r_gmax, r_gexp, r_d, r_p2, r_one, rank_done, r_top, top_done, flag_ready, route_ready = (
            sem(n) for n in ("logits_done", "group_max", "group_exp", "top_gap", "second_exp", "chosen_ready",
                             "rank_done", "rank_top", "top_done", "flag_ready", "route_ready"))

        def signals(tag):
            return {n: sem(f"{tag}_{n}") for n in (
                "sel_ready", "selw_ready", "gather_lo", "gather_hi", "xg_lo", "xg_hi", "gate_done", "up_done",
                          "silu_done", "h_ready", "hT_done", "hT_copied", "swt_done", "swt_copied", "y0_done",
                          "y1_done", "y0_copied", "y1_copied")}

        moe = signals("moe")
        over = [signals(f"over{l}") for l in range(DEPTH)]
        over_loaded = [sem(f"over{l}_loaded") for l in range(DEPTH)]
        over_free = [sem(f"over{l}_slots_free") for l in range(DEPTH)]
        over_shift = [sem(f"over{l}_shifted") for l in range(DEPTH)]
        acc_done = sem("acc_done")
        lru_cvd, lru_gm, lru_g, lru_t, lru_a, lru_sq, lru_sqr, lru_y = (sem(n) for n in (
            "lru_conv", "lru_gate_mm", "lru_gates", "lru_tanh", "lru_decay", 
            "lru_squares", "lru_sum", "lru_out"))
        sp_exp, sp_in = sem("softplus_exp"), sem("softplus_in")
        r_rope, r_sc, r_scd, r_o, r_oc, r_y, r_silu, r_gain = (sem(n) for n in (
            "ret_rope", "ret_score", "ret_decayed", "ret_out", "ret_out_copied", "ret_y", "ret_silu", "ret_gate_gain"))
        x_hi, x_lo, w_hi, w_lo, w_used, a_hi, a_lo = (sem(n) for n in (
            "x_high_ready", "x_low_ready", "w_high_ready", "w_low_ready", "w_used", "act_high_ready", "act_low_ready"))
        f_cv0, f_cv, f_act, f_gelu = (sem(n) for n in (
            "ffn_conv0", "ffn_conv", "ffn_act", "ffn_gelu"))
        out_ready, stored = sem("out_ready"), sem("stored")

        def columns(w, n, width=512):
            return w[:, n * 512:n * 512 + width].rearrange("(c p) f -> p c f", p=P)

        def slot(i, a, b):
            return ring[:, i % RING, 0:a * b].rearrange("p (a b) -> p a b", b=b)

        unloaded = []
        items = []

        def item(src, a, b, used, value):
            items.append((src, slot(len(items), a, b), used, value))
            return len(items) - 1

        def hole(used, value):
            unloaded.append(len(items))
            items.append((None, None, used, value))
            return len(items) - 1

        def split_buffers(name, holes):
            at = [holes[b // 2] % RING * SLOT + b % 2 * 2048 for b in range(TILES)]
            return [tuple(part(f"{name}_{half}{b}", "ring", at[b] + n * 1024, [P, C // TILES, 512])
                          for n, half in enumerate(("high", "low"))) for b in range(TILES)]

        G_EIN, G_UQ, G_UKV, G_EO, G_QKV, G_OO, G_IN2, G_OUT2 = 0, 4, 6, 8, 10, 16, 18, 24
        EIN = [0, 1, 3, 2]
        I_EIN = [item(columns(w_in, n, min(512, EVEN_IN - 512 * n)), C, min(512, EVEN_IN - 512 * n), pj_done,
                      2 * g + 2) for g, n in enumerate(EIN)]
        I_UQ = item(w_uq.rearrange("(c p) f -> p c f", p=P), 2, 768, pj_done, 2 * G_UKV)
        I_UKV = item(w_ukv.rearrange("(c p) f -> p c f", p=P), 1, 1024, pj_done, 2 * G_EO)

        def out_items(w, g):
            return [item(columns(w, n), C, 512, pj_done, 2 * g + 3 + n) for n in range(2)]

        I_EO = out_items(w_o, G_EO)

        def expert_source(l, e, k):
            if k < 2:
                return w_gate[l, bass.ds(e, 1)].rearrange("o (c p) f -> p (o c) f", p=P)
            if k < 4:
                return w_up[l, bass.ds(e, 1)].rearrange("o (c p) f -> p (o c) f", p=P)
            return w_down[l, bass.ds(e, 1)].rearrange("o (j p) f -> p (o j) f", p=P)

        def as_expert(v, k):
            return v.rearrange("p (a b) -> p a b", b=FE if k < 4 else D)

        def expert_used(l, n):
            return (moe["gate_done"], moe["up_done"], moe["y1_done"])[n % 6 // 2], PAIRS * l + n // 6 + 1

        def expert_items(l):
            first = len(items)
            for n in range(6 * PAIRS):
                if n >= 6 * AHEAD or n % POOL < RING:
                    items.append((None, None, *expert_used(l, n)))
            return first

        I_MOE = [expert_items(0)]
        QKV, IN2 = [4, 0, 1, 2, 3, 5], [5, 0, 1, 2, 3, 4]
        def split_items(w, order, k0, g_end):
            first, its = len(items), []
            for g, n in enumerate(order):
                if g % (RING - 2) == 0:
                    for _ in range(2):
                        hole(pj_done, 2 * g_end)
                its.append(item(columns(w, n), C, 512, w_lo, k0 + TILES * (g + 1)))
            return (first, first + 1), its

        holes, I_QKV = split_items(w_qkv, QKV, 0, G_OO)
        S_QKV = dict(g0=G_QKV, items=I_QKV, bufs=split_buffers("qkv", holes), k0=0, u0=0, x0=0, free=(acc_done, 1))
        I_OO = out_items(w_o2, G_OO)
        I_MOE.append(expert_items(1))
        K_IN2, U_IN2 = 6 * TILES, 6 * (TILES - 1)
        holes, I_IN2 = split_items(w_in2, IN2, K_IN2, G_OUT2)
        S_IN2 = dict(g0=G_IN2, items=I_IN2, bufs=split_buffers("in2", holes), k0=K_IN2, u0=U_IN2, x0=T,
                     free=(acc_done, 2))
        K_FFN, U_FFN, X_FFN = 2 * K_IN2, 2 * U_IN2, 2 * T
        I_OUT2 = out_items(w_out2, G_OUT2)
        I_UP = [item(columns(ffn_up, n), C, 512, w_lo, K_FFN + 4 * n + 4) for n in range(FF2 // 512)]
        I_DN = [item(ffn_down[512 * n:512 * (n + 1), :].rearrange("(c p) f -> p c f", p=P), 4, D, w_lo, K_FFN + FF2_T + 4 * n + 4)
                for n in range(6)]

        def ffn_weights(k):
            if k < FF2_T:
                return I_UP[k // 4], slot(I_UP[k // 4], C, 512)[:, :, k % 4 * P:(k % 4 + 1) * P]
            i = I_DN[(k - FF2_T) // 4]
            return i, slot(i, 4, D)[:, k % 4, :].rearrange("p (a b) -> p a b", b=P)

        def ring_item(l, k):
            return I_MOE[l] + k

        def after_turns(l, k):
            return ring_item(l, k) + 6 * AHEAD // POOL * RING

        def loads(i):
            return len([j for j in range(i % RING, i + 1, RING) if j not in unloaded])

        def arrived(i):
            return slot_loaded[i % RING], 16 * loads(i)

        def split_tile(s, k):
            i = s["items"][k // TILES]
            rows_ = C // TILES
            return i, slot(i, C, 512)[:, k % TILES * rows_:(k % TILES + 1) * rows_, :], s["bufs"][k % TILES]

        def split_used(s, k):
            if k % TILES == TILES - 1:
                return pj_done, 2 * (s["g0"] + k // TILES) + 2
            return w_used, s["u0"] + k // TILES * (TILES - 1) + k % TILES + 1

        TR = {}
        tr_groups = 0
        for name, groups in (("x", 4), ("qk", 4), ("c", 2), ("qb", 4), ("kb", 4), ("ao", 2), ("ln0", 4), ("ln1", 4),
                             ("ln2", 4), ("n1", 4), ("rqk", 4), ("yr", 2), ("n2", 4)):
            TR[name] = (tr_groups, groups)
            tr_groups += groups

        N_MLA0, N_NA0 = 0, B_HEADS

        def counted(eng, steps):
            n = [0]

            def link(ins):
                n[0] += 1
                ins.then_inc(steps, 1)
                eng.wait_ge(steps, n[0])
            return link

        def rope(e, link, x4, rot, half, heads, tmp):
            for t in range(T):
                x1, x2 = x4[:, t, :, 0:half], x4[:, t, :, half:2 * half]
                cos = rot[:, 0, t, :].unsqueeze(1).broadcast_to([P, heads, half])
                sin = rot[:, 1, t, :].unsqueeze(1).broadcast_to([P, heads, half])
                a, b, c, d = (m[:, 0:heads * half].rearrange("p (h f) -> p h f", f=half) for m in tmp)
                e.tensor_tensor(a, x1, cos, ALU.mult)
                e.tensor_tensor(b, x2, sin, ALU.mult)
                e.tensor_tensor(c, x2, cos, ALU.mult)
                link(e.tensor_tensor(d, x1, sin, ALU.mult))
                e.tensor_tensor(x1, a, b, ALU.subtract)
                last = e.tensor_tensor(x2, c, d, ALU.add)
                if t == 0:
                    link(last)
            return last

        block = ctx.enter_context(nc.Block())

        @block.sync
        def _(sp):
            sp.dma_start(X[:, :, :], x.rearrange("(t p) d -> p t d", p=P)).then_inc(x_loaded, 16)
            sp.dma_start(KT[:, :], table).then_inc(x_loaded, 16)

            def load(i):
                src, view, _, _ = items[i]
                if i >= RING:
                    sp.wait_ge(items[i - RING][2], items[i - RING][3])
                sp.dma_start(view, src).then_inc(slot_loaded[i % RING], 16)

            def load_expert(l, k, e, loaded=None):
                slot_no = ring_item(l, k) % RING
                signal = slot_loaded[slot_no] if loaded is None else loaded
                sp.dma_start(as_expert(ring[:, slot_no, :], k), expert_source(l, e, k)).then_inc(signal, 16)

            def load_experts(l, arena_free):
                for n in range(6 * AHEAD):
                    k, e, place = n % 6, n // 6 * 2 + n % 2, n % POOL
                    if n >= POOL:
                        sp.wait_ge(*expert_used(l, n - POOL))
                    elif place < RING:
                        i = ring_item(l, place)
                        sp.wait_ge(items[i - RING][2], items[i - RING][3])
                    elif place < POOL - 1:
                        sp.wait_ge(pj_done, arena_free)
                    else:
                        sp.wait_ge(logits_done, l + 1)
                    if place < RING:
                        slot_no = ring_item(l, place) % RING
                        sp.dma_start(as_expert(ring[:, slot_no, :], k), expert_source(l, e, k))\
                            .then_inc(slot_loaded[slot_no], 16)
                    else:
                        sp.dma_start(as_expert(FIRST[place - RING], k), expert_source(l, e, k))\
                            .then_inc(early_loaded[place - RING], 16)
                for k in range(6):
                    sp.wait_ge(*expert_used(l, 6 * AHEAD - POOL + k))
                    load_expert(l, k, AHEAD * 2 + k % 2)
                with sp.Fori(AHEAD + 1, PAIRS) as p:
                    for k in range(6):
                        used = (moe["gate_done"], moe["up_done"], moe["y1_done"])[k // 2]
                        sp.wait_ge(used, p + PAIRS * l)
                        load_expert(l, k, p * 2 + k % 2)
                sp.wait_ge(flag_ready, l + 1)
                more = sp.value_load(FLAG[0:1, l:l + 1], min_val=0, max_val=1)
                with sp.If(more > 0):
                    with sp.Fori(0, ROUNDS_MORE) as r:
                        with sp.Fori(0, PAIRS) as p:
                            sp.wait_ge(over_free[l], r * PAIRS + p + 1)
                            for k in range(6):
                                load_expert(l, k, p * 2 + k % 2, over_loaded[l])
                    sp.wait_ge(over_free[l], ROUNDS_MORE * PAIRS + 1)

            for i in I_EIN:
                load(i)
                if i == 0:
                    sp.dma_start(COLS[:, :], cols).then_inc(const_loaded, 16)
                    sp.dma_start(ROWS[:, :], rows[0, :].partition_broadcast(P)).then_inc(const_loaded, 16)
            sp.dma_start(WR[:, :, :, :], w_route).then_inc(const_loaded, 16)
            for i in [I_UQ, I_UKV] + I_EO:
                load(i)
            load_experts(0, 2 * G_EO + 1)
            for i in I_QKV + I_OO:
                load(i)
                if i == I_QKV[0]:
                    sp.dma_start(G[:, :, :], na_bias).then_inc(bias_loaded, 16)
            load_experts(1, 2 * G_OO + 1)
            for i in I_IN2 + I_OUT2 + I_UP + I_DN:
                load(i)
                if i == I_IN2[1]:
                    sp.dma_start(KT2[:, :], table2).then_inc(table2_loaded, 16)
                    sp.dma_start(GATE[:, :, :], gates).then_inc(table2_loaded, 16)
            for t in range(T):
                sp.wait_ge(out_ready, t + 1)
                sp.dma_start(out[t * P:(t + 1) * P, :], X[:, t, :]).then_inc(stored, 16)
            sp.wait_ge(stored, 16 * T)

        @block.gpsimd
        def _(pool):
            def norm_rows(n):
                pool.dma_start(LNR[:, :, :].rearrange("p a d -> p (a d)"),
                               ln_rows[n, :].partition_broadcast(P)).then_inc(ln_loaded, 16)

            def low_tiles(s, ks):
                for k in ks:
                    _, src, (high, low) = split_tile(s, k)
                    pool.wait_ge(w_hi, s["k0"] + k + 1)
                    nc.gpsimd.tensor_tensor(low[:, :, :], src, high[:, :, :], ALU.subtract).then_inc(w_lo, 1)

            link = counted(pool, pool_step)
            pool.wait_ge(rope_ready, 1)
            norm_rows(0)
            for t in range(T):
                pool.wait_ge(pj_free[t], G_EO)
            q4 = QB[:, :, :].rearrange("p t (h f) -> p t h f", f=B_QK)
            link(rope(nc.gpsimd, link, q4[:, :, :, B_NOPE:B_QK], rot_b, B_HALF, B_HEADS, ROTB))
            link(rope(nc.gpsimd, link, E[:, :, KR0:EVEN_IN].unsqueeze(2), rot_b, B_HALF, 1, ROTB))
            kv4 = KV[:, :, :].rearrange("p t (h f) -> p t h f", f=B_NOPE + B_V)
            kc4 = KC.rearrange("p t (h f) -> p t h f", f=B_QK)
            pool.wait_ge(tr_done, sum(TR["qk"]))
            for t in range(T):
                nc.gpsimd.tensor_copy(kc4[:, t, :, 0:B_NOPE], kv4[:, t, :, 0:B_NOPE])
                last = nc.gpsimd.tensor_copy(kc4[:, t, :, B_NOPE:B_QK],
                                             E[:, t, KR0:EVEN_IN].unsqueeze(1).broadcast_to([P, B_HEADS, B_ROPE]))
            last.then_inc(mla_ready, 1)
            pool.wait_ge(ao_scale, 1)
            pool.wait_ge(const_loaded, 48)
            sub = ROWS[:, R_SUB:R_SUB + P].unsqueeze(1).broadcast_to([P, A_HEADS, P])
            ao = [AO[:, t, :].rearrange("p (h e) -> p h e", h=A_HEADS) for t in range(T)]
            for t in range(T):
                last = nc.gpsimd.tensor_tensor(ao[t], ao[t], rs_a[:, t, :].unsqueeze(2).broadcast_to([P, A_HEADS, P]),
                                               ALU.mult)
            link(last)
            for t in range(T):
                last = nc.gpsimd.tensor_tensor(ao[t], ao[t], sub, ALU.mult)
            last.then_inc(ao_ready, 1)
            pool.wait_ge(x_ready, 2)
            norm_rows(1)
            low_tiles(S_QKV, range(3 * TILES))
            pool.wait_ge(x_ready, 4)
            norm_rows(2)
            low_tiles(S_QKV, range(3 * TILES, 6 * TILES))
            for a in range(N_NA0, N_NA0 + C_HEADS):
                pool.wait_ge(a_rec, a - N_NA0 + 1)
                nc.gpsimd.tensor_scalar(PN[a % 4][:, 0, :], PN[a % 4][:, 0, :], sm[:, a % 4, 0:1], None,
                                        ALU.mult).then_inc(a_p0, 1)
            pool.wait_ge(x_ready, 6)
            norm_rows(3)
            low_tiles(S_IN2, range(3 * TILES))
            pool.wait_ge(x_ready, 8)
            norm_rows(4)
            low_tiles(S_IN2, range(3 * TILES, 6 * TILES))
            pool.wait_ge(r_silu, 1)
            pool.wait_ge(ln_loaded, 16 * 5)
            for t in range(T):
                last = nc.gpsimd.tensor_tensor(TOK[:, t, 1536:2048], TOK[:, t, 1536:2048], LNR[:, 0, 0:RET_HEADS * RET_DIM],
                                               ALU.mult)
            last.then_inc(r_gain, 1)
            pool.wait_ge(r_gain, 1)
            norm_rows(5)

        @block.tensor
        def _(pe):
            def transposes(name, source, width=P, blocks=None):
                k0, groups = TR[name]
                blocks = 2 * groups if blocks is None else blocks
                for g in range(groups):
                    k = k0 + g
                    if k >= 4:
                        pe.wait_ge(tr_dve if k % 2 else tr_act, (k - 4) // 2 + 1)
                    for b in range(2 * g, min(2 * g + 2, blocks)):
                        for t in range(T):
                            last = nc.tensor.transpose(
                                bank[4 + k % 4][0:width, (b % 2) * SEQ + t * P:(b % 2) * SEQ + (t + 1) * P],
                                source(b, t), ident)
                    last.then_inc(tr_done, 1)

            def transposes_by_token(name, source, ready=None, n0=0, tiles=range(T)):
                k0 = TR[name][0]
                for t in tiles:
                    if ready is not None:
                        pe.wait_ge(ready, n0 + t + 1)
                    for h in range(2):
                        k = k0 + 2 * t + h
                        if k >= 4:
                            pe.wait_ge(tr_dve if k % 2 else tr_act, (k - 4) // 2 + 1)
                        for j in range(4):
                            c = 4 * h + j
                            last = nc.tensor.transpose(bank[4 + k % 4][:, j * P:(j + 1) * P],
                                                       source[:, t, c * P:(c + 1) * P], ident)
                        last.then_inc(tr_done, 1)

            def transposed(name):
                k = sum(TR[name])
                pe.wait_ge(tr_act, k // 2)
                pe.wait_ge(tr_dve, k // 2)

            def normed_and_first_chunk(name, source, ready, n0, s):
                for t in range(T):
                    transposes_by_token(name, source, ready, n0, [t])
                    split_project(s, 0, [t])

            def project(g, i, lhsT, rhs, kt, tiles=range(T)):
                pe.wait_ge(*arrived(i))
                for t in tiles:
                    if g >= 2:
                        pe.wait_ge(pj_free[t], g - 1)
                    width = rhs(0).shape[1]
                    for c in range(kt):
                        last = nc.tensor.matmul(bank[g % 2 * 2 + t][:, 0:width], lhsT(c, t), rhs(c),
                                                start=(c == 0), stop=(c == kt - 1))
                    last.then_inc(pj_done, 1)

            def mixed_tile(c, t):
                return MT[:, c, t * P:(t + 1) * P]

            def recurrence_tile(c, t):
                return LX[:, c, t * P:(t + 1) * P]

            def project_out(g0, i, rows=range(C), tile=mixed_tile):
                for t in range(T):
                    for n in range(2):
                        if t == 0:
                            pe.wait_ge(*arrived(i[n]))
                        pe.wait_ge(pj_free[t], g0 + n - 1)
                        for c in rows:
                            last = nc.tensor.matmul(bank[(g0 + n) % 2 * 2 + t][:, :], tile(c, t),
                                                    slot(i[n], C, 512)[:, c, :], start=(c == 0), stop=(c == C - 1))
                        if rows[-1] == C - 1:
                            last.then_inc(pj_done, 1)

            def project_t(g, i):
                pe.wait_ge(*arrived(i))
                for half in range(2):
                    if g >= 2:
                        pe.wait_ge(pj_free[half], g - 1)
                    for f in range(2):
                        for c in range(C):
                            last = nc.tensor.matmul(
                                bank[g % 2 * 2 + half][:, f * SEQ:(f + 1) * SEQ],
                                slot(i, C, 512)[:, c, (2 * half + f) * P:(2 * half + f + 1) * P],
                                XT[:, c, :], start=(c == 0), stop=(c == C - 1))
                    last.then_inc(pj_done, 1)

            def split_products(s, j, tiles, target, operands):
                g = s["g0"] + j
                for q in range(TILES):
                    if tiles[0] == 0:
                        pe.wait_ge(w_lo, s["k0"] + TILES * j + q + 1)
                    for t in tiles:
                        if q == 0:
                            pe.wait_ge(pj_free[t], g - 1)
                        parts = target(t)
                        for part_ in parts:
                            for c in range(2 * q, 2 * q + 2):
                                for n, (a, b) in enumerate(operands(t, part_, c, s["bufs"][q])):
                                    last = nc.tensor.matmul(part_(bank[g % 2 * 2 + t]), a, b,
                                                            start=(part_ is parts[0] and c == 0 and n == 0),
                                                            stop=(part_ is parts[-1] and c == C - 1 and n == 2))
                        if q == TILES - 1:
                            last.then_inc(pj_done, 1)
                    if q < TILES - 1 and tiles[-1] == T - 1:
                        last.then_inc(w_used, 1)

            def split_project(s, j, tiles=range(T)):
                if j == 0:
                    pe.wait_ge(x_lo, s["x0"] + tiles[-1] + 1)

                def operands(t, _, c, bufs):
                    tok = slice(t * P, (t + 1) * P)
                    high, low = (b[:, c % 2, :] for b in bufs)
                    return (XHI[:, c, tok], high), (XHI[:, c, tok], low), (XLO[:, c, tok], high)

                split_products(s, j, tiles, lambda t: [lambda b: b[:, :]], operands)

            def split_project_t(s, j):
                halves = [lambda b: b[:, 0:SEQ], lambda b: b[:, SEQ:2 * SEQ]]

                def operands(half, part_, c, bufs):
                    f = 2 * half + halves.index(part_)
                    high, low = (b[:, c % 2, f * P:(f + 1) * P] for b in bufs)
                    return (high, XHI[:, c, :]), (high, XLO[:, c, :]), (low, XHI[:, c, :])

                split_products(s, j, range(2), lambda half: halves, operands)

            def x_tile(c, t):
                return XT[:, c, t * P:(t + 1) * P]

            def attention(a0, n, q, k, v, probs, probs_t, free):
                for i in range(n + 4):
                    if i < n:
                        a = a0 + i
                        if i >= 3:
                            pe.wait_ge(free, i - 2)
                        for t in range(T):
                            last = nc.tensor.matmul(bank[4 + a % 3][:, t * SEQ:(t + 1) * SEQ], q(i, t), k(i),
                                                    start=True, stop=True)
                        last.then_inc(a_score, 1)
                    if 0 <= i - 3 < n:
                        a = a0 + i - 3
                        pe.wait_ge(a_p, a + 1)
                        if a0 == N_NA0:
                            pe.wait_ge(a_p0, i - 2)
                        if a >= 2:
                            pe.wait_ge(a_ptc, a - 1)
                        for t in range(T):
                            for kt in range(T):
                                last = nc.tensor.transpose(
                                    bank[a % 2][:, kt * SEQ + t * P:kt * SEQ + (t + 1) * P],
                                    probs[a % 4][:, t, kt * P:(kt + 1) * P], ident)
                        last.then_inc(a_pt, 1)
                    if 0 <= i - 4 < n:
                        a = a0 + i - 4
                        pair = a // 2
                        pe.wait_ge(a_ptc, a + 1)
                        if a % 2 == 0 and pair >= 2:
                            pe.wait_ge(a_o, pair - 1)
                        for kt in range(T):
                            last = nc.tensor.matmul(bank[2 + pair % 2][(a % 2) * 64:(a % 2) * 64 + 64, 0:SEQ],
                                                    v(i - 4, kt), probs_t[a % 2][:, kt, :],
                                                    start=(kt == 0), stop=(kt == T - 1))
                        last.then_inc(a_pv, 1)

            def gather(s):
                for c in range(C):
                    for t in range(T):
                        last = nc.tensor.matmul(bank[6 + c // 4][:, c % 4 * P:(c % 4 + 1) * P],
                                                X[:, t, c * P:(c + 1) * P], SEL[:, t, :],
                                                start=(t == 0), stop=(t == T - 1))
                    if c == C // 2 - 1:
                        last.then_inc(s["gather_lo"], 1)
                last.then_inc(s["gather_hi"], 1)

            def experts(s, n, g, matrix, used=None):
                pe.wait_ge(s["xg_lo"], g + 1)
                pe.wait_ge(s["xg_hi"], g + 1)
                for m, done in ((0, s["gate_done"]), (1, s["up_done"])):
                    w = [matrix(2 * m), matrix(2 * m + 1)]
                    for c in range(C):
                        for e in range(2):
                            last = nc.tensor.matmul(bank[4 + m][64 * e:64 * e + 64, :],
                                                    XG[:, c, 64 * e:64 * e + 64], w[e][:, c, :],
                                                    start=(c == 0), stop=(c == C - 1))
                    last.then_inc(done, 1)
                pe.wait_ge(s["sel_ready"], g + 2)
                gather(s)
                pe.wait_ge(s["h_ready"], n + 1)
                for j in range(FE // P):
                    last = nc.tensor.transpose(bank[4][:, j * P:(j + 1) * P], H[:, j * P:(j + 1) * P], ident)
                last.then_inc(s["hT_done"], 1)
                pe.wait_ge(s["selw_ready"], n + 1)
                for t in range(T):
                    last = nc.tensor.transpose(bank[5][:, t * P:(t + 1) * P], SELW[:, t, :], ident)
                last.then_inc(s["swt_done"], 1)
                w = [matrix(4), matrix(5)]
                pe.wait_ge(s["hT_copied"], n + 1)
                for half, free, done in ((0, s["xg_lo"], s["y0_done"]), (1, s["xg_hi"], s["y1_done"])):
                    pe.wait_ge(free, g + 2)
                    for j in range(FE // P):
                        for e in range(2):
                            last = nc.tensor.matmul(bank[6 + half][64 * e:64 * e + 64, :],
                                                    HT[:, j, 64 * e:64 * e + 64],
                                                    w[e][:, j, 512 * half:512 * half + 512],
                                                    start=(j == 0), stop=(j == FE // P - 1))
                    last.then_inc(done, 1)
                pe.wait_ge(s["swt_copied"], n + 1)
                for half, copied in ((0, s["y0_copied"]), (1, s["y1_copied"])):
                    pe.wait_ge(copied, n + 1)
                    for t in range(T):
                        last = nc.tensor.matmul(bank[2 * t + half][:, :], SWT[:, t, :],
                                                Y[:, 512 * half:512 * half + 512],
                                                start=False, stop=False, skip_group_check=True)
                if used is not None:
                    last.then_inc(used, 1)

            def moe_layer(l):
                for t in range(T):
                    for c in range(C):
                        last = nc.tensor.matmul(bank[4][:, t * 64:t * 64 + ROUTE], x_tile(c, t), WR[:, l, c, :],
                                                start=(c == 0), stop=(c == C - 1))
                last.then_inc(logits_done, 1)
                for b in range(4):
                    nc.tensor.matmul(bank[b][:, :], zeros, KT[:, 0:512],
                                     start=True, stop=False, skip_group_check=True)
                pe.wait_ge(r_one, l + 1)
                for t in range(T):
                    if t:
                        nc.tensor.matmul(bank[4][:, t * 64:t * 64 + EXPERTS], ones, ELOG[:, 0, :],
                                         start=True, stop=False)
                    last = nc.tensor.matmul(bank[4][:, t * 64:t * 64 + EXPERTS], earlier, ELOG[:, t, :],
                                            start=(t == 0), stop=True)
                last.then_inc(rank_done, 1)
                pe.wait_ge(r_top, l + 1)
                nc.tensor.transpose(bank[5][0:1, 0:P], rtop, ident).then_inc(top_done, 1)
                pe.wait_ge(moe["sel_ready"], (PAIRS + 1) * l + 1)
                gather(moe)

                def ring_matrix(k, count, loaded=None):
                    slot_no = ring_item(l, k) % RING
                    pe.wait_ge(slot_loaded[slot_no] if loaded is None else loaded, count)
                    return as_expert(ring[:, slot_no, :], k)

                def early_matrix(n):
                    turn, place = n // POOL, n % POOL
                    if place < RING:
                        i = ring_item(l, place) + turn * RING
                        pe.wait_ge(*arrived(i))
                        return as_expert(ring[:, i % RING, :], n % 6)
                    pe.wait_ge(early_loaded[place - RING], 16 * (6 * AHEAD // POOL * l + turn + 1))
                    return as_expert(FIRST[place - RING], n % 6)

                for p in range(AHEAD):
                    experts(moe, p + PAIRS * l, p + (PAIRS + 1) * l, lambda k: early_matrix(6 * p + k))
                with pe.Fori(AHEAD, PAIRS) as p:
                    experts(moe, p + PAIRS * l, p + (PAIRS + 1) * l,
                            lambda k: ring_matrix(k, (p - AHEAD + loads(after_turns(l, k))) * 16))
                pe.wait_ge(flag_ready, l + 1)
                more = pe.value_load(FLAG[0:1, l:l + 1], min_val=0, max_val=1)
                with pe.If(more > 0):
                    s = over[l]
                    pe.drain().then_inc(over_free[l], 1)
                    with pe.Fori(0, ROUNDS_MORE) as r:
                        pe.wait_ge(s["sel_ready"], r * (PAIRS + 1) + 1)
                        gather(s)
                        with pe.Fori(0, PAIRS) as p:
                            n = r * PAIRS + p
                            experts(s, n, r * (PAIRS + 1) + p,
                                    lambda k: ring_matrix(k, (n + 1) * 96, over_loaded[l]), over_free[l])
                pe.drain().then_inc(acc_done, 1)

            pe.wait_ge(x_loaded, 32)
            transposes_by_token("x", X)
            transposed("x")
            for g, n in enumerate(EIN):
                w = min(512, EVEN_IN - 512 * n)
                project(G_EIN + g, I_EIN[g], x_tile, lambda c: slot(I_EIN[g], C, w)[:, c, :], C)
            pe.wait_ge(rope_ready, 1)
            transposes("qk", lambda b, t: E[:, t, b * P:(b + 1) * P])
            pe.wait_ge(rank_ready, 1)
            transposes("c", lambda b, t: E[:, t, CQ0 + b * P:CQ0 + (b + 1) * P], blocks=3)
            transposed("c")
            def d_scores(h):
                if h >= 2:
                    pe.wait_ge(d_exp, 2 * (h - 1))
                for m in range(2):
                    half = slice(m * A_DIM, (m + 1) * A_DIM)
                    for t in range(T):
                        last = nc.tensor.matmul(bank[4 + 2 * (h % 2) + m][:, t * SEQ:(t + 1) * SEQ],
                                                QKT[half, h, t * P:(t + 1) * P], QKT[half, 4 + h, :],
                                                start=True, stop=True)
                    last.then_inc(d_score, 1)

            transposed("qk")
            for h in range(2):
                d_scores(h)
            for n in range(2):
                project(G_UQ + n, I_UQ, lambda c, t: CT[:, c, t * P:(t + 1) * P],
                        lambda c: slot(I_UQ, 2, 768)[:, c, 384 * n:384 * n + 384], 2)
            for n in range(2):
                project(G_UKV + n, I_UKV, lambda c, t: CT[:, 2, t * P:(t + 1) * P],
                        lambda c: slot(I_UKV, 1, 1024)[:, 0, 512 * n:512 * n + 512], 1)
            for t in range(T):
                pe.wait_ge(pj_free[t], G_EO)
            for i in range(1, A_HEADS + 2):
                if 2 <= i < A_HEADS:
                    d_scores(i)
                if i >= 2:
                    h = i - 2
                    pe.wait_ge(d_ptc, h + 1)
                    if h >= 2:
                        pe.wait_ge(d_o, h - 1)
                    for t in range(T):
                        for kt in range(T):
                            last = nc.tensor.matmul(bank[2 + h % 2][:, t * P:(t + 1) * P],
                                                    PT[h % 2][:, kt, t * P:(t + 1) * P],
                                                    E[:, kt, VA0 + h * P:VA0 + (h + 1) * P],
                                                    start=(kt == 0), stop=(kt == T - 1))
                    last.then_inc(d_pv, 1)
                if i - 1 < A_HEADS:
                    h = i - 1
                    pe.wait_ge(d_w, h + 1)
                    if h >= 2:
                        pe.wait_ge(d_ptc, h - 1)
                    for t in range(T):
                        for kt in range(T):
                            last = nc.tensor.transpose(bank[h % 2][:, kt * SEQ + t * P:kt * SEQ + (t + 1) * P],
                                                       PB[2 * (h % 2)][:, t, kt * P:(kt + 1) * P], ident)
                    last.then_inc(d_pt, 1)
            pe.wait_ge(mla_ready, 1)
            pe.wait_ge(d_o, A_HEADS)
            pe.wait_ge(d_sq, A_HEADS)
            transposes("qb", lambda b, t: QB[:, t, b * B_QK:(b + 1) * B_QK], B_QK)
            transposes("kb", lambda b, t: KC[:, t, b * B_QK:(b + 1) * B_QK], B_QK)
            transposed("kb")
            attention(N_MLA0, B_HEADS, lambda h, t: QBT[0:B_QK, h, t * P:(t + 1) * P], lambda h: KBT[0:B_QK, h, :],
                      lambda h, kt: KV[:, kt, h * 128 + B_NOPE:(h + 1) * 128], PB, PT, a_exp)
            pe.wait_ge(ao_ready, 1)
            transposes("ao", lambda b, t: AO[:, t, b * P:(b + 1) * P])
            transposed("ao")
            pe.wait_ge(a_o, B_HEADS // 2)
            project_out(G_EO, I_EO)
            transposes_by_token("ln0", X, x_ready, 0)
            transposed("ln0")
            moe_layer(0)

            normed_and_first_chunk("ln1", X, x_ready, 2, S_QKV)
            for n in range(1, 5):
                split_project_t(S_QKV, n)
            split_project(S_QKV, 5)
            for t in range(2):
                pe.wait_ge(pj_free[t], G_OO)

            def head_rows(h):
                return slice(h % 2 * C_DIM, h % 2 * C_DIM + C_DIM)

            attention(N_NA0, C_HEADS, lambda h, t: OQ[head_rows(h), h // 2, t * P:(t + 1) * P],
                      lambda h: OK[head_rows(h), h // 2, :],
                      lambda h, kt: OV[:, kt, h * C_DIM:(h + 1) * C_DIM], PN, PTN, a_free)
            pe.wait_ge(a_o, (B_HEADS + C_HEADS) // 2)
            project_out(G_OO, I_OO)
            transposes_by_token("ln2", X, x_ready, 4)
            transposed("ln2")
            moe_layer(1)

            normed_and_first_chunk("n1", XN, xn_ready, 0, S_IN2)
            for n in range(1, 3):
                split_project_t(S_IN2, n)
            split_project(S_IN2, 3)
            pe.wait_ge(table2_loaded, 32)
            pe.wait_ge(lru_cvd, LRU_T)
            for m in range(2):
                for half in range(2):
                    for f in range(2):
                        c = 2 * half + f
                        last = nc.tensor.matmul(bank[4 + 2 * m + half][:, f * SEQ:(f + 1) * SEQ],
                                                GATE[:, m, c * P:(c + 1) * P], LX[:, c, :], start=True, stop=True)
                    last.then_inc(lru_gm, 1)
            split_project(S_IN2, 4)
            split_project(S_IN2, 5, [0])
            pe.wait_ge(r_rope, 1)
            pe.wait_ge(lru_g, 4)
            transposes("rqk", lambda b, t: TOK[:, t, b * P:(b + 1) * P])
            pe.wait_ge(pj_free[0], G_IN2 + 5)
            pe.wait_ge(lru_sq, 1)
            for c in range(LRU_T):
                last = nc.tensor.matmul(bank[0][:, 0:SEQ], ones, LT_[:, c, :], start=(c == 0), stop=(c == LRU_T - 1))
            last.then_inc(lru_sqr, 1)
            transposed("rqk")
            for h in range(RET_HEADS):
                nc.tensor.matmul(bank[4 + h][:, 0:SEQ], RQK[:, 4 + h, 0:P], RQK[:, h, :], start=True, stop=True)
                nc.tensor.matmul(bank[4 + h][:, SEQ:DEC_W], RQK[:, 4 + h, P:SEQ], RQK[:, h, P:SEQ],
                                 start=True, stop=True).then_inc(r_sc, 1)
            split_project(S_IN2, 5, [1])
            pe.wait_ge(pj_free[0], G_OUT2)
            pe.wait_ge(pj_free[1], G_OUT2)
            for h in range(RET_HEADS):
                pe.wait_ge(r_scd, h + 1)
                if h >= 2:
                    pe.wait_ge(r_oc, h - 1)
                b = bank[4 + h % 2]
                v = [TOK[:, t, 1024 + h * P:1024 + (h + 1) * P] for t in range(T)]
                nc.tensor.matmul(b[:, 0:P], RS[:, h, 0:P], v[0], start=True, stop=True)
                nc.tensor.matmul(b[:, P:SEQ], RS[:, h, P:SEQ], v[0], start=True, stop=False)
                nc.tensor.matmul(b[:, P:SEQ], RS[:, h, SEQ:DEC_W], v[1], start=False, stop=True).then_inc(r_o, 1)
            pe.wait_ge(lru_y, 1)
            project_out(G_OUT2, I_OUT2, range(LRU_T), recurrence_tile)
            pe.wait_ge(r_y, 1)
            transposes("yr", lambda b, t: YR[:, t, b * P:(b + 1) * P])
            transposed("yr")
            project_out(G_OUT2, I_OUT2, range(LRU_T, C))
            transposes_by_token("n2", XN, xn_ready, 2)
            pe.wait_ge(x_lo, X_FFN + T)
            for f in range(FF2_T):
                pe.wait_ge(w_lo, K_FFN + f + 1)
                if f >= 4:
                    pe.wait_ge(f_cv, f - 3)
                for c in range(C):
                    w_high, w_low = WHI[f % WBUF][:, c, :], WLO[f % WBUF][:, c, :]
                    for n, (w, xs) in enumerate(((w_high, XHI), (w_high, XLO), (w_low, XHI))):
                        last = nc.tensor.matmul(bank[f % 4][:, 0:SEQ], w, xs[:, c, :], start=(c == 0 and n == 0),
                                                stop=(c == C - 1 and n == 2))
                last.then_inc(w_used, 1)

            def down(c, t):
                i, tok = (FF2_T + c) % WBUF, slice(t * P, (t + 1) * P)
                for half in range(2):
                    w_high, w_low = WHI[i][:, 4 * half:4 * half + 4, :], WLO[i][:, 4 * half:4 * half + 4, :]
                    a_high, a_low = AHI[c % WBUF][:, tok], ALO[c % WBUF][:, tok]
                    for n, (a, w) in enumerate(((a_high, w_high), (a_high, w_low), (a_low, w_high))):
                        last = nc.tensor.matmul(bank[4 + 2 * t + half][:, :], a, w.rearrange("p a b -> p (a b)"),
                                                start=(c == 0 and n == 0), stop=(c == DOWN_T - 1 and n == 2))
                return last

            for c in range(DOWN_T - WBUF):
                pe.wait_ge(w_lo, K_FFN + FF2_T + c + 1)
                pe.wait_ge(a_lo, c + 1)
                for t in range(T):
                    last = down(c, t)
                last.then_inc(w_used, 1)
            for t in range(T):
                for c in range(DOWN_T - WBUF, DOWN_T):
                    if t == 0:
                        pe.wait_ge(w_lo, K_FFN + FF2_T + c + 1)
                        pe.wait_ge(a_lo, c + 1)
                    last = down(c, t)
                last.then_inc(w_used, 1)

        @block.scalar
        def _(act):
            def evac_transposes(name, dest, width=P, blocks=None, gain=None):
                k0, groups = TR[name]
                blocks = 2 * groups if blocks is None else blocks
                for g in range(groups):
                    k = k0 + g
                    if k % 2:
                        continue
                    act.wait_ge(tr_done, k + 1)
                    n = min(2, blocks - 2 * g)
                    if gain is None:
                        last = nc.scalar.copy(dest(2 * g, n), bank[4 + k % 4][0:width, 0:n * SEQ].rearrange(
                            "p (a b) -> p a b", b=SEQ))
                    else:
                        for b in range(n):
                            last = nc.scalar.activation(dest(2 * g + b, 1), bank[4 + k % 4][0:width, b * SEQ:(b + 1) * SEQ],
                                                        ACT.Copy, scale=gain(2 * g + b))
                    last.then_inc(tr_act, 1)

            def evac_token(name, t, gain=None):
                k = TR[name][0] + 2 * t
                act.wait_ge(tr_done, k + 1)
                src = bank[4 + k % 4][:, :].rearrange("p (c s) -> p c s", s=P)
                if gain is None:
                    last = nc.scalar.copy(XT[:, 0:4, t * P:(t + 1) * P], src)
                else:
                    for c in range(4):
                        last = nc.scalar.activation(XT[:, c, t * P:(t + 1) * P], src[:, c, :], ACT.Copy,
                                                    scale=COLS[:, gain + c:gain + c + 1])
                last.then_inc(tr_act, 1)

            def evac_by_token(name, gain=None):
                for t in range(T):
                    evac_token(name, t, gain)

            def evac_chunk(g, dest):
                act.wait_ge(pj_done, 2 * g + 1)
                nc.scalar.copy(dest, bank[g % 2 * 2][:, 0:dest.free_size()].rearrange("p (a b) -> p a b", b=dest.shape[2])
                               if len(dest.shape) == 3 else bank[g % 2 * 2][:, 0:dest.shape[1]]).then_inc(pj_free[0], 1)

            roots = [0]

            def root(v):
                roots[0] += 1
                act.wait_ge(var_ready, roots[0])
                nc.scalar.activation(v, v, ACT.Sqrt).then_inc(std_ready, 1)

            def token_roots():
                for t in range(T):
                    root(var_l[:, t:t + 1])

            def attention(a0, n, probs, probs_t, scale):
                for i in range(n + 3):
                    if i >= 3:
                        a = a0 + i - 3
                        act.wait_ge(a_pt, a + 1)
                        if a >= 2:
                            act.wait_ge(a_pv, a - 1)
                        nc.scalar.copy(probs_t[a % 2][:, :, :], bank[a % 2][:, :].rearrange("p (a b) -> p a b", b=SEQ))\
                            .then_inc(a_ptc, 1)
                    if i < n:
                        a = a0 + i
                        act.wait_ge(a_nb, a + 1)
                        if a >= 4 and scale is not None:
                            act.wait_ge(a_pt, a - 3)
                        for t in range(T):
                            src = bank[4 + a % 3][:, t * SEQ:(t + 1) * SEQ] if scale is not None else probs[a % 4][:, t, :]
                            last = nc.scalar.activation(probs[a % 4][:, t, :], src, ACT.Exp, bias=nb[:, a % 4, t:t + 1],
                                                        scale=1.0 if scale is None else scale,
                                                        accum_out=sm[:, a % 4, t:t + 1])
                        last.then_inc(a_exp, 1)

            def experts(s, n, g):
                act.wait_ge(s["gate_done"], n + 1)
                nc.scalar.activation(SG, bank[4][:, :], ACT.Silu).then_inc(s["silu_done"], 1)
                act.wait_ge(s["gather_lo"], g + 2)
                nc.scalar.copy(XG[:, 0:4, :], bank[6][:, :].rearrange("p (a b) -> p a b", b=P)).then_inc(s["xg_lo"], 1)
                act.wait_ge(s["hT_done"], n + 1)
                nc.scalar.copy(HT[:, :, :], bank[4][:, :].rearrange("p (a b) -> p a b", b=P)).then_inc(s["hT_copied"], 1)
                act.wait_ge(s["swt_done"], n + 1)
                nc.scalar.copy(SWT[:, :, :], bank[5][:, 0:SEQ].rearrange("p (a b) -> p a b", b=P)).then_inc(s["swt_copied"], 1)
                act.wait_ge(s["y0_done"], n + 1)
                nc.scalar.copy(Y[:, 0:512], bank[6][:, :]).then_inc(s["y0_copied"], 1)

            def first_tokens(s, g):
                act.wait_ge(s["gather_lo"], g + 1)
                nc.scalar.copy(XG[:, 0:4, :], bank[6][:, :].rearrange("p (a b) -> p a b", b=P)).then_inc(s["xg_lo"], 1)

            def moe_layer(l):
                act.wait_ge(r_gmax, l + 1)
                for t in range(T):
                    last = nc.scalar.activation(rg[:, t, 0:GROUPS], LOG[:, t, 0:GROUPS], ACT.Exp, bias=gmn[:, t:t + 1],
                                                accum_out=gsum[:, t:t + 1])
                last.then_inc(r_gexp, 1)
                act.wait_ge(r_d, l + 1)
                nc.scalar.activation(p2, p2, ACT.Exp).then_inc(r_p2, 1)
                first_tokens(moe, (PAIRS + 1) * l)
                with act.Fori(0, PAIRS) as p:
                    experts(moe, p + PAIRS * l, p + (PAIRS + 1) * l)
                act.wait_ge(flag_ready, l + 1)
                more = act.value_load(FLAG[0:1, l:l + 1], min_val=0, max_val=1)
                with act.If(more > 0):
                    with act.Fori(0, ROUNDS_MORE) as r:
                        first_tokens(over[l], r * (PAIRS + 1))
                        with act.Fori(0, PAIRS) as p:
                            experts(over[l], r * PAIRS + p, r * (PAIRS + 1) + p)

            def high_tiles(s, ks):
                for k in ks:
                    i, src, (high, _) = split_tile(s, k)
                    act.wait_ge(*arrived(i))
                    act.wait_ge(*(s["free"] if k < TILES else split_used(s, k - TILES)))
                    nc.scalar.copy(high[:, :, :], src).then_inc(w_hi, 1)

            def high_input(name, t):
                for copied in (tr_act, tr_dve):
                    act.wait_ge(copied, TR[name][0] // 2 + t + 1)
                nc.scalar.copy(XHI[:, :, t * P:(t + 1) * P], XT[:, :, t * P:(t + 1) * P]).then_inc(x_hi, 1)

            def next_tiles(s, j, evac):
                more = j + 1 < len(s["items"])
                if more:
                    high_tiles(s, range(TILES * (j + 1), TILES * (j + 2) - 1))
                evac()
                if more:
                    high_tiles(s, [TILES * (j + 2) - 1])

            evac_by_token("x")
            for g, n in enumerate(EIN):
                if g == 3:
                    root(var_b[:, :, :])
                evac_chunk(G_EIN + g, E[:, 0, 512 * n:min(512 * n + 512, EVEN_IN)])
            act.wait_ge(const_loaded, 48)
            act.wait_ge(lam_ready, 1)
            nc.scalar.activation(lamv, lamv, ACT.Exp).then_inc(lam_exp, 1)
            evac_transposes("qk", lambda b, n: QKT[:, b:b + n, :])
            evac_transposes("c", lambda b, n: CT[:, b, :], blocks=3, gain=lambda b: COLS[:, Q_QN + b:Q_QN + b + 1])
            def d_exps(h):
                for m in range(2):
                    act.wait_ge(d_nb, 2 * h + m + 1)
                    if h >= 2:
                        act.wait_ge(d_pt, h - 1)
                    for t in range(T):
                        last = nc.scalar.activation(PB[2 * (h % 2) + m][:, t, :],
                                                    bank[4 + 2 * (h % 2) + m][:, t * SEQ:(t + 1) * SEQ], ACT.Exp,
                                                    bias=dnb[:, h % 2, m, t:t + 1], scale=A_DIM ** -0.5,
                                                    accum_out=dsm[:, h % 2, m, t:t + 1])
                    last.then_inc(d_exp, 1)

            for h in range(2):
                d_exps(h)
            for n in range(2):
                evac_chunk(G_UQ + n, QB[:, 0, 384 * n:384 * n + 384])
            for n in range(2):
                evac_chunk(G_UKV + n, KV[:, 0, 512 * n:512 * n + 512])
            for i in range(1, A_HEADS + 2):
                if 2 <= i < A_HEADS:
                    d_exps(i)
                if i - 1 < A_HEADS:
                    h = i - 1
                    act.wait_ge(d_pt, h + 1)
                    if h >= 2:
                        act.wait_ge(d_pv, h - 1)
                    nc.scalar.copy(PT[h % 2][:, :, :], bank[h % 2][:, :].rearrange("p (a b) -> p a b", b=SEQ))\
                        .then_inc(d_ptc, 1)
                if i >= 2:
                    h = i - 2
                    act.wait_ge(d_o, h + 1)
                    for t in range(T):
                        last = nc.scalar.activation(SQA[:, t, h * P:(h + 1) * P], AO[:, t, h * P:(h + 1) * P],
                                                    ACT.Square, accum_out=var_a[:, t, h:h + 1])
                    last.then_inc(d_sq, 1)
            root(var_a[:, :, :])
            evac_transposes("qb", lambda b, n: QBT[0:B_QK, b:b + n, :], B_QK)
            evac_transposes("kb", lambda b, n: KBT[0:B_QK, b:b + n, :], B_QK)
            attention(N_MLA0, B_HEADS, PB, PT, B_QK ** -0.5)
            evac_transposes("ao", lambda b, n: MT[:, b:b + n, :])
            token_roots()
            evac_by_token("ln0")
            moe_layer(0)
            high_tiles(S_QKV, range(2))
            for t in range(T):
                root(var_l[:, t:t + 1])
                if t == 0:
                    high_tiles(S_QKV, range(2, TILES))
                evac_token("ln1", t)
                high_input("ln1", t)
            for n in range(6):
                dest = (OQ if n < 3 else OK)[:, 4 * ((n - 1) % 2):4 * ((n - 1) % 2) + 2, :] if 0 < n < 5 else \
                    OV[:, 0, 512 * (n // 5):512 * (n // 5) + 512]
                next_tiles(S_QKV, n, lambda: evac_chunk(G_QKV + n, dest))
            attention(N_NA0, C_HEADS, PN, PTN, None)
            token_roots()
            evac_by_token("ln2")
            moe_layer(1)
            high_tiles(S_IN2, range(2))
            for t in range(T):
                root(var_l[:, t:t + 1])
                root(var_l[:, t:t + 1])
                if t == 0:
                    high_tiles(S_IN2, range(2, TILES))
                evac_token("n1", t, Q_N1)
                high_input("n1", t)

            def evac_2(n):
                evac_chunk(G_IN2 + n, TOK[:, 0, 512 * (IN2[n] - 2):512 * (IN2[n] - 1)])

            next_tiles(S_IN2, 0, lambda: evac_2(0))
            next_tiles(S_IN2, 1, lambda: evac_chunk(G_IN2 + 1, XL[:, 0:2, :]))
            g = G_IN2 + 2
            high_tiles(S_IN2, range(3 * TILES, 4 * TILES - 1))
            act.wait_ge(pj_done, 2 * g + 1)
            nc.scalar.activation(GL[:, 0:2, :], bank[g % 2 * 2][:, :].rearrange("p (a b) -> p a b", b=SEQ),
                                 ACT.Gelu_apprx_tanh).then_inc(pj_free[0], 1)
            act.wait_ge(pj_done, 2 * g + 2)
            act.wait_ge(pj_free[1], g)
            nc.scalar.activation(GL[:, 2:4, :], bank[g % 2 * 2 + 1][:, :].rearrange("p (a b) -> p a b", b=SEQ),
                                 ACT.Gelu_apprx_tanh).then_inc(pj_free[1], 1)
            high_tiles(S_IN2, [4 * TILES - 1])
            for t in range(T):
                act.wait_ge(pj_free[t], G_IN2 + 1)
                last = nc.scalar.activation(TOK[:, t, 1536:2048], TOK[:, t, 1536:2048], ACT.Silu)
            last.then_inc(r_silu, 1)
            act.wait_ge(sp_in, 1)
            nc.scalar.activation(spl[1], spl[1], ACT.Exp).then_inc(sp_exp, 1)
            next_tiles(S_IN2, 3, lambda: evac_2(3))
            act.wait_ge(sp_in, 2)
            for c in range(LRU_T):
                for m, dst in ((0, LA), (1, LI)):
                    act.wait_ge(lru_gm, 2 * m + c // 2 + 1)
                    last = nc.scalar.activation(dst[:, c, :], bank[4 + 2 * m + c // 2][:, c % 2 * SEQ:(c % 2 + 1) * SEQ],
                                                ACT.Tanh, scale=0.5, bias=spl[3 + m][:, c:c + 1])
                last.then_inc(lru_g, 1)
            act.wait_ge(lru_t, 1)
            nc.scalar.activation(LT_[:, :, :], LA[:, :, :], ACT.Tanh, scale=-1.0).then_inc(lru_a, 1)
            nc.scalar.activation(LA[:, :, :], LA[:, :, :], ACT.Exp).then_inc(lru_a, 1)
            root(LT_[:, :, :])
            next_tiles(S_IN2, 4, lambda: evac_2(4))
            evac_2(5)
            evac_transposes("rqk", lambda b, n: RQK[:, b:b + n, :])
            root(LI[:, 0, :])
            root(var_h[:, :, :])
            evac_transposes("yr", lambda b, n: MT[:, 4 + b:4 + b + n, :])
            def high_weights(k):
                i, src = ffn_weights(k)
                act.wait_ge(*arrived(i))
                if k >= WBUF:
                    act.wait_ge(w_used, U_FFN + k - WBUF + 1)
                nc.scalar.copy(WHI[k % WBUF][:, :, :], src).then_inc(w_hi, 1)

            def high_products(c):
                act.wait_ge(f_act, c + 1)
                nc.scalar.copy(AHI[c % WBUF][:, :], ACTT[:, c, :]).then_inc(a_hi, 1)

            act.wait_ge(lru_y, 1)
            act.wait_ge(tr_done, sum(TR["yr"]))
            for k in range(WBUF):
                high_weights(k)
            token_roots()
            for t in range(T):
                evac_token("n2", t, Q_N2)
                high_input("n2", t)
            for f in range(FF2_T + 2):
                if f < FF2_T:
                    act.wait_ge(w_used, U_FFN + f + 1)
                    if f >= 4:
                        act.wait_ge(f_gelu if f - 4 < DOWN_T else f_act, f - 3 if f - 4 < DOWN_T else f - 3 - DOWN_T)
                    nc.scalar.activation(CV[f % 4], bank[f % 4][:, 0:SEQ], ACT.Identity,
                                         scale=COLS[:, Q_FW + 2 * FF2_T + f:Q_FW + 2 * FF2_T + f + 1],
                                         bias=COLS[:, Q_FB + f:Q_FB + f + 1]).then_inc(f_cv0, 1)
                    high_weights(f + WBUF)
                    if EARLY_A <= f < EARLY_A + WBUF:
                        high_products(f - EARLY_A)
                if 2 <= f < DOWN_T + 2:
                    act.wait_ge(f_cv, f - 1)
                    nc.scalar.activation(ACTT[:, f - 2, :], CV[(f - 2) % 4], ACT.Gelu_apprx_tanh).then_inc(f_gelu, 1)
            for c in range(WBUF, DOWN_T):
                high_weights(FF2_T + c)
                high_products(c)
            token_roots()

        @block.vector
        def _(dve):
            v = nc.vector
            link = counted(dve, dve_step)

            def evac_transposes(name, dest, width=P, blocks=None, gain=None):
                k0, groups = TR[name]
                blocks = 2 * groups if blocks is None else blocks
                for g in range(groups):
                    k = k0 + g
                    if k % 2 == 0:
                        continue
                    dve.wait_ge(tr_done, k + 1)
                    n = min(2, blocks - 2 * g)
                    if gain is None:
                        last = v.tensor_copy(dest(2 * g, n), bank[4 + k % 4][0:width, 0:n * SEQ].rearrange(
                            "p (a b) -> p a b", b=SEQ))
                    else:
                        for b in range(n):
                            last = v.tensor_scalar(dest(2 * g + b, 1), bank[4 + k % 4][0:width, b * SEQ:(b + 1) * SEQ],
                                                   gain(2 * g + b), None, ALU.mult)
                    last.then_inc(tr_dve, 1)

            def evac_token(name, t, gain=None):
                k = TR[name][0] + 2 * t + 1
                dve.wait_ge(tr_done, k + 1)
                dst = XT[:, 4:8, t * P:(t + 1) * P]
                src = bank[4 + k % 4][:, :].rearrange("p (c s) -> p c s", s=P)
                if gain is None:
                    last = v.tensor_copy(dst, src)
                else:
                    last = v.tensor_tensor(dst, src, COLS[:, gain + 4:gain + 8].unsqueeze(2).broadcast_to([P, 4, P]),
                                           ALU.mult)
                last.then_inc(tr_dve, 1)

            def evac_by_token(name, gain=None):
                for t in range(T):
                    evac_token(name, t, gain)

            def evac_chunk(g, dest):
                dve.wait_ge(pj_done, 2 * g + 2)
                src = bank[g % 2 * 2 + 1]
                v.tensor_copy(dest, src[:, 0:dest.free_size()].rearrange("p (a b) -> p a b", b=dest.shape[2])
                              if len(dest.shape) == 3 else src[:, 0:dest.shape[1]]).then_inc(pj_free[1], 1)

            def add_out(g0, t, alpha):
                for n in range(2):
                    dve.wait_ge(pj_done, 2 * g0 + 2 * t + n + 1)
                    xs = X[:, t, 512 * n:512 * n + 512]
                    v.scalar_tensor_tensor(xs, xs, alpha, bank[(g0 + n) % 2 * 2 + t][:, :], ALU.mult, ALU.add)\
                        .then_inc(pj_free[t], 1)
                dve.wait_ge(pj_free[t], g0 + 2)

            def add_experts(t):
                for h in range(2):
                    xs = X[:, t, 512 * h:512 * h + 512]
                    last = v.scalar_tensor_tensor(xs, xs, ALPHA, bank[2 * t + h][:, :], ALU.mult, ALU.add)
                link(last)

            roots = [0]

            def inverse_root(var, out_):
                dve.wait_ge(std_ready, roots[0])
                link(v.reciprocal(out_, var))

            def ask_root(ins):
                roots[0] += 1
                ins.then_inc(var_ready, 1)

            norms = [0]

            def layer_norm(add, then=None, evac=None, low=None):
                for t in range(T):
                    add(t)
                    if t and evac is not None:
                        evac(t - 1)
                    for h in range(2):
                        last = v.bn_stats(bst[:, t, h, :], X[:, t, 512 * h:512 * h + 512])
                    link(last)
                    if t and low is not None:
                        low(t - 1)
                    link(v.bn_aggr(mv[:, t, :], bst[:, t, :, :].rearrange("p a b -> p (a b)")))
                    ask_root(v.tensor_scalar(var_l[:, t:t + 1], mv[:, t, 1:2], LN_EPS, None, ALU.add))
                    dve.wait_ge(ln_loaded, 16 * (norms[0] + 1))
                    link(v.scalar_tensor_tensor(X[:, t, :], X[:, t, :], mv[:, t, 0:1], LNR[:, 0, :], ALU.subtract, ALU.mult))
                    inverse_root(var_l[:, t:t + 1], rs_l[:, t:t + 1])
                    v.scalar_tensor_tensor(X[:, t, :], X[:, t, :], rs_l[:, t:t + 1], LNR[:, 1, :], ALU.mult, ALU.add)\
                        .then_inc(x_ready, 1)
                    if then is not None:
                        dve.wait_ge(x_ready, T * norms[0] + t + 1)
                        then(t)
                norms[0] += 1
                dve.wait_ge(x_ready, T * norms[0])
                if evac is not None:
                    evac(T - 1)
                if low is not None:
                    low(T - 1)

            def token_rms(t, xn):
                link(v.tensor_tensor_reduce(xn[:, t, :], X[:, t, :], X[:, t, :], 1.0, 0.0, ALU.mult, ALU.add,
                                            var_l[:, t:t + 1]))
                ask_root(v.tensor_scalar(var_l[:, t:t + 1], var_l[:, t:t + 1], 1.0 / D, RMS_EPS, ALU.mult, ALU.add))
                inverse_root(var_l[:, t:t + 1], rs_l[:, t:t + 1])

            def normed(t, xn):
                token_rms(t, xn)
                v.tensor_scalar(xn[:, t, :], X[:, t, :], rs_l[:, t:t + 1], None, ALU.mult).then_inc(xn_ready, 1)

            def low_input(t, x0):
                tok = slice(t * P, (t + 1) * P)
                dve.wait_ge(x_hi, x0 + t + 1)
                v.tensor_tensor(XLO[:, :, tok], XT[:, :, tok], XHI[:, :, tok], ALU.subtract).then_inc(x_lo, 1)

            def continue_pair(i, a0, dest):
                if i >= 5 and (i - 5) % 2 == 1:
                    pair = (a0 + i - 5) // 2
                    dve.wait_ge(a_pv, 2 * pair + 2)
                    v.tensor_copy(dest(pair - a0 // 2), bank[2 + pair % 2][:, 0:SEQ]).then_inc(a_o, 1)

            def attention(a0, n, probs, dest, scale, bias):
                for i in range(n + 5):
                    if i < n:
                        a = a0 + i
                        dve.wait_ge(a_score, a + 1)
                        ps = bank[4 + a % 3][:, :].rearrange("p (t k) -> p t k", t=T)
                        if bias is None:
                            link(v.tensor_reduce(mx[:, a % 4, :], ps, AX, ALU.max))
                            v.tensor_scalar(nb[:, a % 4, :], mx[:, a % 4, :], -scale, None, ALU.mult).then_inc(a_nb, 1)
                        else:
                            if a >= 4:
                                dve.wait_ge(a_pt, a - 3)
                            for t in range(T):
                                last = v.scalar_tensor_tensor(probs[a % 4][:, t, :], ps[:, t, :], scale, bias(i, t),
                                                              ALU.mult, ALU.add)
                            last.then_inc(a_free, 1)
                            dve.wait_ge(a_free, i + 1)
                            v.tensor_reduce(nb[:, a % 4, :], probs[a % 4][:, :, :], AX, ALU.max, negate=True)\
                                .then_inc(a_nb, 1)
                    if 0 <= i - 1 < n:
                        a = a0 + i - 1
                        dve.wait_ge(a_exp, a + 1)
                        if bias is not None:
                            v.reciprocal(sm[:, a % 4, :], sm[:, a % 4, :]).then_inc(a_rec, 1)
                            dve.wait_ge(a_rec, i)
                            v.tensor_scalar(probs[a % 4][:, 1, :], probs[a % 4][:, 1, :], sm[:, a % 4, 1:2], None, ALU.mult)\
                                .then_inc(a_p, 1)
                            continue_pair(i, a0, dest)
                            continue
                        link(v.reciprocal(sm[:, a % 4, :], sm[:, a % 4, :]))
                        for t in range(T):
                            last = v.tensor_scalar(probs[a % 4][:, t, :], probs[a % 4][:, t, :], sm[:, a % 4, t:t + 1], None,
                                                   ALU.mult)
                        last.then_inc(a_p, 1)
                    continue_pair(i, a0, dest)

            def select(s, pair, g):
                io = iota_s.unsqueeze(1).broadcast_to([P, 2, SLOTS])
                for t in range(T):
                    last = v.tensor_tensor(SEL[:, t, :].rearrange("p (e s) -> p e s", e=2), io,
                                           RANK[:, t, bass.ds(pair * 2, 2)].unsqueeze(2).broadcast_to([P, 2, SLOTS]),
                                           ALU.is_equal)
                last.then_inc(s["sel_ready"], 1)

            def first_tokens(s, g):
                dve.wait_ge(s["gather_hi"], g + 1)
                v.tensor_copy(XG[:, 4:8, :], bank[7][:, :].rearrange("p (a b) -> p a b", b=P)).then_inc(s["xg_hi"], 1)

            def experts(s, pair, n, g):
                dve.wait_ge(s["sel_ready"], g + 1)
                for t in range(T):
                    last = v.tensor_tensor(SELW[:, t, :].rearrange("p (e s) -> p e s", e=2),
                                           SEL[:, t, :].rearrange("p (e s) -> p e s", e=2),
                                           WGT[:, t, bass.ds(pair * 2, 2)].unsqueeze(2).broadcast_to([P, 2, SLOTS]),
                                           ALU.mult)
                last.then_inc(s["selw_ready"], 1)
                dve.wait_ge(s["selw_ready"], n + 1)
                dve.wait_ge(s["gather_hi"], g + 1)
                select(s, pair + 1, g)
                dve.wait_ge(s["silu_done"], n + 1)
                dve.wait_ge(s["up_done"], n + 1)
                v.tensor_tensor(H, SG, bank[5][:, :], ALU.mult).then_inc(s["h_ready"], 1)
                dve.wait_ge(s["gather_hi"], g + 2)
                v.tensor_copy(XG[:, 4:8, :], bank[7][:, :].rearrange("p (a b) -> p a b", b=P)).then_inc(s["xg_hi"], 1)
                dve.wait_ge(s["y1_done"], n + 1)
                v.tensor_copy(Y[:, 512:1024], bank[7][:, :]).then_inc(s["y1_copied"], 1)

            def moe_layer(l, then, evac, low):
                dve.wait_ge(logits_done, l + 1)
                lg = bank[4][:, 0:128].rearrange("p (t f) -> p t f", t=T)[:, :, 0:ROUTE]
                br = ROWS[:, R_BR + l * ROUTE:R_BR + (l + 1) * ROUTE].unsqueeze(1).broadcast_to([P, T, ROUTE])
                link(v.tensor_tensor(LOG[:, :, :], lg, br, ALU.add))

                def first_of(vals, top, width, at, cand, one):
                    bc = top.unsqueeze(2).broadcast_to([P, T, width])
                    io = iota_e[:, 0:width].unsqueeze(1).broadcast_to([P, T, width])
                    link(v.tensor_tensor(cand, vals, bc, ALU.is_equal))
                    link(v.tensor_tensor(cand, cand, io, ALU.mult))
                    link(v.tensor_reduce(at, cand, AX, ALU.min))
                    link(v.tensor_tensor(one, io, at.unsqueeze(2).broadcast_to([P, T, width]), ALU.is_equal))

                lgr = LOG[:, :, 0:GROUPS]
                link(v.tensor_reduce(m1, lgr, AX, ALU.max))
                v.tensor_scalar(gmn, m1, -1.0, None, ALU.mult).then_inc(r_gmax, 1)
                first_of(lgr, m1, GROUPS, i1, ru[:, :, 0:GROUPS], ru[:, :, 4:4 + GROUPS])
                link(v.tensor_scalar(ru[:, :, 4:8], ru[:, :, 4:8], -1.0, -NEG, ALU.add, ALU.mult))
                for t in range(T):
                    last = v.tensor_tensor(ELOG[:, t, :].rearrange("p (g e) -> p g e", g=GROUPS),
                                           LOG[:, t, GROUPS:ROUTE].rearrange("p (g e) -> p g e", g=GROUPS),
                                           ru[:, t, 4:8].unsqueeze(2).broadcast_to([P, GROUPS, PER_GROUP]), ALU.add)
                link(last)
                link(v.tensor_reduce(m1, ELOG[:, :, :], AX, ALU.max))
                first_of(ELOG[:, :, :], m1, EXPERTS, i1, RANK[:, :, 0:EXPERTS], ONE1[:, :, :])
                link(v.scalar_tensor_tensor(ELOG[:, :, :], ONE1[:, :, :], 3 * NEG, ELOG[:, :, :], ALU.mult, ALU.add))
                link(v.tensor_reduce(m2, ELOG[:, :, :], AX, ALU.max))
                v.tensor_tensor(p2, m2, m1, ALU.subtract).then_inc(r_d, 1)
                first_of(ELOG[:, :, :], m2, EXPERTS, i2, RANK[:, :, 0:EXPERTS], ONE2[:, :, :])
                v.tensor_tensor(ELOG[:, :, :], ONE1[:, :, :], ONE2[:, :, :], ALU.add).then_inc(r_one, 1)
                dve.wait_ge(r_gexp, l + 1)
                link(v.reciprocal(gw, gsum))
                dve.wait_ge(r_p2, l + 1)
                link(v.tensor_scalar(g2, p2, 1.0, None, ALU.add))
                link(v.reciprocal(g1, g2))
                link(v.tensor_tensor(g1, g1, gw, ALU.mult))
                link(v.tensor_tensor(g2, g1, p2, ALU.mult))
                link(v.tensor_tensor(ONE1[:, :, :], ONE1[:, :, :], g1.unsqueeze(2).broadcast_to([P, T, EXPERTS]), ALU.mult))
                link(v.tensor_tensor(ONE2[:, :, :], ONE2[:, :, :], g2.unsqueeze(2).broadcast_to([P, T, EXPERTS]), ALU.mult))
                link(v.tensor_tensor(WGT[:, :, 0:EXPERTS], ONE1[:, :, :], ONE2[:, :, :], ALU.add))
                dve.wait_ge(rank_done, l + 1)
                dve.wait_ge(r_one, l + 1)
                rk = bank[4][:, 0:128].rearrange("p (t f) -> p t f", t=T)[:, :, 0:EXPERTS]
                link(v.scalar_tensor_tensor(RANK[:, :, 0:EXPERTS], rk, 1.0, ELOG[:, :, :], ALU.add, ALU.mult))
                link(v.tensor_scalar(RANK[:, :, 0:EXPERTS], RANK[:, :, 0:EXPERTS], -1.0, None, ALU.add))
                v.tensor_reduce(rtop, RANK[:, :, :].rearrange("p t e -> p (t e)"), AX, ALU.max).then_inc(r_top, 1)
                if l:
                    dve.wait_ge(moe["gather_hi"], (PAIRS + 1) * l)
                select(moe, 0, 0)
                dve.wait_ge(top_done, l + 1)
                link(v.tensor_reduce(rtop2[0:1, :], bank[5][0:1, 0:P], AX, ALU.max))
                v.tensor_scalar(FLAG[0:1, l:l + 1], rtop2[0:1, :], SLOTS - 0.5, None, ALU.is_ge).then_inc(flag_ready, 1)
                first_tokens(moe, (PAIRS + 1) * l)
                with dve.Fori(0, PAIRS) as p:
                    experts(moe, p, p + PAIRS * l, p + (PAIRS + 1) * l)
                dve.wait_ge(flag_ready, l + 1)
                more = dve.value_load(FLAG[0:1, l:l + 1], min_val=0, max_val=1)
                with dve.If(more > 0):
                    s = over[l]
                    dve.wait_ge(moe["gather_hi"], (PAIRS + 1) * (l + 1))
                    with dve.Fori(0, ROUNDS_MORE) as r:
                        v.tensor_scalar(RANK[:, :, 0:EXPERTS], RANK[:, :, 0:EXPERTS], float(-SLOTS), None, ALU.add)\
                            .then_inc(over_shift[l], 1)
                        dve.wait_ge(over_shift[l], r + 1)
                        select(s, 0, 0)
                        first_tokens(s, r * (PAIRS + 1))
                        with dve.Fori(0, PAIRS) as p:
                            experts(s, p, r * PAIRS + p, r * (PAIRS + 1) + p)
                dve.wait_ge(acc_done, l + 1)
                layer_norm(add_experts, then, evac, low)

            v.memset(RANK[:, :, :], -1.0)
            link(v.memset(WGT[:, :, :], 0.0))
            evac_by_token("x")
            for g, n in enumerate(EIN[0:3]):
                evac_chunk(G_EIN + g, E[:, 1, 512 * n:min(512 * n + 512, EVEN_IN)])
            dve.wait_ge(pj_free[0], 3)
            dve.wait_ge(pj_free[1], 3)
            sq = SQA[:, :, 0:Q_RANK + KV_RANK]
            link(v.tensor_tensor(sq, E[:, :, CQ0:KR0], E[:, :, CQ0:KR0], ALU.mult))
            v.tensor_reduce(var_b[:, :, 0], sq[:, :, 0:Q_RANK], AX, ALU.add)
            link(v.tensor_reduce(var_b[:, :, 1], sq[:, :, Q_RANK:Q_RANK + KV_RANK], AX, ALU.add))
            v.tensor_scalar(var_b[:, :, 0], var_b[:, :, 0], 1.0 / Q_RANK, RMS_EPS, ALU.mult, ALU.add)
            ask_root(v.tensor_scalar(var_b[:, :, 1], var_b[:, :, 1], 1.0 / KV_RANK, RMS_EPS, ALU.mult, ALU.add))
            rope(v, link, E[:, :, 0:1024].rearrange("p t (h f) -> p t h f", f=A_DIM), rot_a, A_HALF, 16, ROT)\
                .then_inc(rope_ready, 1)
            inverse_root(var_b[:, :, :], rs_b[:, :, :])
            for t in range(T):
                v.tensor_scalar(E[:, t, CQ0:CKV0], E[:, t, CQ0:CKV0], rs_b[:, t, 0:1], None, ALU.mult)
                last = v.tensor_scalar(E[:, t, CKV0:KR0], E[:, t, CKV0:KR0], rs_b[:, t, 1:2], None, ALU.mult)
            last.then_inc(rank_ready, 1)
            dve.wait_ge(const_loaded, 48)
            dve.wait_ge(rope_ready, 1)
            lam = ROWS[:, R_LAM:R_LAM + 4 * A_DIM].rearrange("p (a b f) -> p a b f", a=2, b=2)
            lt = ROT[3][:, 0:2 * A_DIM].rearrange("p (a f) -> p a f", a=2)
            link(v.tensor_tensor(lt, lam[:, :, 0, :], lam[:, :, 1, :], ALU.mult))
            v.tensor_reduce(lamv, lt, AX, ALU.add).then_inc(lam_ready, 1)
            evac_chunk(G_EIN + 3, E[:, 1, 1024:1536])
            dve.wait_ge(lam_exp, 1)
            link(v.scalar_tensor_tensor(nlam, lamv[:, 1:2], -LAMBDA_INIT, lamv[:, 0:1], ALU.add, ALU.subtract))
            dve.wait_ge(pj_free[0], 4)
            evac_transposes("qk", lambda b, n: QKT[:, b:b + n, :])
            evac_transposes("c", lambda b, n: CT[:, b, :], blocks=3, gain=lambda b: COLS[:, Q_QN + b:Q_QN + b + 1])
            def d_maxima(h):
                for m in range(2):
                    dve.wait_ge(d_score, 2 * h + m + 1)
                    ps = bank[4 + 2 * (h % 2) + m][:, :].rearrange("p (t k) -> p t k", t=T)
                    link(v.tensor_reduce(dmx[:, h % 2, m, :], ps, AX, ALU.max))
                    v.tensor_scalar(dnb[:, h % 2, m, :], dmx[:, h % 2, m, :], -(A_DIM ** -0.5), None, ALU.mult)\
                        .then_inc(d_nb, 1)

            def d_weights(h):
                dve.wait_ge(d_exp, 2 * h + 2)
                s4 = dsm[:, h % 2, :, :]
                link(v.reciprocal(s4, s4))
                link(v.tensor_scalar(s4[:, 1, :], s4[:, 1, :], nlam, None, ALU.mult))
                e0, e1 = PB[2 * (h % 2)], PB[2 * (h % 2) + 1]
                for t in range(T):
                    last = v.tensor_scalar(e0[:, t, :], e0[:, t, :], s4[:, 0, t:t + 1], None, ALU.mult)
                link(last)
                for t in range(T):
                    last = v.scalar_tensor_tensor(e0[:, t, :], e1[:, t, :], s4[:, 1, t:t + 1], e0[:, t, :], ALU.mult, ALU.add)
                last.then_inc(d_w, 1)

            for h in range(2):
                d_maxima(h)
            for n in range(2):
                evac_chunk(G_UQ + n, QB[:, 1, 384 * n:384 * n + 384])
            d_weights(0)
            for n in range(2):
                evac_chunk(G_UKV + n, KV[:, 1, 512 * n:512 * n + 512])
            for i in range(2, A_HEADS + 2):
                if i - 1 < A_HEADS:
                    d_weights(i - 1)
                if i < A_HEADS:
                    d_maxima(i)
                h = i - 2
                dve.wait_ge(d_pv, h + 1)
                v.tensor_copy(AO[:, :, h * P:(h + 1) * P], bank[2 + h % 2][:, 0:SEQ].rearrange("p (t e) -> p t e", t=T))\
                    .then_inc(d_o, 1)
            dve.wait_ge(d_sq, A_HEADS)
            ask_root(v.tensor_scalar(var_a[:, :, :], var_a[:, :, :], 1.0 / (2 * A_DIM), RMS_EPS, ALU.mult, ALU.add))
            evac_transposes("qb", lambda b, n: QBT[0:B_QK, b:b + n, :], B_QK)
            inverse_root(var_a[:, :, :], rs_a[:, :, :])
            v.tensor_scalar(rs_a[:, :, :], rs_a[:, :, :], 1.0 - LAMBDA_INIT, None, ALU.mult).then_inc(ao_scale, 1)
            evac_transposes("kb", lambda b, n: KBT[0:B_QK, b:b + n, :], B_QK)
            attention(N_MLA0, B_HEADS, PB, lambda pair: MT[:, 4 + pair, :], B_QK ** -0.5, None)
            evac_transposes("ao", lambda b, n: MT[:, b:b + n, :])
            layer_norm(lambda t: add_out(G_EO, t, ALPHA))
            evac_by_token("ln0")
            moe_layer(0, None, lambda t: evac_token("ln1", t), lambda t: low_input(t, 0))
            evac_chunk(G_QKV, OV[:, 1, 0:512])
            for n in range(4):
                evac_chunk(G_QKV + 1 + n, (OQ if n < 2 else OK)[:, 4 * (n % 2) + 2:4 * (n % 2) + 4, :])
            evac_chunk(G_QKV + 5, OV[:, 1, 512:1024])
            dve.wait_ge(bias_loaded, 16)
            attention(N_NA0, C_HEADS, PN, lambda pair: MT[:, pair, :], C_DIM ** -0.5,
                      lambda h, t: G[:, h, (2 - 2 * t) * GRID_W:(2 - 2 * t) * GRID_W + SEQ])
            layer_norm(lambda t: add_out(G_OO, t, ALPHA))
            evac_by_token("ln2")
            moe_layer(1, lambda t: normed(t, XN), lambda t: evac_token("n1", t, Q_N1),
                      lambda t: low_input(t, T))
            def evac_2(n):
                evac_chunk(G_IN2 + n, TOK[:, 1, 512 * (IN2[n] - 2):512 * (IN2[n] - 1)])

            ll = COLS[:, Q_LAM:Q_LAM + LRU_T]
            link(v.tensor_scalar(spl[0], ll, -1.0, 0.0, ALU.mult, ALU.max))
            link(v.tensor_scalar(spl[1], ll, -1.0, None, ALU.mult))
            v.tensor_tensor(spl[1], spl[1], ll, ALU.min).then_inc(sp_in, 1)
            v.tensor_scalar(spl[3], COLS[:, Q_BA:Q_BA + LRU_T], 0.5, None, ALU.mult)
            v.tensor_scalar(spl[4], COLS[:, Q_BX:Q_BX + LRU_T], 0.5, None, ALU.mult).then_inc(sp_in, 1)
            evac_2(0)
            evac_chunk(G_IN2 + 1, XL[:, 2:4, :])
            dve.wait_ge(pj_free[0], G_IN2 + 2)
            dve.wait_ge(pj_free[1], G_IN2 + 2)

            def tap(j, c):
                return COLS[:, Q_CW + j * LRU_T + c:Q_CW + j * LRU_T + c + 1]

            for c in range(LRU_T):
                last = v.tensor_scalar(LX[:, c, :], XL[:, c, :], tap(3, c), COLS[:, Q_CB + c:Q_CB + c + 1], ALU.mult, ALU.add)
            link(last)
            for j in range(1, LRU_CONV):
                for c in range(LRU_T):
                    last = v.scalar_tensor_tensor(LX[:, c, j:SEQ], XL[:, c, 0:SEQ - j], tap(3 - j, c), LX[:, c, j:SEQ],
                                                  ALU.mult, ALU.add)
                    if j == LRU_CONV - 1:
                        last.then_inc(lru_cvd, 1)
                if j < LRU_CONV - 1:
                    link(last)
            dve.wait_ge(sp_exp, 1)
            link(v.tensor_scalar(spl[2], spl[1], 2.0, None, ALU.add))
            link(v.reciprocal(spl[2], spl[2]))
            link(v.tensor_tensor(spl[1], spl[1], spl[2], ALU.mult))
            link(v.tensor_tensor(spl[2], spl[1], spl[1], ALU.mult))
            ser = spl_series
            link(v.tensor_scalar(ser, spl[2], 1.0 / 19, 1.0 / 17, ALU.mult, ALU.add))
            for k in (15, 13, 11, 9, 7, 5, 3, 1):
                link(v.tensor_tensor(ser, ser, spl[2], ALU.mult))
                link(v.tensor_scalar(ser, ser, 1.0 / k, None, ALU.add))
            link(v.tensor_tensor(ser, ser, spl[1], ALU.mult))
            link(v.scalar_tensor_tensor(spl[0], ser, 2.0, spl[0], ALU.mult, ALU.add))
            link(v.tensor_scalar(spl[0], spl[0], -4.0, None, ALU.mult))
            dve.wait_ge(pj_free[1], G_IN2 + 3)
            evac_2(3)
            dve.wait_ge(lru_g, LRU_T)
            for c in range(LRU_T):
                last = v.tensor_scalar(LA[:, c, :], LA[:, c, :], 1.0, spl[0][:, c:c + 1], ALU.add, ALU.mult)
            last.then_inc(lru_t, 1)
            link(v.tensor_scalar(LI[:, :, :], LI[:, :, :], 0.5, 0.5, ALU.mult, ALU.add))
            link(v.tensor_tensor(LI[:, :, :], LI[:, :, :], LX[:, :, :], ALU.mult))
            dve.wait_ge(lru_a, 2)
            link(v.tensor_tensor(XL[:, :, :], LA[:, :, :], LA[:, :, :], ALU.mult))
            ask_root(v.scalar_tensor_tensor(LT_[:, :, :], XL[:, :, :], 1.0, LT_[:, :, :], ALU.add, ALU.mult))
            evac_2(4)
            dve.wait_ge(pj_free[0], G_IN2 + 5)
            dve.wait_ge(pj_free[1], G_IN2 + 5)
            dve.wait_ge(table2_loaded, 32)
            rope(v, link, TOK[:, :, 0:1024].rearrange("p t (h f) -> p t h f", f=RET_DIM), rot_c, RET_DIM // 2, 8, ROT2)\
                .then_inc(r_rope, 1)
            dve.wait_ge(std_ready, roots[0])
            link(v.tensor_tensor(LI[:, :, :], LI[:, :, :], LT_[:, :, :], ALU.mult))
            for c in range(LRU_T):
                last = v.tensor_tensor_scan(LX[:, c, :], LA[:, c, :], LI[:, c, :], 0.0, ALU.mult, ALU.add)
            link(last)
            link(v.tensor_tensor(LX[:, :, :], LX[:, :, :], GL[:, :, :], ALU.mult))
            v.tensor_tensor(LT_[:, :, :], LX[:, :, :], LX[:, :, :], ALU.mult).then_inc(lru_sq, 1)
            evac_transposes("rqk", lambda b, n: RQK[:, b:b + n, :])
            dve.wait_ge(lru_sqr, 1)
            ask_root(v.tensor_scalar(LI[:, 0, :], bank[0][:, 0:SEQ], 1.0 / LRU, RMS_EPS, ALU.mult, ALU.add))
            for h in range(RET_HEADS):
                dve.wait_ge(r_sc, h + 1)
                v.tensor_tensor(RS[:, h, :], bank[4 + h][:, 0:DEC_W], KT2[:, L_DEC + h * DEC_W:L_DEC + (h + 1) * DEC_W],
                                ALU.mult).then_inc(r_scd, 1)
            inverse_root(LI[:, 0, :], LI[:, 1, :])
            for c in range(LRU_T):
                last = v.scalar_tensor_tensor(LX[:, c, :], LX[:, c, :], COLS[:, Q_LN + c:Q_LN + c + 1], LI[:, 1, :],
                                              ALU.mult, ALU.mult)
            last.then_inc(lru_y, 1)
            evac_2(5)
            for h in range(RET_HEADS):
                dve.wait_ge(r_o, h + 1)
                v.tensor_copy(YR[:, :, h * P:(h + 1) * P], bank[4 + h % 2][:, 0:SEQ].rearrange("p (t e) -> p t e", t=T))\
                    .then_inc(r_oc, 1)
            dve.wait_ge(r_oc, RET_HEADS)
            for t in range(T):
                for h in range(RET_HEADS):
                    last = v.bn_stats(hst[:, t, h, :], YR[:, t, h * P:(h + 1) * P])
            link(last)
            for t in range(T):
                for h in range(RET_HEADS):
                    last = v.bn_aggr(hmv[:, t, h, :], hst[:, t, h, :])
            link(last)
            ask_root(v.tensor_scalar(var_h[:, :, :], hmv[:, :, :, 1], RMS_EPS, None, ALU.add))
            inverse_root(var_h[:, :, :], rs_h[:, :, :])
            for t in range(T):
                for h in range(RET_HEADS):
                    last = v.tensor_scalar(YR[:, t, h * P:(h + 1) * P], YR[:, t, h * P:(h + 1) * P], hmv[:, t, h, 0:1],
                                           rs_h[:, t, h:h + 1], ALU.subtract, ALU.mult)
            link(last)
            dve.wait_ge(r_gain, 1)
            for t in range(T):
                last = v.tensor_tensor(YR[:, t, :], YR[:, t, :], TOK[:, t, 1536:2048], ALU.mult)
            last.then_inc(r_y, 1)
            evac_transposes("yr", lambda b, n: MT[:, 4 + b:4 + b + n, :])
            def low_weights(k):
                dve.wait_ge(w_hi, K_FFN + k + 1)
                v.tensor_tensor(WLO[k % WBUF][:, :, :], ffn_weights(k)[1], WHI[k % WBUF][:, :, :], ALU.subtract)\
                    .then_inc(w_lo, 1)

            def low_products(c):
                dve.wait_ge(a_hi, c + 1)
                v.tensor_tensor(ALO[c % WBUF][:, :], ACTT[:, c, :], AHI[c % WBUF][:, :], ALU.subtract).then_inc(a_lo, 1)

            for k in range(WBUF):
                low_weights(k)
            for t in range(T):
                add_out(G_OUT2, t, 1.0)
                normed(t, XN)
            for t in range(T):
                evac_token("n2", t, Q_N2)
                low_input(t, X_FFN)
            for f in range(FF2_T):
                dve.wait_ge(f_cv0, f + 1)
                for j in (1, 2):
                    wj = COLS[:, Q_FW + (2 - j) * FF2_T + f:Q_FW + (2 - j) * FF2_T + f + 1]
                    ins = v.scalar_tensor_tensor(CV[f % 4][:, j:SEQ], bank[f % 4][:, 0:SEQ - j], wj, CV[f % 4][:, j:SEQ],
                                                 ALU.mult, ALU.add)
                    if j == 1:
                        link(ins)
                    else:
                        ins.then_inc(f_cv, 1)
                if f >= DOWN_T:
                    g = f - DOWN_T
                    dve.wait_ge(f_gelu, g + 1)
                    dve.wait_ge(f_cv, f + 1)
                    v.tensor_tensor(ACTT[:, g, :], ACTT[:, g, :], CV[f % 4], ALU.mult).then_inc(f_act, 1)
                low_weights(f + WBUF)
                if EARLY_A <= f < EARLY_A + WBUF:
                    low_products(f - EARLY_A)
            for c in range(WBUF, DOWN_T):
                low_weights(FF2_T + c)
                low_products(c)
            dve.wait_ge(ln_loaded, 16 * 6)
            for t in range(T):
                dve.wait_ge(w_used, U_FFN + FF2_T + DOWN_T - WBUF + t + 1)
                for h in range(2):
                    xs = X[:, t, 512 * h:512 * h + 512]
                    last = v.tensor_tensor(xs, xs, bank[4 + 2 * t + h][:, :], ALU.add)
                link(last)
                token_rms(t, XN)
                v.scalar_tensor_tensor(X[:, t, :], X[:, t, :], rs_l[:, t:t + 1], LNR[:, 0, :], ALU.mult, ALU.mult)\
                    .then_inc(out_ready, 1)


def lay_out(i):
    table, table2 = shape_constants()

    def feature_columns(a):
        a = a.reshape(-1, a.shape[-1] // P, P)
        return a.transpose(2, 0, 1).reshape(P, -1)

    cols = np.concatenate([feature_columns(a) for a in (
        i["norm1_gain_2"], i["lru_conv_w_2"][0], i["lru_conv_b_2"], i["lru_gate_a_b_2"], i["lru_gate_x_b_2"],
        i["lru_lambda_2"], i["lru_norm_gain_2"], i["norm2_gain_2"], i["ffn_conv_w_2"][0], i["ffn_conv_b_2"],
        i["even_q_norm_g"], i["even_kv_norm_g"])], 1)
    rows = np.concatenate([i["even_subln_g"][0], i["even_lam_q1"][0], i["even_lam_k1"][0], i["even_lam_q2"][0],
                           i["even_lam_k2"][0]] +
                          [a for l in range(DEPTH) for a in (i["b_router_group"][l], i["b_router_expert"][l])])[None]
    ln_rows = np.zeros((6, 2 * D), np.float32)
    for l in range(DEPTH):
        for n, name in enumerate(("ln1", "ln2")):
            ln_rows[2 * l + n, :D] = i[f"{name}_g"][l]
            ln_rows[2 * l + n, D:] = i[f"{name}_b"][l]
    ln_rows[4, :RET_HEADS * RET_DIM] = i["ret_norm_gain_2"][0]
    ln_rows[5, :D] = i["final_norm_gain_2"]
    route = np.concatenate([i["w_router_group"], i["w_router_expert"]], 2)
    route = route.reshape(DEPTH, C, P, ROUTE).transpose(2, 0, 1, 3)
    rr, cc, m, j = np.meshgrid(np.arange(2), np.arange(GRID_W), np.arange(BIAS_ROWS), np.arange(GRID_W), indexing="ij")
    start = np.clip(cc - NA_COLS // 2, 0, GRID_W - NA_COLS)
    inside = (j >= start) & (j < start + NA_COLS)
    col = np.clip(j - cc + NA_COLS - 1, 0, 2 * NA_COLS - 2)
    bias = i["odd_rel_bias"][0][:, m + 5 - rr, col]
    bias = np.where(inside[None], bias, np.float32(NEG))
    bias = bias.transpose(1, 2, 0, 3, 4).reshape(P, C_HEADS, BIAS_ROWS * GRID_W)
    gates = np.zeros((P, 2, LRU_T, P), np.float32)
    for n, name in enumerate(("lru_gate_a_w_2", "lru_gate_x_w_2")):
        for h in range(8):
            o = h % 2 * 64
            gates[o:o + 64, n, h // 2, o:o + 64] = i[name][0, h]
    return {
        "x": i["x"][0], "w_in": i["even_w_in"][0], "w_uq": i["even_w_uq"][0], "w_ukv": i["even_w_ukv"][0],
        "w_o": i["even_w_o"][0], "w_qkv": i["odd_w_qkv"][0], "na_bias": bias, "w_o2": i["odd_w_o"][0],
        "ln_rows": ln_rows, "rows": rows, "cols": cols, "w_route": route, "w_gate": i["w_gate"], "w_up": i["w_up"],
        "w_down": i["w_down"], "w_in2": i["w_in_2"][0], "gates": gates.reshape(P, 2, LRU_T * P),
        "w_out2": i["w_out_2"][0], "ffn_up": i["ffn_up_w_2"][0], "ffn_down": i["ffn_down_w_2"][0],
        "table": table, "table2": table2,
    }


def kernel(**inputs):
    import concourse.bacc as bacc
    from concourse.bass_utils import run_bass_kernel_spmd

    laid = lay_out({k: np.asarray(a) for k, a in inputs.items()})
    nc = bacc.Bacc("TRN2", target_bir_lowering=False, num_devices=1)
    arrays, args = {}, []
    for name, a in laid.items():
        a = np.ascontiguousarray(a)
        arrays[f"in_{name}"] = a
        args.append(nc.dram_tensor(f"in_{name}", a.shape, mybir.dt.from_np(a.dtype), kind="ExternalInput").ap())
    out = nc.dram_tensor("out", (SEQ, D), F32, kind="ExternalOutput").ap()
    bass_two_blocks(nc, *args, out)
    r = run_bass_kernel_spmd(nc, [arrays], core_ids=[0])
    return np.asarray(r.results[0]["out"]).reshape(1, SEQ, D)
```
